# Optimizing a Trainium2 kernel written in Bass

```python
import math
import jax, jax.numpy as jnp
from jax import lax
import numpy as np

D_MODEL = 1024
BATCH = 1
SEQ = 256
DEPTH = 2

CHUNK = 64
Q_BLOCK = 128
HEAD_DIM = 64
MEM_LEN = 256
MEM_HEADS = 4
MEM_W = MEM_HEADS * HEAD_DIM
MIX_W = D_MODEL
BR_W = MIX_W - MEM_W
A_HEADS = BR_W // HEAD_DIM
B_HEADS = BR_W // (2 * HEAD_DIM)
LORA_W = 64
LORA_A = 64
N_A = DEPTH // 2
N_B = DEPTH - N_A
A_SHIFT = 3 * BR_W + LORA_W + LORA_A
A_IN = A_SHIFT + BR_W + 2 * MEM_W
B_IN = 2 * BR_W + 2 * MEM_W
NORM_EPS = 1e-6
LNX_EPS = 64e-5


def rms_norm(x, g):
    xf = x.astype(jnp.float32)
    y = xf * lax.rsqrt(jnp.mean(xf * xf, axis=-1, keepdims=True) + NORM_EPS)
    return (y * g.astype(jnp.float32)).astype(x.dtype)

def token_shift(z):
    return jnp.pad(z, ((0, 0), (1, 0), (0, 0)))[:, :-1]

def alibi_slopes(n):
    def pow2(m):
        start = 2.0 ** (-8.0 / m)
        return [start ** (i + 1) for i in range(m)]
    if math.log2(n).is_integer():
        s = pow2(n)
    else:
        c = 2 ** int(math.floor(math.log2(n)))
        s = pow2(c) + pow2(2 * c)[0::2][: n - c]
    return jnp.asarray(np.array(s, dtype=np.float32))

def rwkv7_time_mix(z, mu, w0, w2, a0, a2, k_k, k_a, r_k, lnx_w, lnx_b):
    B, S, _ = z.shape
    z = z.astype(jnp.float32)
    z = z + (token_shift(z) - z) * mu
    r, k, v, wd, ad = jnp.split(z, [BR_W, 2 * BR_W, 3 * BR_W, 3 * BR_W + LORA_W], axis=-1)
    w = -jax.nn.softplus(-(w0 + jnp.tanh(wd) @ w2)) - 0.5
    decay = jnp.exp(-jnp.exp(w))
    a = jax.nn.sigmoid(a0 + ad @ a2)
    heads = lambda t: t.reshape(B, S, A_HEADS, HEAD_DIM)
    kk = heads(k * k_k)
    kk = kk * lax.rsqrt(jnp.maximum(jnp.sum(kk * kk, axis=-1, keepdims=True), 1e-12))
    k = k * (1.0 + (a - 1.0) * k_a)
    r, k, v, decay, a = heads(r), heads(k), heads(v), heads(decay), heads(a)

    def step(state, inp):
        r_t, w_t, k_t, v_t, kk_t, a_t = inp
        sa = jnp.einsum('bhvk,bhk->bhv', state, -kk_t)
        state = (state * w_t[:, :, None, :]
                 + sa[..., None] * (kk_t * a_t)[:, :, None, :]
                 + v_t[..., None] * k_t[:, :, None, :])
        y_t = jnp.einsum('bhvk,bhk->bhv', state, r_t)
        return state, y_t

    tm = lambda t: jnp.moveaxis(t, 1, 0)
    state0 = jnp.zeros((B, A_HEADS, HEAD_DIM, HEAD_DIM), jnp.float32)
    _, y = lax.scan(step, state0, (tm(r), tm(decay), tm(k), tm(v), tm(kk), tm(a)))
    y = jnp.moveaxis(y, 0, 1)
    mean = jnp.mean(y, axis=-1, keepdims=True)
    var = jnp.mean(jnp.square(y - mean), axis=-1, keepdims=True)
    y = ((y - mean) * lax.rsqrt(var + LNX_EPS)).reshape(B, S, BR_W) * lnx_w + lnx_b
    bonus = jnp.sum(r * k * r_k, axis=-1, keepdims=True) * v
    return y + bonus.reshape(B, S, BR_W)

def diff_attention(q, k_sh, v_sh, lq1, lk1, lq2, lk2, subln, lam_init):
    B, S, _ = q.shape
    q = q.reshape(B, S, B_HEADS, 2, HEAD_DIM) * (HEAD_DIM ** -0.5)
    k = k_sh.reshape(B, S, B_HEADS, 2, HEAD_DIM)
    v = v_sh.reshape(B, S, B_HEADS, 2 * HEAD_DIM)
    lq1f, lk1f = lq1.astype(jnp.float32), lk1.astype(jnp.float32)
    lq2f, lk2f = lq2.astype(jnp.float32), lk2.astype(jnp.float32)
    lam = jnp.exp(jnp.sum(lq1f * lk1f)) - jnp.exp(jnp.sum(lq2f * lk2f)) + lam_init
    slopes = alibi_slopes(B_HEADS)
    pos = jnp.arange(S)
    nb = S // Q_BLOCK
    qb = jnp.moveaxis(q.reshape(B, nb, Q_BLOCK, B_HEADS, 2, HEAD_DIM), 1, 0)

    def block(args):
        q_blk, i = args
        t = i * Q_BLOCK + jnp.arange(Q_BLOCK)
        s = jnp.einsum('bqhcd,bkhcd->bhcqk', q_blk, k, preferred_element_type=jnp.float32)
        dist = jnp.abs(t[:, None] - pos[None, :]).astype(jnp.float32)
        bias = -slopes[:, None, None] * dist
        allowed = (pos[None, :] // CHUNK) <= (t[:, None] // CHUNK)
        s = jnp.where(allowed, s + bias[None, :, None], -jnp.inf)
        p = jax.nn.softmax(s, axis=-1)
        attn = (p[:, :, 0] - lam * p[:, :, 1]).astype(v.dtype)
        return jnp.einsum('bhqk,bkhe->bqhe', attn, v)

    o = lax.map(block, (qb, jnp.arange(nb)))
    o = jnp.moveaxis(o, 0, 1).reshape(B, S, B_HEADS, 2 * HEAD_DIM)
    o = rms_norm(o, subln) * (1.0 - lam_init)
    return o.reshape(B, S, BR_W)

def memory_cross_attention(q, mem_n, w_mem_kv):
    B, S, _ = q.shape
    k, v = jnp.split(mem_n @ w_mem_kv, 2, axis=-1)
    k = k.reshape(B, -1, MEM_HEADS, HEAD_DIM)
    v = v.reshape(B, -1, MEM_HEADS, HEAD_DIM)
    q = q.reshape(B, S, MEM_HEADS, HEAD_DIM)
    s = jnp.einsum('bshd,bmhd->bhsm', q, k, preferred_element_type=jnp.float32) * (HEAD_DIM ** -0.5)
    p = jax.nn.softmax(s, axis=-1).astype(v.dtype)
    o = jnp.einsum('bhsm,bmhd->bshd', p, v)
    return o.reshape(B, S, MEM_W)

def first_inputs(seed: int = 0) -> dict:
    key = jax.random.key(seed)
    ks = jax.random.split(key, 32)
    nrm = lambda k, shape, scale: scale * jax.random.normal(k, shape, jnp.float32)
    gain = lambda k, shape: 1.0 + 0.05 * jax.random.normal(k, shape, jnp.float32)
    return {
        'x': jax.random.normal(ks[0], (BATCH, SEQ, D_MODEL), jnp.float32),
        'mem': jax.random.normal(ks[1], (BATCH, MEM_LEN, D_MODEL), jnp.float32),
        'pre_norm': gain(ks[2], (DEPTH, D_MODEL)),
        'post_norm': gain(ks[3], (DEPTH, D_MODEL)),
        'w_out': nrm(ks[4], (DEPTH, MIX_W, D_MODEL), MIX_W ** -0.5),
        'mem_norm': gain(ks[5], (DEPTH, D_MODEL)),
        'w_mem_kv': nrm(ks[6], (DEPTH, D_MODEL, 2 * MEM_W), D_MODEL ** -0.5),
        'a_w_in': nrm(ks[7], (N_A, D_MODEL, A_IN), D_MODEL ** -0.5),
        'a_shift_mu': jax.random.uniform(ks[8], (N_A, A_SHIFT), jnp.float32),
        'a_w0': jax.random.uniform(ks[9], (N_A, BR_W), jnp.float32, minval=-6.0, maxval=0.0),
        'a_w2': nrm(ks[10], (N_A, LORA_W, BR_W), 0.5 * LORA_W ** -0.5),
        'a_a0': nrm(ks[11], (N_A, BR_W), 0.1),
        'a_a2': nrm(ks[12], (N_A, LORA_A, BR_W), 0.5 * LORA_A ** -0.5),
        'a_k_k': 0.85 + 0.05 * jax.random.normal(ks[13], (N_A, BR_W), jnp.float32),
        'a_k_a': gain(ks[14], (N_A, BR_W)),
        'a_r_k': nrm(ks[15], (N_A, A_HEADS, HEAD_DIM), 0.1),
        'a_lnx_w': gain(ks[16], (N_A, BR_W)),
        'a_lnx_b': nrm(ks[17], (N_A, BR_W), 0.02),
        'kv_norm': gain(ks[18], (D_MODEL,)),
        'w_kv': nrm(ks[19], (D_MODEL, 2 * BR_W), D_MODEL ** -0.5),
        'b_w_in': nrm(ks[20], (N_B, D_MODEL, B_IN), D_MODEL ** -0.5),
        'b_lam_q1': nrm(ks[21], (N_B, HEAD_DIM), 0.1),
        'b_lam_k1': nrm(ks[22], (N_B, HEAD_DIM), 0.1),
        'b_lam_q2': nrm(ks[23], (N_B, HEAD_DIM), 0.1),
        'b_lam_k2': nrm(ks[24], (N_B, HEAD_DIM), 0.1),
        'b_subln': gain(ks[25], (N_B, 2 * HEAD_DIM)),
    }

def first_block(x, mem, pre_norm, post_norm, w_out, mem_norm, w_mem_kv,
              a_w_in, a_shift_mu, a_w0, a_w2, a_a0, a_a2, a_k_k, a_k_a, a_r_k, a_lnx_w, a_lnx_b,
              kv_norm, w_kv,
              b_w_in, b_lam_q1, b_lam_k1, b_lam_q2, b_lam_k2, b_subln):
    k_sh = None
    v_sh = None
    for l in range(DEPTH):
        h = rms_norm(x, pre_norm[l])
        mem_n = rms_norm(mem, mem_norm[l])
        if l < N_A:
            i = l
            proj = h @ a_w_in[i]
            z, gate, q_mem, g_mem = jnp.split(
                proj, [A_SHIFT, A_SHIFT + BR_W, A_SHIFT + BR_W + MEM_W], axis=-1)
            y_br = rwkv7_time_mix(z, a_shift_mu[i], a_w0[i], a_w2[i], a_a0[i], a_a2[i],
                                  a_k_k[i], a_k_a[i], a_r_k[i], a_lnx_w[i], a_lnx_b[i])
        else:
            if l == N_A:
                k_sh, v_sh = jnp.split(rms_norm(x, kv_norm) @ w_kv, 2, axis=-1)
            i = l - N_A
            proj = h @ b_w_in[i]
            q, gate, q_mem, g_mem = jnp.split(
                proj, [BR_W, 2 * BR_W, 2 * BR_W + MEM_W], axis=-1)
            lam_init = 0.8 - 0.6 * math.exp(-0.3 * l)
            y_br = diff_attention(q, k_sh, v_sh, b_lam_q1[i], b_lam_k1[i], b_lam_q2[i],
                                  b_lam_k2[i], b_subln[i], lam_init)
        y_mem = memory_cross_attention(q_mem, mem_n, w_mem_kv[l])
        y = jnp.concatenate([(y_br * jax.nn.silu(gate.astype(jnp.float32))).astype(x.dtype),
                             y_mem * jax.nn.silu(g_mem)], axis=-1) @ w_out[l]
        x = x + rms_norm(y, post_norm[l])
    return x


DEPTH_2 = 1

N_META = 16
D_FF = 2816
RET_HEADS = 4
RET_DK = 256
RET_DV = 512
RET_CHUNK = 128
ATT_HEADS = 8
ATT_DH = 128
IDX_HEADS = 8
IDX_DH = 64
TOPK_MAX = 256
DSA_QBLOCK = 32
ROPE_THETA = 10000.0
EPS = 1e-6
RET_QK = RET_HEADS * RET_DK
RET_V = RET_HEADS * RET_DV
ATT_W = ATT_HEADS * ATT_DH
IDX_Q = IDX_HEADS * IDX_DH
IN_SPLITS = (RET_QK, RET_QK, RET_V, RET_V, ATT_W, ATT_W, ATT_W, IDX_Q, IDX_DH, IDX_HEADS, D_MODEL, D_MODEL)
D_IN = sum(IN_SPLITS)


def rmsnorm(x, g):
    xf = x.astype(jnp.float32)
    y = xf * lax.rsqrt(jnp.mean(xf * xf, axis=-1, keepdims=True) + EPS)
    return (y * g.astype(jnp.float32)).astype(x.dtype)

def rope(x, pos):
    d = x.shape[-1]
    inv_freq = ROPE_THETA ** (-jnp.arange(0, d, 2, dtype=jnp.float32) / d)
    ang = pos.astype(jnp.float32)[:, None] * inv_freq[None, :]
    cos = jnp.cos(ang)[:, None, :]
    sin = jnp.sin(ang)[:, None, :]
    xf = x.astype(jnp.float32)
    x1, x2 = xf[..., : d // 2], xf[..., d // 2:]
    return jnp.concatenate([x1 * cos - x2 * sin, x2 * cos + x1 * sin], axis=-1).astype(x.dtype)

def swiglu(u, w_gate, w_up, w_down):
    return (jax.nn.silu(u @ w_gate) * (u @ w_up)) @ w_down

def retention(q, k, v):
    out_dtype = v.dtype
    q, k, v = (a.astype(jnp.float32) for a in (q, k, v))
    B, H, T, _ = q.shape
    C = RET_CHUNK
    n = (T - N_META) // C
    log_g = jnp.log1p(-(2.0 ** (-5.0 - jnp.arange(H, dtype=jnp.float32))))

    def decay_matrix(c):
        i = jnp.arange(c, dtype=jnp.float32)
        diff = i[:, None] - i[None, :]
        return jnp.where(diff >= 0, jnp.exp(log_g[:, None, None] * jnp.maximum(diff, 0.0)), 0.0)

    qm, km, vm = q[:, :, :N_META], k[:, :, :N_META], v[:, :, :N_META]
    y_meta = jnp.einsum('bhqk,bhke->bhqe', jnp.einsum('bhqd,bhkd->bhqk', qm, km) * decay_matrix(N_META), vm)
    zeta_m = jnp.exp(log_g[:, None] * (N_META - 1.0 - jnp.arange(N_META, dtype=jnp.float32)))
    state0 = jnp.einsum('bhkd,bhke->bhde', km * zeta_m[..., None], vm)

    d_in = decay_matrix(C)
    pos_c = jnp.arange(C, dtype=jnp.float32)
    xi = jnp.exp(log_g[:, None] * (pos_c + 1.0))[..., None]
    zeta = jnp.exp(log_g[:, None] * (C - 1.0 - pos_c))[..., None]
    g_chunk = jnp.exp(log_g * C)[:, None, None]

    def to_chunks(a):
        return a[:, :, N_META:].reshape(B, H, n, C, a.shape[-1]).transpose(2, 0, 1, 3, 4)

    def step(state, qkv):
        qc, kc, vc = qkv
        inner = jnp.einsum('bhqk,bhke->bhqe', jnp.einsum('bhqd,bhkd->bhqk', qc, kc) * d_in, vc)
        cross = jnp.einsum('bhqd,bhde->bhqe', qc, state) * xi
        state = g_chunk * state + jnp.einsum('bhkd,bhke->bhde', kc * zeta, vc)
        return state, inner + cross

    _, y_chunks = lax.scan(step, state0, (to_chunks(q), to_chunks(k), to_chunks(v)))
    y_real = y_chunks.transpose(1, 2, 0, 3, 4).reshape(B, H, n * C, v.shape[-1])
    y = jnp.concatenate([y_meta, y_real], axis=2)
    y = y * lax.rsqrt(jnp.mean(y * y, axis=-1, keepdims=True) + EPS)
    return y.astype(out_dtype)

def dsa_attention(q, k, v, qi, ki, wi, k_top):
    B, T, H, dh = q.shape
    nb = -(-T // DSA_QBLOCK)
    t_pad = nb * DSA_QBLOCK
    pad = t_pad - T

    def blocks(a):
        a = jnp.pad(a, [(0, 0), (0, pad)] + [(0, 0)] * (a.ndim - 2))
        return a.reshape((B, nb, DSA_QBLOCK) + a.shape[2:]).swapaxes(0, 1)

    pos_blocks = jnp.arange(t_pad, dtype=jnp.int32).reshape(nb, DSA_QBLOCK)
    key_pos = jnp.arange(T, dtype=jnp.int32)
    meta_pos = jnp.arange(N_META, dtype=jnp.int32)
    k_meta, v_meta = k[:, :N_META], v[:, :N_META]
    scale = ATT_DH ** -0.5
    idx_scale = (IDX_DH ** -0.5) * (IDX_HEADS ** -0.5)
    gather = jax.vmap(lambda a, i: a[i])

    def one_block(args):
        qb, qib, wib, tq = args
        rel = jax.nn.relu(jnp.einsum('bqhd,bsd->bqhs', qib, ki))
        score = jnp.einsum('bqh,bqhs->bqs', wib, rel).astype(jnp.float32) * idx_scale
        admissible = (key_pos[None, :] >= N_META) & (key_pos[None, :] <= tq[:, None])
        score = jnp.where(admissible[None], score, -jnp.inf)
        _, sel = lax.top_k(score, k_top)
        sel_ok = (sel >= N_META) & (sel <= tq[None, :, None])
        k_sel = gather(k, sel)
        v_sel = gather(v, sel)
        s_meta = jnp.einsum('bqhd,bmhd->bhqm', qb, k_meta).astype(jnp.float32) * scale
        s_meta = jnp.where((meta_pos[None, :] <= tq[:, None])[None, None], s_meta, -jnp.inf)
        s_sel = jnp.einsum('bqhd,bqkhd->bhqk', qb, k_sel).astype(jnp.float32) * scale
        s_sel = jnp.where(sel_ok[:, None], s_sel, -jnp.inf)
        p = jax.nn.softmax(jnp.concatenate([s_meta, s_sel], axis=-1), axis=-1).astype(v.dtype)
        return (jnp.einsum('bhqm,bmhd->bqhd', p[..., :N_META], v_meta)
                + jnp.einsum('bhqk,bqkhd->bqhd', p[..., N_META:], v_sel))

    out = lax.map(one_block, (blocks(q), blocks(qi), blocks(wi), pos_blocks))
    return out.swapaxes(0, 1).reshape(B, t_pad, H, dh)[:, :T]

def hybrid_mixer(u, pos, k_top, w_in, w_ret_out, w_att_out, w_mix_out):
    B, T, _ = u.shape
    proj = u @ w_in
    offs = [int(o) for o in np.cumsum(IN_SPLITS)[:-1]]
    rq, rk, rv, rg, aq, ak, av, iq, ik, iw, g_ret, g_att = jnp.split(proj, offs, axis=-1)
    rq = rope(rq.reshape(B, T, RET_HEADS, RET_DK), pos)
    rk = rope(rk.reshape(B, T, RET_HEADS, RET_DK), pos) * (RET_DK ** -0.5)
    rv = rv.reshape(B, T, RET_HEADS, RET_DV)
    yr = retention(rq.transpose(0, 2, 1, 3), rk.transpose(0, 2, 1, 3), rv.transpose(0, 2, 1, 3))
    yr = yr.transpose(0, 2, 1, 3).reshape(B, T, RET_V)
    yr = (jax.nn.silu(rg) * yr) @ w_ret_out
    aq = rope(aq.reshape(B, T, ATT_HEADS, ATT_DH), pos)
    ak = rope(ak.reshape(B, T, ATT_HEADS, ATT_DH), pos)
    av = av.reshape(B, T, ATT_HEADS, ATT_DH)
    iq = rope(iq.reshape(B, T, IDX_HEADS, IDX_DH), pos)
    ik = rope(ik.reshape(B, T, 1, IDX_DH), pos)[:, :, 0]
    ya = dsa_attention(aq, ak, av, iq, ik, iw, k_top).reshape(B, T, ATT_W) @ w_att_out
    merged = jax.nn.sigmoid(g_ret) * yr + jax.nn.sigmoid(g_att) * ya
    return merged @ w_mix_out

def second_inputs(seed: int = 0) -> dict:
    key = jax.random.key(seed)
    ks = jax.random.split(key, 16)
    f32 = jnp.float32

    def dense(k, fan_in, fan_out):
        return jax.random.normal(k, (DEPTH_2, fan_in, fan_out), f32) * fan_in ** -0.5

    def gain(k, shape):
        return 1.0 + 0.02 * jax.random.normal(k, shape, f32)

    return {
        'x': jax.random.normal(ks[0], (BATCH, SEQ, D_MODEL), f32),
        'meta_tokens': jax.random.normal(ks[1], (N_META, D_MODEL), f32),
        'ffn1_norm': gain(ks[2], (DEPTH_2, D_MODEL)),
        'ffn1_w_gate': dense(ks[3], D_MODEL, D_FF),
        'ffn1_w_up': dense(ks[4], D_MODEL, D_FF),
        'ffn1_w_down': dense(ks[5], D_FF, D_MODEL),
        'mix_norm': gain(ks[6], (DEPTH_2, D_MODEL)),
        'w_in': dense(ks[7], D_MODEL, D_IN),
        'w_ret_out': dense(ks[8], RET_V, D_MODEL),
        'w_att_out': dense(ks[9], ATT_W, D_MODEL),
        'w_mix_out': dense(ks[10], D_MODEL, D_MODEL),
        'ffn2_norm': gain(ks[11], (DEPTH_2, D_MODEL)),
        'ffn2_w_gate': dense(ks[12], D_MODEL, D_FF),
        'ffn2_w_up': dense(ks[13], D_MODEL, D_FF),
        'ffn2_w_down': dense(ks[14], D_FF, D_MODEL),
        'final_norm': gain(ks[15], (D_MODEL,)),
    }

def second_block(x, meta_tokens, ffn1_norm, ffn1_w_gate, ffn1_w_up, ffn1_w_down, mix_norm, w_in, w_ret_out, w_att_out, w_mix_out, ffn2_norm, ffn2_w_gate, ffn2_w_up, ffn2_w_down, final_norm):
    B, L, D = x.shape
    k_top = min(TOPK_MAX, L // 4)
    meta = jnp.broadcast_to(meta_tokens.astype(x.dtype)[None], (B, N_META, D))
    h = jnp.concatenate([meta, x], axis=1)
    pos = jnp.arange(h.shape[1], dtype=jnp.int32)
    for l in range(DEPTH_2):
        h = h + 0.5 * swiglu(rmsnorm(h, ffn1_norm[l]), ffn1_w_gate[l], ffn1_w_up[l], ffn1_w_down[l])
        h = h + hybrid_mixer(rmsnorm(h, mix_norm[l]), pos, k_top, w_in[l], w_ret_out[l], w_att_out[l], w_mix_out[l])
        h = h + 0.5 * swiglu(rmsnorm(h, ffn2_norm[l]), ffn2_w_gate[l], ffn2_w_up[l], ffn2_w_down[l])
    y = rmsnorm(h, final_norm)
    return y[:, N_META:]


def setup_inputs(seed=0):
    out = dict(first_inputs(seed))
    for name, value in second_inputs(seed + 1).items():
        if name != "x":
            out[name + "_2"] = value
    return out


def reference(
    x, mem, pre_norm, post_norm, w_out, mem_norm, w_mem_kv, a_w_in, a_shift_mu, a_w0, a_w2,
    a_a0, a_a2, a_k_k, a_k_a, a_r_k, a_lnx_w, a_lnx_b, kv_norm, w_kv, b_w_in, b_lam_q1,
    b_lam_k1, b_lam_q2, b_lam_k2, b_subln, meta_tokens_2, ffn1_norm_2, ffn1_w_gate_2,
    ffn1_w_up_2, ffn1_w_down_2, mix_norm_2, w_in_2, w_ret_out_2, w_att_out_2, w_mix_out_2,
    ffn2_norm_2, ffn2_w_gate_2, ffn2_w_up_2, ffn2_w_down_2, final_norm_2,
):
    x = first_block(
        x, mem, pre_norm, post_norm, w_out, mem_norm, w_mem_kv, a_w_in, a_shift_mu, a_w0, a_w2,
        a_a0, a_a2, a_k_k, a_k_a, a_r_k, a_lnx_w, a_lnx_b, kv_norm, w_kv, b_w_in, b_lam_q1,
        b_lam_k1, b_lam_q2, b_lam_k2, b_subln,
    )
    return second_block(
        x, meta_tokens_2, ffn1_norm_2, ffn1_w_gate_2, ffn1_w_up_2, ffn1_w_down_2, mix_norm_2,
        w_in_2, w_ret_out_2, w_att_out_2, w_mix_out_2, ffn2_norm_2, ffn2_w_gate_2, ffn2_w_up_2,
        ffn2_w_down_2, final_norm_2,
    )


_drawn_inputs = setup_inputs


def setup_inputs(seed=0):
    import zlib

    import numpy as np

    out = dict(_drawn_inputs(seed))
    spreads = {}
    factors = {'mem_norm': 7.294,
     'b_lam_q1': 2.758,
     'b_lam_k1': 4.443,
     'ffn1_norm_2': 8.0,
     'mix_norm_2': 5.692,
     'ffn2_norm_2': 21.468,
     'final_norm_2': 8.295}
    for name, (base, spread) in spreads.items():
        noise = np.random.default_rng([zlib.crc32(name.encode()), seed]).standard_normal(out[name].shape)
        drawn = base * np.exp(spread * noise) if base else spread * noise
        out[name] = __import__('jax').numpy.asarray(drawn.astype(out[name].dtype))
    for name, factor in factors.items():
        out[name] = (out[name] * factor).astype(out[name].dtype)
    return out
```

```python
import math
from contextlib import ExitStack

import numpy as np
import concourse.bass as bass
from concourse import mybir

P = 128
D = 1024
KT = D // P
S = 256
N_META = 16
T = S + N_META
MEM = 256
BR = 768
BT = BR // P
HD = 64
MW = 256
MT = MW // P
MEM_HEADS = 4
Z_TILES = (3 * BR + 128) // P
LAM_INIT = 0.8 - 0.6 * math.exp(-0.3)
RET_HEADS, RET_DV = 4, 512
ATT_HEADS = 8
IDX_HEADS, IDX_DH = 8, 64
TOPK = min(256, S // 4)
FF = 2816
FT = FF // P
EPS = 1e-6
LNX_EPS = 64e-5
CH = 128
DECAY_C = math.exp(-0.5)
MID = DECAY_C * CH / 2
BIG = 1e30
TAKEN = -3e38
QT = [(0, 128, 128), (128, 128, 256), (256, 16, 272)]
QO = [0, 128, 384]
QW = 656
KO = [0, 272, 416]
KQ = [(0, 272), (128, 144), (256, 16)]
KW = 432

F32 = mybir.dt.float32
ALU = mybir.AluOpType
ACT = mybir.ActivationFunctionType
AX_X = mybir.AxisListType.X

VECTORS = [("pre0", 8), ("pre1", 8), ("post0", 8), ("post1", 8), ("memn0", 8), ("memn1", 8), ("kvn", 8),
           ("mu", Z_TILES), ("w0", BT), ("a0", BT), ("kk", BT), ("ka", BT), ("rk", BT), ("lnw", BT), ("lnb", BT),
           ("subln", 1), ("lam", 4), ("ffn1", 8), ("mix", 8), ("ffn2", 8), ("final", 8)]
COL, NCOL = {}, 0
for _name, _n in VECTORS:
    COL[_name] = NCOL
    NCOL += _n

TABLES_A = [("ident", P), ("ones_d", P), ("blk", P), ("blkm", P), ("ones", P), ("ones128", P), ("ones512", P),
            ("dist", 384), ("mid", 2)]
TABLES_R = [("neg_up", P), ("neg_m0", P), ("m0t", P)] + [(f"m{j}", P) for j in range(1, 7)] + [("up", P), ("upinc", P)]
TABLES_B = [("rcos", T), ("rsin", T), ("acos", T), ("asin", T), ("icos", T), ("isin", T), ("decay", RET_HEADS * KW),
            ("adm", QW), ("meta", 3 * N_META)]


def offsets(tables):
    at, out = 0, {}
    for name, n in tables:
        out[name] = (at, n)
        at += n
    return out, at


OFF_A, W_A = offsets(TABLES_A)
OFF_R, W_R = offsets(TABLES_R)
OFF_B, W_B = offsets(TABLES_B)


def alibi_slopes(n):
    c = 2 ** int(math.floor(math.log2(n)))

    def pow2(m):
        start = 2.0 ** (-8.0 / m)
        return [start ** (i + 1) for i in range(m)]
    s = pow2(n) if c == n else pow2(c) + pow2(2 * c)[0::2][: n - c]
    return [float(np.float32(x)) for x in s]


def rope_tables(d):
    inv = (np.float32(10000.0) ** (-np.arange(0, d, 2, dtype=np.float32) / np.float32(d))).astype(np.float32)
    ang = (np.arange(T, dtype=np.float32)[None, :] * inv[:, None]).astype(np.float32)
    return np.cos(ang).astype(np.float32), np.sin(ang).astype(np.float32)


def const_tables():
    i = np.arange(P)
    r, c = i[:, None], i[None, :]
    a = {"ident": r == c, "ones_d": np.full((P, P), 1.0 / D), "blk": (r // HD == c // HD) * 1.0,
         "blkm": (r // HD == c // HD) / HD, "ones": np.ones((P, P)), "ones128": np.full((P, P), 1.0 / P),
         "ones512": np.full((P, P), 1.0 / RET_DV), "mid": np.array([[MID, -MID]] * P)}
    t = np.concatenate([r, 128 + r, 128 + r], 1)
    key = np.arange(384)[None, :]
    key = np.where(key < 128, key, key - 128)
    tok = np.where(np.arange(384)[None, :] < 128, t[:, :1], t[:, 1:2])
    a["dist"] = np.where(key // 64 <= tok // 64, np.abs(tok - key), BIG)
    m = {"neg_up": (c > r) * -1.0, "up": (c > r) * 1.0, "upinc": (c >= r) * 1.0}
    for j in range(7):
        n = 1 << j
        m[f"m{j}"] = ((r // (2 * n) == c // (2 * n)) & (r // n > c // n)) * 1.0
    m["neg_m0"], m["m0t"] = -m["m0"], m["m0"].T
    b = {}
    b["rcos"], b["rsin"] = rope_tables(256)
    co, si = rope_tables(128)
    b["acos"], b["asin"] = np.concatenate([co, co]), np.concatenate([-si, si])
    co, si = rope_tables(64)
    b["icos"], b["isin"] = np.concatenate([co] * 4), np.concatenate([-si, -si, si, si])
    dec = np.zeros((P, RET_HEADS, KW))
    for h in range(RET_HEADS):
        g = np.log1p(-(2.0 ** (-5.0 - h)))
        for j, (q0, n) in enumerate(KQ):
            diff = (q0 + np.arange(n))[None, :] - (P * j + i)[:, None]
            dec[:, h, KO[j]:KO[j] + n] = np.where(diff >= 0, np.exp(g * np.maximum(diff, 0)), 0.0) / 16.0
    b["decay"] = dec.reshape(P, -1)
    adm, meta = np.full((P, QW), -BIG), np.full((P, 3 * N_META), -BIG)
    for j, (q0, n, w) in enumerate(QT):
        q, k = q0 + i[:, None], np.arange(w)[None, :]
        adm[:, QO[j]:QO[j] + w] = np.where((k >= N_META) & (k <= q), 0.0, -BIG)
        k = np.arange(N_META)[None, :]
        meta[:, N_META * j:N_META * (j + 1)] = np.where(k <= q, 0.0, -BIG)
    b["adm"], b["meta"] = adm, meta
    pack = lambda tables, src: np.ascontiguousarray(
        np.concatenate([np.asarray(src[n], np.float32) for n, _ in tables], 1))
    return pack(TABLES_A, a), pack(TABLES_R, m), pack(TABLES_B, b)


class Queue:

    def __init__(self, engine, sem):
        self.engine, self.sem, self.count, self.items, self.met = engine, sem, 0, [], {}

    def wait(self, *marks):
        for mark in marks:
            if mark is None:
                continue
            if isinstance(mark, list):
                self.wait(*mark)
                continue
            sem, value = mark
            if self.met.get(sem, 0) < value:
                self.met[sem] = value
                self.items.append((self.engine.wait_ge, (sem, value), {}, None, 0))

    def op(self, fn, *args, after=(), **kw):
        self.wait(*after)
        self.count += 1
        self.items.append((fn, args, kw, self.sem, 1))
        return (self.sem, self.count)

    def quiet(self, fn, *args, after=(), **kw):
        self.wait(*after)
        self.items.append((fn, args, kw, None, 0))

    def dma(self, out, in_, sem, value, after=()):
        self.wait(*after)
        self.items.append((self.engine.dma_start, (out, in_), {}, sem, 16))
        return (sem, value)

    def last(self):
        return (self.sem, self.count) if self.count else None

    def emit(self):
        for fn, args, kw, sem, inc in self.items:
            ins = fn(*args, **kw)
            if sem is not None:
                ins.then_inc(sem, inc)


class Ring:

    def __init__(self, bufs):
        self.free = [(b, []) for b in bufs]

    def take(self):
        return self.free.pop(0)

    def give(self, buf, *marks):
        self.free.append((buf, list(marks)))


def skewed(streams):
    live, streams = [], list(streams)
    while live or streams:
        if streams:
            live.append(streams.pop(0))
        for g in list(live):
            try:
                next(g)
            except StopIteration:
                live.remove(g)


def build(nc, xT, memT, metaT, vecs, tab_a, tab_r, tab_b, lora, w, outT):
    with ExitStack() as ctx:
        def sem(name):
            return ctx.enter_context(nc.semaphore(name))

        def sb(name, shape, scope=ctx):
            return scope.enter_context(nc.sbuf_tensor(name, shape, F32))

        V = Queue(nc.vector, sem("s_vector"))
        A = Queue(nc.scalar, sem("s_scalar"))
        PE = Queue(nc.tensor, sem("s_tensor"))
        G = Queue(nc.gpsimd, sem("s_pool"))
        SP = Queue(nc.sync, sem("s_sync"))
        vec, act, ten, pool = nc.vector, nc.scalar, nc.tensor, nc.gpsimd

        banks = Ring([ctx.enter_context(nc.psum_tensor(f"bank{i}", [P, 512], F32)) for i in range(8)])

        res = sb("res", [P, KT, T])
        hn = sb("hn", [P, KT, T])
        cols = sb("cols", [P, NCOL])
        ta = sb("ta", [P, W_A])
        rstd = sb("rstd", [P, T])

        N_SLOT = 5
        slots = Ring([(sb(f"wslot{i}", [P, 2048]), sem(f"s_wslot{i}")) for i in range(N_SLOT)])
        slot_fills = {}

        def tab(name):
            o, n = OFF_A[name]
            return ta[:, o:o + n]

        ident = tab("ident")

        def col(name, i=0):
            return cols[:, COL[name] + i:COL[name] + i + 1]

        def load(src, n):
            (buf, s), freed = slots.take()
            slot_fills[s] = slot_fills.get(s, 0) + 16
            return (buf, s), SP.dma(buf[:, 0:n] if len(src.shape) == 2 else
                                    buf[:, 0:n].rearrange("p (c n) -> p c n", c=src.shape[1]),
                                    src, s, slot_fills[s], after=freed)

        s_in = [sem(f"s_in{i}") for i in range(5)]
        m_x = A.dma(res[:, :, N_META:T], xT, s_in[0], 16)
        m_ta = SP.dma(ta[:, :], tab_a, s_in[1], 16)
        m_cols = A.dma(cols[:, :], vecs, s_in[2], 16)

        def groups(panels, size):
            return [panels[i:i + size] for i in range(0, len(panels), size)]

        def project(name, panels, x_tile, n_tok, x_marks, evac, kt=KT):
            wd = w[name]
            per = max(1, 16 // kt)
            for grp in groups(panels, per):
                if kt <= 16:
                    slot, m_w = load(wd[grp[0]:grp[0] + len(grp)].rearrange("c p n -> p c n"), len(grp) * kt * P)
                    parts = [(slot, m_w, 0, kt)]
                else:
                    half = kt // 2
                    parts = []
                    for j in range(2):
                        slot, m_w = load(wd[grp[0]][:, j * half * P:(j + 1) * half * P], half * P)
                        parts.append((slot, m_w, j * half, half))
                for c, panel in enumerate(grp):
                    bank, freed = banks.take()
                    ps = bank[:, 0:n_tok]
                    for slot, m_w, k0, nk in parts:
                        for k in range(nk):
                            kk = k0 + k
                            at = (c * nk + k) * P
                            last = kk == kt - 1
                            args = (ps, slot[0][:, at:at + P], x_tile(kk))
                            end = k == nk - 1 and c == len(grp) - 1
                            if last or end:
                                mark = PE.op(ten.matmul, *args, start=(kk == 0), stop=last,
                                             after=[m_w, x_marks, freed])
                            else:
                                PE.quiet(ten.matmul, *args, start=(kk == 0), stop=last,
                                         after=[m_w, x_marks, freed])
                            if end:
                                slots.give(slot, mark)
                    banks.give(bank, *evac(panel, ps, mark))

        def project_tokens(name, panels, x_rows, x_marks, evac, n_tiles):
            for i0 in range(0, len(panels), 2):
                slot, m_w = load(w[name][panels[i0]:panels[i0] + 2].rearrange("c p n -> p c n"), 2 * D)
                wv = slot[0][:, 0:2 * D].rearrange("p (c k n) -> p c k n", c=2, k=KT)
                for t in range(n_tiles):
                    bank, freed = banks.take()
                    for k in range(KT):
                        fn = PE.op if k == KT - 1 else PE.quiet
                        mark = fn(ten.matmul, bank[:, 0:256].rearrange("p (c n) -> p c n", c=2), x_rows(k, t),
                                  wv[:, :, k, :], start=(k == 0), stop=(k == KT - 1),
                                  after=[m_w, x_marks, freed])
                    banks.give(bank, *evac(i0 // 2, t, bank[:, 0:256], mark))
                slots.give(slot, mark)

        def rsqrt(out, x, eps, op, marks):
            m = V.op(vec.tensor_scalar, out, x, eps, None, op, after=marks)
            m = A.op(act.activation, out, out, ACT.Ln, after=[m])
            return A.op(act.activation, out, out, ACT.Exp, scale=-0.5, after=[m])

        def norm_stat(sq_tile, n, n_tok, table, eps, m_sq, out, freed_out=None):
            bank, freed = banks.take()
            for k in range(n):
                fn = PE.op if k == n - 1 else PE.quiet
                mark = fn(ten.matmul, bank[:, 0:n_tok], tab(table), sq_tile(k), start=(k == 0), stop=(k == n - 1),
                          after=[m_ta, m_sq[k] if isinstance(m_sq, list) else m_sq, freed])
            m = rsqrt(out, bank[:, 0:n_tok], eps, ALU.add, [mark, freed_out])
            banks.give(bank, m)
            return m

        def rmsnorm(src, dst, sq, rs, gain, m_src, n_tok, m_dst_free, m_sq_free=None):
            m_sq = []
            for k in range(KT):
                a = [m_src[k] if isinstance(m_src, list) else m_src, m_sq_free]
                if k % 2:
                    m_sq.append(V.op(vec.tensor_tensor, sq[:, k, 0:n_tok], src(k), src(k), ALU.mult, after=a))
                else:
                    m_sq.append(A.op(act.activation, sq[:, k, 0:n_tok], src(k), ACT.Square, after=a))
            m_rs = norm_stat(lambda k: sq[:, k, 0:n_tok], KT, n_tok, "ones_d", EPS, m_sq, rs, m_dst_free)
            return [V.op(vec.scalar_tensor_tensor, dst(k), src(k), col(gain, k), rs, ALU.mult, ALU.mult,
                         after=[m_rs, m_cols, m_dst_free]) for k in range(KT)]

        def everyone():
            return [q.last() for q in (V, A, PE, G, SP)]

        def new_phase():
            marks = everyone()
            for q in (V, A, PE, G):
                q.wait(*marks)
            return marks

        first = ExitStack()
        kmT = sb("kmT", [P, 2, MT, MEM], first)
        vm = sb("vm", [P, 2, MEM // P, MW], first)
        ymix = sb("ymix", [P, KT, S], first)
        tmp256 = Ring([sb(f"tmp{i}", [P, S], first) for i in range(4)])
        small = sb("small", [P, 48], first)
        x1 = lambda k: res[:, k, N_META:T]
        h1 = lambda k: hn[:, k, 0:S]

        def memory_attention(layer, qm, gm, m_q, m_kv, m_g, bufs):
            marks = []

            def head(h):
                j, o = h // 2, HD * (h % 2)
                pbuf, freed_p = bufs["p"].take()
                ptb, freed_pt = bufs["pt"].take()
                st, freed_st = bufs["st"].take()
                bank, freed = banks.take()
                for t in range(2):
                    m_s = PE.op(ten.matmul, bank[:, t * MEM:(t + 1) * MEM], qm[o:o + HD, j, t * P:(t + 1) * P],
                                kmT[o:o + HD, layer, j, :], start=True, stop=True, after=[m_q, m_kv, freed])
                sc = bank[:, :].rearrange("p (t m) -> p t m", t=2)
                m1 = V.op(vec.tensor_reduce, st[:, 0:2], sc, AX_X, ALU.max, after=[m_s, freed_st])
                m2 = V.op(vec.tensor_scalar, st[:, 2:4], st[:, 0:2], -(HD ** -0.5), None, ALU.mult, after=[m1])
                for t in range(2):
                    m3 = A.op(act.activation, pbuf[:, t, :], sc[:, t, :], ACT.Exp, bias=st[:, 2 + t:3 + t],
                              scale=HD ** -0.5, accum_out=st[:, 4 + t:5 + t], after=[m2, freed_p])
                banks.give(bank, m3)
                m4 = V.op(vec.reciprocal, st[:, 6:8], st[:, 4:6], after=[m3])
                for t in range(2):
                    m5 = V.op(vec.tensor_scalar, pbuf[:, t, :], pbuf[:, t, :], st[:, 6 + t:7 + t], None, ALU.mult,
                              after=[m4])
                yield
                bank, freed = banks.take()
                pt = bank[:, :].rearrange("p (k q) -> p k q", k=2)
                for t in range(2):
                    for k in range(2):
                        m6 = PE.op(ten.transpose, pt[:, k, t * P:(t + 1) * P], pbuf[:, t, k * P:(k + 1) * P], ident,
                                   after=[m5, freed])
                m7 = A.op(act.activation, ptb[:, :, :], pt, ACT.Copy, after=[m6, freed_pt])
                banks.give(bank, m7)
                bufs["p"].give(pbuf, m6)
                bufs["st"].give(st, m5)
                yield
                bank, freed = banks.take()
                for k in range(2):
                    m8 = PE.op(ten.matmul, bank[o:o + HD, 0:S], vm[:, layer, k, h * HD:(h + 1) * HD], ptb[:, k, :],
                               start=(k == 0), stop=(k == 1), after=[m7, m_kv, freed])
                bufs["pt"].give(ptb, m8)
                m9 = V.op(vec.tensor_tensor, ymix[o:o + HD, BT + j, :], bank[o:o + HD, 0:S], gm[o:o + HD, j, :],
                          ALU.mult, after=[m8, m_g])
                banks.give(bank, m9)
                marks.append(m9)
                yield

            skewed(head(h) for h in range(MEM_HEADS))
            return marks

        def mix_out(layer, m_y, ybuf, sqbuf):
            m_yt, m_sq = [None] * KT, [None] * KT

            def evac(panel, ps, mark):
                m_yt[panel] = V.op(vec.tensor_copy, ybuf[:, panel, :], ps, after=[mark])
                m_sq[panel] = A.op(act.activation, sqbuf[:, panel, :], ybuf[:, panel, :], ACT.Square,
                                   after=[m_yt[panel]])
                return (m_yt[panel],)

            project(f"w_out{layer}", list(range(KT)), lambda k: ymix[:, k, :], S, m_y, evac)
            m_rs = norm_stat(lambda k: sqbuf[:, k, :], KT, S, "ones_d", EPS, m_sq, rstd[:, 0:S])
            out = []
            for k in range(KT):
                m = V.op(vec.scalar_tensor_tensor, ybuf[:, k, :], ybuf[:, k, :], col(f"post{layer}", k),
                         rstd[:, 0:S], ALU.mult, ALU.mult, after=[m_rs, m_yt[k]])
                out.append(V.op(vec.tensor_tensor, x1(k), x1(k), ybuf[:, k, :], ALU.add, after=[m]))
            return out

        ph = ExitStack()
        tr = sb("tr", [P, W_R], ph)
        zr, zk, zv = (sb(n, [P, BT, S], ph) for n in ("zr", "zk", "zv"))
        zl = sb("zl", [P, S], ph)
        gate = sb("gate", [P, BT, S], ph)
        qm = sb("qm", [P, MT, MEM], ph)
        gm = sb("gm", [P, MT, MEM], ph)
        ed = sb("ed", [P, BT, 2, CH + 1], ph)
        inv = sb("inv", [P, BT, S], ph)
        av_ = sb("av_", [P, BT, S], ph)
        kk = sb("kkh", [P, BT, S], ph)
        mem_hg = sb("mem_hg", [P, 2 * KT * MEM], ph)
        mem_h = mem_hg[:, 0:KT * MEM].rearrange("p (k m) -> p k m", k=KT)
        mem_g = mem_hg[:, KT * MEM:].rearrange("p (k m) -> p k m", k=KT)
        zt_ring = Ring([sb(f"zt{i}", [P, S + 1], ph) for i in range(2)])
        lw = sb("lw", [P, 2 * BR], ph)
        work = sb("work", [P, 5, 1024], ph)
        xt_all = sb("xt_all", [P, 6, 512], ph)
        wu_u = sb("wu_u", [P, 2, BT * HD], ph)
        st1 = sb("st1", [P, BT, HD], ph)
        vtok = mem_hg[:, 0:2 * BR].rearrange("p (c n) -> p c n", c=2)
        btok, ktok = mem_hg[:, 2 * BR:3 * BR], mem_hg[:, 3 * BR:4 * BR]
        wu_w = mem_hg[:, 4 * BR:5 * BR].rearrange("p (h n) -> p h n", h=2)
        ysb = hn[:, :, :].rearrange("p a b -> p (a b)")[:, 0:BT * S].rearrange("p (i s) -> p i s", i=BT)

        def tabr(name):
            o, n = OFF_R[name]
            return tr[:, o:o + n]

        m_mem = A.dma(mem_h[:, :, :], memT, s_in[3], 16)
        m_lw = A.dma(lw[:, 0:BR], lora, s_in[4], 16)
        s_in2 = [sem("s_tab_r"), sem("s_tab_b"), sem("s_meta")]
        m_tr = A.dma(tr[:, :], tab_r, s_in2[0], 16)
        m_zero = V.op(vec.memset, zt_ring.free[0][0][:, 0:1], 0.0)
        m_zero = V.op(vec.memset, zt_ring.free[1][0][:, 0:1], 0.0)
        m_zero = V.op(vec.memset, ed[:, :, :, 0:1], 0.0)
        work_flat = work[:, :, :].rearrange("p a b -> p (a b)")
        sq = work_flat[:, 0:KT * S].rearrange("p (k s) -> p k s", k=KT)
        m_h = rmsnorm(x1, h1, sq, rstd[:, 0:S], "pre0", m_x, S, None)

        m_z = {}

        def shift_evac(panel, ps, mark):
            if panel == 18:
                dst = zl[:, :]
            else:
                dst = (zr, zk, zv)[panel // BT][:, panel % BT, :]
            zt, freed = zt_ring.take()
            m1 = A.op(act.activation, zt[:, 1:S + 1], ps, ACT.Copy, after=[mark, freed, m_zero])
            m2 = V.op(vec.tensor_tensor, dst, zt[:, 0:S], zt[:, 1:S + 1], ALU.subtract, after=[m1])
            m_z[panel] = V.op(vec.scalar_tensor_tensor, dst, dst, col("mu", panel), zt[:, 1:S + 1],
                              ALU.mult, ALU.add, after=[m2, m_cols])
            zt_ring.give(zt, m_z[panel])
            return (m1,)

        project("a_w_in", [18], h1, S, m_h, shift_evac)
        m_th = A.op(act.activation, zl[0:64, :], zl[0:64, :], ACT.Tanh, after=[m_z[18]])
        m_ed, m_inv, m_a = {}, {}, {}
        ones_s = tab("ones")

        m_cum = {}

        def low_rank(i):
            bank, freed = banks.take()
            m = PE.op(ten.matmul, bank[:, 0:S], lw[0:64, i * P:(i + 1) * P], zl[0:64, :], start=True, stop=True,
                      after=[m_lw, m_th, freed])
            e, freed_e = tmp256.take()
            m1 = A.op(act.activation, e[:, :], bank[:, 0:S], ACT.Sigmoid, bias=col("w0", i),
                      after=[m, m_cols, freed_e])
            banks.give(bank, m1)
            for c in range(2):
                m_cum[i] = V.op(vec.tensor_tensor_scan, ed[:, i, c, 1:CH + 1], ones_s, e[:, c * CH:(c + 1) * CH],
                                0.0, ALU.mult, ALU.add, after=[m1, m_ta, m_zero])
            tmp256.give(e, m_cum[i])
            bank, freed = banks.take()
            m = PE.op(ten.matmul, bank[:, 0:S], lw[64:128, i * P:(i + 1) * P], zl[64:128, :], start=True, stop=True,
                      after=[m_lw, m_z[18], freed])
            m_a[i] = A.op(act.activation, av_[:, i, :], bank[:, 0:S], ACT.Sigmoid, bias=col("a0", i), after=[m])
            banks.give(bank, m_a[i])

        def decays(i):
            mid = tab("mid")
            m_inv[i] = A.op(act.activation, inv[:, i, :].rearrange("p (c t) -> p c t", c=2), ed[:, i, :, 1:CH + 1],
                            ACT.Exp, bias=mid[:, 1:2], scale=DECAY_C, after=[m_cum[i], m_ta])
            m_ed[i] = A.op(act.activation, ed[:, i, :, :], ed[:, i, :, :], ACT.Exp, bias=mid[:, 0:1],
                           scale=-DECAY_C, after=[m_inv[i]])

        project("a_w_in", [6, 7], h1, S, m_h, shift_evac)
        for i in range(BT):
            low_rank(i)
        for i in range(BT):
            decays(i)
        project("a_w_in", [8, 9, 10, 11], h1, S, m_h, shift_evac)

        m_ah, m_bt, m_kt_, m_rh, m_km, m_kk = {}, {}, {}, {}, {}, {}

        def keys(i):
            t, freed_t = tmp256.take()
            m1 = V.op(vec.tensor_scalar, kk[:, i, :], zk[:, i, :], col("kk", i), None, ALU.mult,
                      after=[m_z[6 + i], m_cols])
            m2 = A.op(act.activation, t[:, :], kk[:, i, :], ACT.Square, after=[m1, freed_t])
            bank, freed = banks.take()
            m3 = PE.op(ten.matmul, bank[:, 0:S], tab("blk"), t[:, :], start=True, stop=True, after=[m2, m_ta, freed])
            m4 = rsqrt(t[:, :], bank[:, 0:S], 1e-12, ALU.max, [m3])
            banks.give(bank, m4)
            m5 = V.op(vec.tensor_tensor, kk[:, i, :], kk[:, i, :], t[:, :], ALU.mult, after=[m4, m2])
            m6 = V.op(vec.tensor_scalar, t[:, :], av_[:, i, :], 1.0, col("ka", i), ALU.subtract, ALU.mult,
                      after=[m5, m_a[i]])
            m_km[i] = V.op(vec.scalar_tensor_tensor, zk[:, i, :], t[:, :], 1.0, zk[:, i, :], ALU.add, ALU.mult,
                           after=[m6])
            tmp256.give(t, m_km[i])
            m7 = V.op(vec.tensor_tensor, av_[:, i, :], av_[:, i, :], kk[:, i, :], ALU.mult, after=[m6])
            m_bt[i] = V.op(vec.tensor_tensor, av_[:, i, :], av_[:, i, :], inv[:, i, :], ALU.mult,
                           after=[m7, m_inv[i]])
            m_kt_[i] = V.op(vec.tensor_tensor, inv[:, i, :], inv[:, i, :], zk[:, i, :], ALU.mult,
                            after=[m_bt[i], m_km[i]])
            split = lambda buf: buf[:, i, :].rearrange("p (c t) -> p c t", c=2)
            m_ah[i] = V.op(vec.tensor_tensor, split(kk), split(kk), ed[:, i, :, 0:CH], ALU.mult,
                           after=[m7, m_ed[i]])

        for i in range(BT):
            keys(i)
            project("a_w_in", [i], h1, S, m_h, shift_evac)

        GROUPS = [(p, j) for p in range(2) for j in range(3)]
        b4 = lambda a: a.unsqueeze(1).broadcast_to([P, 4, P])
        v4 = lambda a: a.rearrange("p (g n) -> p g n", g=4)
        m_sq_done = everyone()

        def pieces(g):
            p, j = GROUPS[g]
            for q in range(4):
                yield q, 2 * j + q // 2, HD * p, (q % 2) * CH

        filler = []

        def fill(n=1):
            for _ in range(n):
                if filler:
                    filler.pop(0)()

        m_xt = {}

        def invert(g):
            slot = g % 3
            nlt, xx, yy = work_flat[:, slot * 1536:slot * 1536 + 512], \
                work_flat[:, slot * 1536 + 512:slot * 1536 + 1024], work_flat[:, slot * 1536 + 1024:slot * 1536 + 1536]
            xt = xt_all[:, g, :]
            bank, freed = banks.take()
            for q, i, o, t0 in pieces(g):
                m = PE.op(ten.matmul, bank[:, q * P:(q + 1) * P], av_[o:o + HD, i, t0:t0 + CH],
                          kk[o:o + HD, i, t0:t0 + CH], start=True, stop=True, after=[m_bt[i], m_ah[i], freed])
            m_nlt = V.op(vec.tensor_tensor, v4(nlt), v4(bank[:, :]), b4(tabr("neg_up")), ALU.mult,
                         after=[m, m_tr, m_sq_done])
            banks.give(bank, m_nlt)
            bank, freed = banks.take()
            for q, i, o, t0 in pieces(g):
                m = PE.op(ten.matmul, bank[:, q * P:(q + 1) * P], kk[o:o + HD, i, t0:t0 + CH],
                          av_[o:o + HD, i, t0:t0 + CH], start=True, stop=True, after=[freed])
            m1 = V.op(vec.tensor_tensor, v4(xx), v4(bank[:, :]), b4(tabr("neg_m0")), ALU.mult, after=[m])
            banks.give(bank, m1)
            m_x_ = V.op(vec.tensor_tensor, v4(xx), v4(xx), b4(ident), ALU.add, after=[m1])
            m2 = V.op(vec.tensor_tensor, v4(xt), v4(nlt), b4(tabr("m0t")), ALU.mult, after=[m_nlt])
            m_t_ = V.op(vec.tensor_tensor, v4(xt), v4(xt), b4(ident), ALU.add, after=[m2])
            for level in range(1, 7):
                yield
                bank, freed = banks.take()
                for q in range(4):
                    c = slice(q * P, (q + 1) * P)
                    m = PE.op(ten.matmul, bank[:, c], nlt[:, c], xx[:, c], start=True, stop=True,
                              after=[m_x_, m_nlt, freed])
                m_y = V.op(vec.tensor_tensor, v4(yy), v4(bank[:, :]), b4(tabr(f"m{level}")), ALU.mult, after=[m])
                banks.give(bank, m_y)
                yield
                if level < 6:
                    bank, freed = banks.take()
                    for q in range(4):
                        c = slice(q * P, (q + 1) * P)
                        m = PE.op(ten.matmul, bank[:, c], xt[:, c], yy[:, c], start=True, stop=True,
                                  after=[m_y, m_t_, freed])
                    m_x_ = V.op(vec.tensor_tensor, xx, xx, bank[:, :], ALU.add, after=[m])
                    banks.give(bank, m_x_)
                bank, freed = banks.take()
                for q in range(4):
                    c = slice(q * P, (q + 1) * P)
                    m = PE.op(ten.matmul, bank[:, c], yy[:, c], xt[:, c], start=True, stop=True,
                              after=[m_y, m_t_, freed])
                m_t_ = V.op(vec.tensor_tensor, xt, xt, bank[:, :], ALU.add, after=[m])
                banks.give(bank, m_t_)
                fill()
            m_xt[g] = m_t_

        m_kv = {0: [], 1: []}
        m_gmem, m_gate, m_qm = [], [], []


        def kv_prepare(layer, m_free):
            return [A.op(act.activation, mem_g[:, k, :], mem_h[:, k, :], ACT.Copy, scale=col(f"memn{layer}", k),
                         after=[m_memh, m_free, m_cols]) for k in range(KT)]

        m_sqm = []
        for k in range(KT):
            m_sqm.append(A.op(act.activation, mem_g[:, k, :], mem_h[:, k, :], ACT.Square, after=[m_mem]))
        mrs, freed_mrs = tmp256.take()
        m_mrs = norm_stat(lambda k: mem_g[:, k, :], KT, MEM, "ones_d", EPS, m_sqm, mrs[:, :], freed_mrs)
        for k in range(KT):
            m_memh = V.op(vec.tensor_tensor, mem_h[:, k, :], mem_h[:, k, :], mrs[:, :], ALU.mult, after=[m_mrs])
        tmp256.give(mrs, m_memh)
        m_use = {}

        def kv_keys(layer):
            m_use[layer] = kv_prepare(layer, [m_mrs] if layer == 0 else [PE.last()])

            def evac(panel, ps, mark):
                m = A.op(act.activation, kmT[:, layer, panel, :], ps, ACT.Copy, after=[mark])
                m_kv[layer].append(m)
                return (m,)
            project(f"w_mem{layer}", [0, 1], lambda k: mem_g[:, k, :], MEM, m_use[layer], evac)

        def kv_values(layer):
            def evac(_, t, ps, mark):
                m = A.op(act.activation, vm[:, layer, t, :], ps, ACT.Copy, after=[mark])
                m_kv[layer].append(m)
                return (m,)
            project_tokens(f"w_mem{layer}", [2, 3], lambda k, t: mem_g[:, k, t * P:(t + 1) * P], m_use[layer], evac, 2)

        def silu_evac(dst, marks):
            def evac(panel, ps, mark):
                t, freed = tmp256.take()
                m1 = A.op(act.activation, t[:, :], ps, ACT.Sigmoid, after=[mark, freed])
                m3 = V.op(vec.tensor_tensor, dst(panel), t[:, :], ps, ALU.mult, after=[m1])
                tmp256.give(t, m3)
                marks.append(m3)
                return (m3,)
            return evac

        def qm_evac(panel, ps, mark):
            m = A.op(act.activation, qm[:, panel - 25, :], ps, ACT.Copy, after=[mark])
            m_qm.append(m)
            return (m,)

        gate_evac = silu_evac(lambda p_: gate[:, p_ - 19, :], m_gate)
        gm_evac = silu_evac(lambda p_: gm[:, p_ - 27, :], m_gmem)
        for pair in ([12, 13], [14, 15], [16, 17]):
            filler.append(lambda pair=pair: project("a_w_in", pair, h1, S, m_h, shift_evac))
        for pair in ([19, 20], [21, 22], [23, 24]):
            filler.append(lambda pair=pair: project("a_w_in", pair, h1, S, m_h, gate_evac))
        filler.append(lambda: project("a_w_in", [25, 26], h1, S, m_h, qm_evac))
        filler.append(lambda: project("a_w_in", [27, 28], h1, S, m_h, gm_evac))
        for layer in range(2):
            filler.append(lambda layer=layer: kv_keys(layer))
            filler.append(lambda layer=layer: kv_values(layer))

        skewed(invert(g) for g in range(3))
        skewed(invert(g) for g in range(3, 6))
        fill(len(filler))

        m_bonus, m_vt, m_bk = [], {}, {}
        A.wait(*everyone())
        for c in range(2):
            for part in range(2):
                bank, freed = banks.take()
                for n in range(3):
                    i = 3 * part + n
                    m = PE.op(ten.transpose, bank[:, n * P:(n + 1) * P], zv[:, i, c * CH:(c + 1) * CH], ident,
                              after=[m_z[12 + i], freed])
                m_vt[c, part] = A.op(act.activation, vtok[:, c, part * 384:(part + 1) * 384], bank[:, 0:384],
                                     ACT.Copy, after=[m])
                banks.give(bank, m_vt[c, part])
        for dst, src in ((btok, av_), (ktok, inv)):
            for part in range(2):
                bank, freed = banks.take()
                for n in range(3):
                    i = 3 * part + n
                    m = PE.op(ten.transpose, bank[:, n * P:(n + 1) * P], src[:, i, 0:CH], ident,
                              after=[m_kt_[i], freed])
                m_bk[src is inv, part] = A.op(act.activation, dst[:, part * 384:(part + 1) * 384], bank[:, 0:384],
                                              ACT.Copy, after=[m])
                banks.give(bank, m_bk[src is inv, part])

        for i in range(BT):
            t, freed_t = tmp256.take()
            m1 = V.op(vec.scalar_tensor_tensor, t[:, :], zr[:, i, :], col("rk", i), zk[:, i, :], ALU.mult, ALU.mult,
                      after=[m_z[i], m_km[i], freed_t])
            bank, freed = banks.take()
            m2 = PE.op(ten.matmul, bank[:, 0:S], tab("blk"), t[:, :], start=True, stop=True, after=[m1, freed])
            m3 = V.op(vec.tensor_tensor, zk[:, i, :], bank[:, 0:S], zv[:, i, :], ALU.mult,
                      after=[m2, m_z[12 + i], m_kt_[i]])
            banks.give(bank, m3)
            m_bonus.append(m3)
            tmp256.give(t, m2)
            split = lambda buf: buf[:, i, :].rearrange("p (c t) -> p c t", c=2)
            m_rh[i] = V.op(vec.tensor_tensor, split(zr), split(zr), ed[:, i, :, 1:CH + 1], ALU.mult,
                           after=[m1, m_ed[i]])

        m_ysb = {}
        m_state = None
        m_prev = [m_xt[g] for g in range(6)]
        for c in range(2):
            t0 = c * CH
            mats = {}
            for kind, lhs, rhs, mask in (("ak", inv, kk, "up"), ("rb", av_, zr, "upinc"), ("rk", inv, zr, "upinc")):
                base = {"ak": 0, "rb": 1536, "rk": 3072}[kind]
                for p in range(2):
                    for half in range(2):
                        bank, freed = banks.take()
                        for n in range(3):
                            i = 3 * half + n
                            o = HD * p
                            m = PE.op(ten.matmul, bank[:, n * P:(n + 1) * P], lhs[o:o + HD, i, t0:t0 + CH],
                                      rhs[o:o + HD, i, t0:t0 + CH], start=True, stop=True,
                                      after=[m_kt_[i], m_ah[i], m_rh[i], freed])
                        dst = work_flat[:, base + (p * 2 + half) * 384:base + (p * 2 + half + 1) * 384]
                        m = V.op(vec.tensor_tensor, dst.rearrange("p (g n) -> p g n", g=3),
                                 bank[:, 0:384].rearrange("p (g n) -> p g n", g=3),
                                 tabr(mask).unsqueeze(1).broadcast_to([P, 3, P]), ALU.mult, after=[m, m_prev])
                        banks.give(bank, m)
                        for n in range(3):
                            mats[kind, p, 3 * half + n] = (dst[:, n * P:(n + 1) * P], m)
            m_u = {}
            for p in range(2):
                bank, freed = banks.take()
                for i in range(BT):
                    out = bank[:, i * HD:(i + 1) * HD]
                    h = 2 * i + p
                    a, m_a_ = mats["ak", p, i]
                    if c:
                        PE.quiet(ten.matmul, out, kk[HD * p:HD * p + HD, i, t0:t0 + CH], st1[HD * p:HD * p + HD, i, :],
                                 start=True, stop=False, after=[m_state, freed])
                    m = PE.op(ten.matmul, out, a, vtok[:, c, h * HD:(h + 1) * HD], start=not c, stop=True,
                              after=[m_a_, m_vt[c, i // 3], freed])
                m = A.op(act.activation, wu_w[:, p, :], bank[:, 0:BT * HD], ACT.Copy, after=[m])
                banks.give(bank, m)
                m_u["w", p] = m
            for p in range(2):
                bank, freed = banks.take()
                for i in range(BT):
                    g, q = 3 * p + i // 2, 2 * (i % 2) + c
                    m = PE.op(ten.matmul, bank[:, i * HD:(i + 1) * HD], xt_all[:, g, q * P:(q + 1) * P],
                              wu_w[:, p, i * HD:(i + 1) * HD], start=True, stop=True,
                              after=[m_u["w", p], m_xt[g], freed])
                m = A.op(act.activation, wu_u[:, p, :], bank[:, 0:BT * HD], ACT.Copy, scale=-1.0, after=[m])
                banks.give(bank, m)
                m_u[p] = m
            for i in range(BT):
                bank, freed = banks.take()
                for p in range(2):
                    h, o = 2 * i + p, HD * p
                    out = bank[o:o + HD, 0:CH]
                    vt = vtok[:, c, h * HD:(h + 1) * HD]
                    PE.quiet(ten.matmul, out, wu_u[:, p, i * HD:(i + 1) * HD], mats["rb", p, i][0], start=True,
                             stop=False, after=[m_u[p], mats["rb", p, i][1], freed])
                    m = PE.op(ten.matmul, out, vt, mats["rk", p, i][0], start=False, stop=(c == 0),
                              after=[mats["rk", p, i][1]])
                    if c:
                        m = PE.op(ten.matmul, out, st1[o:o + HD, i, :], zr[o:o + HD, i, t0:t0 + CH], start=False,
                                  stop=True)
                m_ysb[c, i] = A.op(act.activation, ysb[:, i, t0:t0 + CH], bank[:, 0:CH], ACT.Copy, after=[m])
                banks.give(bank, m_ysb[c, i])
            m_prev = [PE.last()]
            if c == 0:
                bank, freed = banks.take()
                for i in range(BT):
                    for p in range(2):
                        h, o = 2 * i + p, HD * p
                        out = bank[o:o + HD, i * HD:(i + 1) * HD]
                        PE.quiet(ten.matmul, out, btok[:, h * HD:(h + 1) * HD], wu_u[:, p, i * HD:(i + 1) * HD],
                                 start=True, stop=False, after=[m_bk[False, i // 3], freed])
                        m = PE.op(ten.matmul, out, ktok[:, h * HD:(h + 1) * HD], vtok[:, 0, h * HD:(h + 1) * HD],
                                  start=False, stop=True, after=[m_bk[True, i // 3]])
                for i in range(BT):
                    m_state = V.op(vec.tensor_scalar, st1[:, i, :], bank[:, i * HD:(i + 1) * HD],
                                   ed[:, i, 0, CH:CH + 1], math.exp(-MID), ALU.mult, ALU.mult, after=[m, m_ed[i]])
                banks.give(bank, m_state)
                m_prev = [PE.last()]

        xt_flat = xt_all[:, :, :].rearrange("p a b -> p (a b)")
        quarter = [xt_flat[:, i * 512:(i + 1) * 512].rearrange("p (a b) -> p a b", a=2) for i in range(4)]
        A.wait(*m_prev)
        bufs = {"p": Ring(quarter[0:2]), "pt": Ring(quarter[2:4]),
                "st": Ring([sb(f"mst{i}", [P, 8], ph) for i in range(3)])}
        m_y = memory_attention(0, qm, gm, m_qm, m_kv[0], m_gmem, bufs)

        for i in range(BT):
            d, freed_d = tmp256.take()
            t, freed_t = tmp256.take()
            bank, freed = banks.take()
            m1 = PE.op(ten.matmul, bank[:, 0:S], tab("blkm"), ysb[:, i, :], start=True, stop=True,
                       after=[m_ysb[0, i], m_ysb[1, i], freed])
            m2 = V.op(vec.tensor_tensor, d[:, :], ysb[:, i, :], bank[:, 0:S], ALU.subtract, after=[m1, freed_d])
            banks.give(bank, m2)
            m3 = A.op(act.activation, t[:, :], d[:, :], ACT.Square, after=[m2, freed_t])
            bank, freed = banks.take()
            m4 = PE.op(ten.matmul, bank[:, 0:S], tab("blkm"), t[:, :], start=True, stop=True, after=[m3, freed])
            m5 = rsqrt(t[:, :], bank[:, 0:S], LNX_EPS, ALU.add, [m4])
            banks.give(bank, m5)
            m6 = V.op(vec.scalar_tensor_tensor, d[:, :], d[:, :], col("lnw", i), t[:, :], ALU.mult, ALU.mult,
                      after=[m5, m3])
            tmp256.give(t, m6)
            m7 = V.op(vec.scalar_tensor_tensor, d[:, :], d[:, :], col("lnb", i), zk[:, i, :], ALU.add, ALU.add,
                      after=[m6, m_bonus[i]])
            m8 = V.op(vec.tensor_tensor, ymix[:, i, :], d[:, :], gate[:, i, :], ALU.mult, after=[m7, m_gate])
            tmp256.give(d, m8)
            m_y.append(m8)

        ybuf = work_flat[:, 0:2048].rearrange("p (k s) -> p k s", k=KT)
        sqb = work_flat[:, 2048:4096].rearrange("p (k s) -> p k s", k=KT)
        V.wait(*m_prev)
        A.wait(*m_prev)
        m_res = mix_out(0, m_y, ybuf, sqb)
        m_old = new_phase()
        ph.close()

        ph = ExitStack()
        hk = sb("hk", [P, KT, S], ph)
        sq = sb("sq", [P, KT, S], ph)
        kT = sb("kT", [P, BT, S], ph)
        qT = sb("qT", [P, BT, S], ph)
        vt = sb("vt", [P, 2, BR], ph)
        gate = sb("gate1", [P, BT, S], ph)
        qm = sb("qm1", [P, MT, MEM], ph)
        gm = sb("gm1", [P, MT, MEM], ph)
        ybuf = sb("ybuf1", [P, KT, S], ph)
        bufs = {"p": Ring([sb(f"mp1{i}", [P, 2, MEM], ph) for i in range(2)]),
                "pt": Ring([sb(f"mpt1{i}", [P, 2, S], ph) for i in range(2)]),
                "st": Ring([sb(f"mst1{i}", [P, 8], ph) for i in range(3)])}
        scb = Ring([sb(f"scb{i}", [P, 2, 384], ph) for i in range(3)])
        ptb1 = Ring([sb(f"ptb1{i}", [P, 384], ph) for i in range(2)])
        stb = Ring([sb(f"stb{i}", [P, 16], ph) for i in range(4)])

        m_h = rmsnorm(x1, h1, sq, rstd[:, 0:S], "pre1", m_res, S, None)
        m_hk = [V.op(vec.scalar_tensor_tensor, hk[:, k, :], x1(k), col("kvn", k), rstd[:, 0:S], ALU.mult, ALU.mult,
                     after=[m_h[k]]) for k in range(KT)]
        LQ = 2 * BT
        m = V.op(vec.tensor_tensor, small[:, LQ:LQ + 2], cols[:, COL["lam"]:COL["lam"] + 2],
                 cols[:, COL["lam"] + 2:COL["lam"] + 4], ALU.mult)
        bank, freed = banks.take()
        m = PE.op(ten.matmul, bank[:, 0:2], tab("ones"), small[:, LQ:LQ + 2], start=True, stop=True, after=[m, freed])
        m = A.op(act.activation, small[:, LQ + 2:LQ + 4], bank[:, 0:2], ACT.Exp, after=[m])
        banks.give(bank, m)
        m = V.op(vec.tensor_tensor, small[:, LQ + 4:LQ + 5], small[:, LQ + 3:LQ + 4], small[:, LQ + 2:LQ + 3],
                 ALU.subtract, after=[m])
        m_lam = V.op(vec.tensor_scalar, small[:, LQ + 5:LQ + 6], small[:, LQ + 4:LQ + 5], LAM_INIT, None,
                     ALU.subtract, after=[m])
        m_sub = V.op(vec.tensor_scalar, small[:, LQ + 6:LQ + 7], col("subln"), 1.0 - LAM_INIT, None, ALU.mult)
        neg_lam, subln = small[:, LQ + 5:LQ + 6], small[:, LQ + 6:LQ + 7]

        m_q, m_k, m_v, m_qm, m_gmem, m_gate = {}, {}, {}, [], [], []

        def q_evac(panel, ps, mark):
            m_q[panel] = A.op(act.activation, qT[:, panel, :], ps, ACT.Copy, scale=HD ** -0.5, after=[mark])
            return (m_q[panel],)

        def k_evac(panel, ps, mark):
            m_k[panel] = A.op(act.activation, kT[:, panel, :], ps, ACT.Copy, after=[mark])
            return (m_k[panel],)

        def v_evac(pair, t, ps, mark):
            m_v[pair, t] = A.op(act.activation, vt[:, t, pair * 256:(pair + 1) * 256], ps, ACT.Copy, after=[mark])
            return (m_v[pair, t],)

        def qm_evac1(panel, ps, mark):
            m = A.op(act.activation, qm[:, panel - 12, :], ps, ACT.Copy, after=[mark])
            m_qm.append(m)
            return (m,)

        gate_evac = silu_evac(lambda p_: gate[:, p_ - 6, :], m_gate)
        gm_evac = silu_evac(lambda p_: gm[:, p_ - 14, :], m_gmem)
        slopes = alibi_slopes(BT)
        m_y = []

        def diff_head(h):
            st, freed_st = stb.take()
            pb, freed_p = scb.take()
            for c in range(2):
                o = HD * c
                bank, freed = banks.take()
                PE.quiet(ten.matmul, bank[:, 0:P], qT[o:o + HD, h, 0:P], kT[o:o + HD, h, 0:P], start=True, stop=True,
                         after=[m_q[h], m_k[h], freed])
                m = PE.op(ten.matmul, bank[:, P:384], qT[o:o + HD, h, P:S], kT[o:o + HD, h, :], start=True, stop=True)
                m1 = V.op(vec.scalar_tensor_tensor, pb[:, c, :], tab("dist"), -slopes[h], bank[:, 0:384], ALU.mult,
                          ALU.add, after=[m, freed_p, freed_st])
                banks.give(bank, m1)
                V.op(vec.tensor_reduce, st[:, 2 * c:2 * c + 1], pb[:, c, 0:P], AX_X, ALU.max, after=[m1])
                m2 = V.op(vec.tensor_reduce, st[:, 2 * c + 1:2 * c + 2], pb[:, c, P:384], AX_X, ALU.max)
            m3 = V.op(vec.tensor_scalar, st[:, 4:8], st[:, 0:4], -1.0, None, ALU.mult, after=[m2])
            for c in range(2):
                for t, (a, b) in enumerate(((0, P), (P, 384))):
                    n = 2 * c + t
                    m4 = A.op(act.activation, pb[:, c, a:b], pb[:, c, a:b], ACT.Exp, bias=st[:, 4 + n:5 + n],
                              accum_out=st[:, 8 + n:9 + n], after=[m3])
            m5 = V.op(vec.reciprocal, st[:, 12:16], st[:, 8:12], after=[m4])
            m6 = V.op(vec.tensor_scalar, st[:, 14:16], st[:, 14:16], neg_lam, None, ALU.mult, after=[m5, m_lam])
            for t, (a, b) in enumerate(((0, P), (P, 384))):
                m7 = V.op(vec.tensor_scalar, pb[:, 0, a:b], pb[:, 0, a:b], st[:, 12 + t:13 + t], None, ALU.mult,
                          after=[m5])
                m8 = V.op(vec.scalar_tensor_tensor, pb[:, 0, a:b], pb[:, 1, a:b], st[:, 14 + t:15 + t], pb[:, 0, a:b],
                          ALU.mult, ALU.add, after=[m6, m7])
            stb.give(st, m8)
            yield
            pt, freed_pt = ptb1.take()
            bank, freed = banks.take()
            for out, src in ((0, 0), (P, P), (2 * P, 2 * P)):
                m9 = PE.op(ten.transpose, bank[:, out:out + P], pb[:, 0, src:src + P], ident, after=[m8, freed])
            m10 = A.op(act.activation, pt[:, :], bank[:, 0:384], ACT.Copy, after=[m9, freed_pt])
            banks.give(bank, m10)
            scb.give(pb, m9)
            yield
            ob, freed = banks.take()
            PE.quiet(ten.matmul, ob[:, 0:S], vt[:, 0, h * P:(h + 1) * P], pt[:, 0:S], start=True, stop=False,
                     after=[m10, freed, m_v[h // 2, 0], m_v[h // 2, 1]])
            m11 = PE.op(ten.matmul, ob[:, P:S], vt[:, 1, h * P:(h + 1) * P], pt[:, S:384], start=False, stop=True)
            ptb1.give(pt, m11)
            t, freed_t = tmp256.take()
            m12 = A.op(act.activation, t[:, :], ob[:, 0:S], ACT.Square, after=[m11, freed_t])
            yield
            r, freed_r = tmp256.take()
            m13 = norm_stat(lambda k: t[:, :], 1, S, "ones128", EPS, m12, r[:, :], freed_r)
            tmp256.give(t, m13)
            m14 = V.op(vec.scalar_tensor_tensor, r[:, :], ob[:, 0:S], subln, r[:, :], ALU.mult, ALU.mult,
                       after=[m13, m_sub])
            banks.give(ob, m14)
            m15 = V.op(vec.tensor_tensor, ymix[:, h, :], r[:, :], gate[:, h, :], ALU.mult, after=[m14, m_gate])
            tmp256.give(r, m15)
            m_y.append(m15)
            yield

        hk1 = lambda k: hk[:, k, :]
        project("b_w_in", list(range(0, 6)), h1, S, m_h, q_evac)
        project("w_kv", list(range(0, 6)), hk1, S, m_hk, k_evac)
        project_tokens("w_kv", list(range(6, 12)), lambda k, t: hk[:, k, t * P:(t + 1) * P], m_hk, v_evac, 2)
        project("b_w_in", list(range(6, 12)), h1, S, m_h, gate_evac)
        project("b_w_in", [12, 13], h1, S, m_h, qm_evac1)
        project("b_w_in", [14, 15], h1, S, m_h, gm_evac)
        skewed(diff_head(h) for h in range(BT))
        m_y += memory_attention(1, qm, gm, m_qm, m_kv[1], m_gmem, bufs)
        m_res = mix_out(1, m_y, ybuf, sq)
        new_phase()
        ph.close()
        first.close()

        m_old = everyone()
        second = ExitStack()
        tb = sb("tb", [P, W_B], second)
        m_meta = A.dma(res[:, :, 0:N_META], metaT, s_in2[2], 16)
        m_tb = A.dma(tb[:, :], tab_b, s_in2[1], 16, after=m_old)
        sq2 = sb("sq2", [P, KT, T], second)
        tmp = Ring([sb(f"tmp2{i}", [P, T], second) for i in range(6)])
        x2 = lambda k: res[:, k, :]
        h2 = lambda k: hn[:, k, :]

        def tabb(name):
            o, n = OFF_B[name]
            return tb[:, o:o + n]

        def ffn(n, m_in):
            ph = ExitStack()
            hidden = sb(f"hidden{n}", [P, FT, T], ph)
            m_h = rmsnorm(x2, h2, sq2, rstd[:, :], f"ffn{n}", m_in, T, None)
            m_hid = []
            gates = {}

            def gate_evac(panel, ps, mark):
                t, freed = tmp.take()
                m1 = A.op(act.activation, t[:, :], ps, ACT.Sigmoid, after=[mark, freed])
                m3 = V.op(vec.tensor_tensor, hidden[:, panel, :], t[:, :], ps, ALU.mult, after=[m1])
                tmp.give(t, m3)
                gates[panel] = m3
                return (m3,)

            def up_evac(panel, ps, mark):
                m = V.op(vec.tensor_tensor, hidden[:, panel, :], hidden[:, panel, :], ps, ALU.mult,
                         after=[mark, gates[panel]])
                m_hid.append(m)
                return (m,)

            for g in groups(list(range(FT)), 2):
                project(f"ffn{n}_gate", g, h2, T, m_h, gate_evac)
                project(f"ffn{n}_up", g, h2, T, m_h, up_evac)
            out = []

            def down_evac(panel, ps, mark):
                m = V.op(vec.scalar_tensor_tensor, x2(panel), ps, 0.5, x2(panel), ALU.mult, ALU.add, after=[mark])
                out.append(m)
                return (m,)

            project(f"ffn{n}_down", list(range(KT)), lambda k: hidden[:, k, :], T, m_hid, down_evac, kt=FT)
            new_phase()
            ph.close()
            return out

        m_res = ffn(1, [[m_meta, m] for m in m_res])

        ph = ExitStack()
        m_h = rmsnorm(x2, h2, sq2, rstd[:, :], "mix", m_res, T, None)
        iq = sb("iq", [P, 4, T], ph)
        ikm = sb("ikm", [P, 2, T], ph)
        iw = sb("iw", [P, 3, IDX_HEADS], ph)
        iww = sb("iww", [P, KT * IDX_HEADS], ph)
        score = sb("score", [P, QW], ph)
        mask = sb("mask", [P, QW], ph)
        top8 = sb("top8", [P, 8], ph)
        rq = sb("rq", [P, 8, T], ph)
        rk = sb("rk", [P, 8, T], ph)
        rv = sb("rv", [P, 3, RET_HEADS * RET_DV], ph)
        rel = Ring([sb(f"rel{i}", [P, QW], ph) for i in range(2)])
        s_iw = sem("s_iw")
        m_iww = SP.dma(iww[:, :], w["iw"], s_iw, 16, after=[V.last(), PE.last(), A.last()])

        def rope_halves(dst, cos, sin):
            def evac(ps, mark, m_free=None):
                a, freed_a = tmp.take()
                b, freed_b = tmp.take()
                m1 = V.op(vec.tensor_tensor, a[:, :], ps, cos, ALU.mult, after=[mark, freed_a, m_tb])
                m2 = V.op(vec.tensor_tensor, b[0:64, :], ps[64:128, :], sin[0:64, :], ALU.mult, after=[freed_b])
                m2 = V.op(vec.tensor_tensor, b[64:128, :], ps[0:64, :], sin[64:128, :], ALU.mult)
                m3 = G.op(pool.tensor_tensor, dst, a[:, :], b[:, :], ALU.add, after=[m1, m2, m_free])
                tmp.give(a, m3)
                tmp.give(b, m3)
                return m2, m3
            return evac

        m_iq, m_ik = {}, None

        def iq_evac(panel, ps, mark):
            nonlocal m_ik
            if panel < 4:
                m2, m_iq[panel] = rope_halves(iq[:, panel, :], tabb("icos"), tabb("isin"))(ps, mark)
            else:
                m2, m3 = rope_halves(ikm[:, 0, :], tabb("icos"), tabb("isin"))(ps, mark)
                m4 = V.op(vec.tensor_copy, ikm[:, 1, :], ikm[:, 0, :], after=[m3])
                for v, r in ((0, 32), (0, 96), (1, 0), (1, 64)):
                    m_ik = V.op(vec.memset, ikm[r:r + 32, v, :], 0.0, after=[m4])
            return (m2,)

        project("idx", list(range(5)), h2, T, m_h, iq_evac)
        bank, freed = banks.take()
        for j, (q0, n, _) in enumerate(QT):
            for k in range(KT):
                fn = PE.op if k == KT - 1 else PE.quiet
                m = fn(ten.matmul, bank[0:n, j * 8:j * 8 + 8], hn[:, k, q0:q0 + n], iww[:, k * 8:k * 8 + 8],
                       start=(k == 0), stop=(k == KT - 1), after=[m_iww, m_h, freed])
        m_iw = V.op(vec.tensor_scalar, iw[:, 0:2, :], bank[:, 0:16].rearrange("p (a b) -> p a b", a=2),
                    (IDX_DH ** -0.5) * (IDX_HEADS ** -0.5), None, ALU.mult, after=[m])
        m_iw = V.op(vec.tensor_scalar, iw[0:16, 2, :], bank[0:16, 16:24], (IDX_DH ** -0.5) * (IDX_HEADS ** -0.5),
                    None, ALU.mult)
        banks.give(bank, m_iw)

        m_score = m_tb
        for h in range(IDX_HEADS):
            ba, freed_a = banks.take()
            bb, freed_b = banks.take()
            r, freed_r = rel.take()
            for j, (q0, n, wd) in enumerate(QT):
                out = ba[:, QO[j]:QO[j] + wd] if j < 2 else bb[0:n, 0:wd]
                m = PE.op(ten.matmul, out, iq[:, h // 2, q0:q0 + n], ikm[:, h % 2, 0:wd], start=True, stop=True,
                          after=[m_iq[h // 2], m_ik, freed_a, freed_b])
            m1 = A.op(act.activation, r[:, 0:384], ba[:, 0:384], ACT.Relu, after=[m, freed_r])
            m2 = A.op(act.activation, r[0:16, 384:QW], bb[0:16, 0:T], ACT.Relu)
            banks.give(ba, m1)
            banks.give(bb, m2)
            prev = m_score
            for j, (q0, n, wd) in enumerate(QT):
                c = slice(QO[j], QO[j] + wd)
                src = (tabb("adm") if h == 0 else score)[0:n, c]
                m_score = V.op(vec.scalar_tensor_tensor, score[0:n, c], r[0:n, c], iw[0:n, j, h:h + 1], src,
                               ALU.mult, ALU.add, after=[m2, m_iw, prev])
            rel.give(r, m_score)

        m_mask = {}

        def top_k(j):
            q0, n, wd = QT[j]
            c = slice(QO[j], QO[j] + wd)
            s = score[0:n, c]
            m = m_score
            for _ in range(TOPK // 8):
                m1 = V.op(vec.max, top8[0:n, :], s, after=[m])
                m = V.op(vec.match_replace, s, top8[0:n, :], s, TAKEN, after=[m1])
            m1 = V.op(vec.tensor_scalar, mask[0:n, c], s, 0.7 * TAKEN, -BIG, ALU.is_gt, ALU.mult, after=[m])
            m2 = V.op(vec.tensor_tensor, mask[0:n, c], mask[0:n, c], tabb("adm")[0:n, c], ALU.add, after=[m1])
            m_mask[j] = V.op(vec.tensor_copy, mask[0:n, QO[j]:QO[j] + N_META],
                             tabb("meta")[0:n, N_META * j:N_META * (j + 1)], after=[m2])

        m_rq = {}
        held = {}

        def ret_rope(dst, kind):
            def evac(panel, ps, mark):
                h, half = (panel % 8) // 2, panel % 2
                if half == 0:
                    held["x1"] = (ps, mark)
                    m = []
                    held["give"] = m
                    return m
                x1_, mk1 = held["x1"]
                t = []
                for src, tabn, mk in ((x1_, "rcos", mk1), (ps, "rsin", mark), (ps, "rcos", mark), (x1_, "rsin", mk1)):
                    b, freed = tmp.take()
                    t.append((b, V.op(vec.tensor_tensor, b[:, :], src, tabb(tabn), ALU.mult, after=[mk, freed, m_tb])))
                ma = G.op(pool.tensor_tensor, dst[:, 2 * h, :], t[0][0][:, :], t[1][0][:, :], ALU.subtract,
                          after=[t[1][1]])
                mb = G.op(pool.tensor_tensor, dst[:, 2 * h + 1, :], t[2][0][:, :], t[3][0][:, :], ALU.add,
                          after=[t[3][1]])
                for n, (b, _) in enumerate(t):
                    tmp.give(b, ma if n < 2 else mb)
                m_rq[kind, h] = mb
                held["give"].append(t[3][1])
                return (t[3][1],)
            return evac

        def project_pair(name, p0, evac):
            bank_a = banks.take()
            bank_b = banks.take()
            slot, m_w = load(w[name][p0:p0 + 2].rearrange("c p n -> p c n"), 2 * D)
            for c, (bank, freed) in enumerate((bank_a, bank_b)):
                for k in range(KT):
                    fn = PE.op if k == KT - 1 else PE.quiet
                    at = (c * KT + k) * P
                    m = fn(ten.matmul, bank[:, 0:T], slot[0][:, at:at + P], h2(k), start=(k == 0), stop=(k == KT - 1),
                           after=[m_w, m_h, freed])
                got = evac(p0 + c, bank[:, 0:T], m)
            slots.give(slot, m)
            banks.give(bank_a[0], *got)
            banks.give(bank_b[0], *got)

        for h in range(RET_HEADS):
            project_pair("ret", 2 * h, ret_rope(rq, "q"))
        top_k(0)
        for h in range(RET_HEADS):
            project_pair("ret", 8 + 2 * h, ret_rope(rk, "k"))
        top_k(1)

        def to_tokens(dst, m_dst):
            def evac(panel, ps, mark):
                t, freed_t = tmp.take()
                m1 = A.op(act.activation, t[:, :], ps, ACT.Copy, after=[mark, freed_t])
                pending.append((panel, t, m1))
                while len(pending) > 1:
                    turn(dst, m_dst)
                return (m1,)
            return evac

        pending = []

        def turn(dst, m_dst):
            panel, t, m1 = pending.pop(0)
            bank, freed = banks.take()
            for j, (q0, n, _) in enumerate(QT):
                m2 = PE.op(ten.transpose, bank[0:n, j * P:(j + 1) * P], t[:, q0:q0 + n], ident, after=[m1, freed])
            tmp.give(t, m2)
            c = slice(panel * P, (panel + 1) * P)
            V.op(vec.tensor_copy, dst[:, 0:2, c], bank[:, 0:2 * P].rearrange("p (a b) -> p a b", a=2), after=[m2])
            m3 = V.op(vec.tensor_copy, dst[0:16, 2, c], bank[0:16, 2 * P:3 * P])
            banks.give(bank, m3)
            m_dst[panel] = m3

        m_rv = {}
        project("rv", list(range(16)), h2, T, m_h, to_tokens(rv, m_rv))
        turn(rv, m_rv)
        top_k(2)

        yr = sb("yr", [P, 16, T], ph)
        pr = Ring([sb(f"pr{i}", [P, KW], ph) for i in range(2)])
        m_yr = {}

        def ret_head(h):
            pb, freed_p = pr.take()
            bank, freed = banks.take()
            for j, (k0, n, _) in enumerate(QT):
                q0, nq = KQ[j]
                for d in range(2):
                    fn = PE.op if d else PE.quiet
                    m = fn(ten.matmul, bank[0:n, KO[j]:KO[j] + nq], rk[:, 2 * h + d, k0:k0 + n],
                           rq[:, 2 * h + d, q0:T], start=(d == 0), stop=(d == 1),
                           after=[m_rq["q", h], m_rq["k", h], freed])
            dec = tabb("decay")[:, h * KW:(h + 1) * KW]
            V.op(vec.tensor_tensor, pb[:, 0:416], bank[:, 0:416], dec[:, 0:416], ALU.mult, after=[m, freed_p])
            m1 = V.op(vec.tensor_tensor, pb[0:16, 416:KW], bank[0:16, 416:KW], dec[0:16, 416:KW], ALU.mult)
            banks.give(bank, m1)
            yield
            m_sq, outs = [], []
            for e in range(4):
                ob, freed = banks.take()
                c = slice(h * RET_DV + e * P, h * RET_DV + (e + 1) * P)
                for j, (k0, n, _) in enumerate(QT):
                    q0, nq = KQ[j]
                    fn = PE.op if j == 2 else PE.quiet
                    m2 = fn(ten.matmul, ob[:, q0:T], rv[0:n, j, c], pb[0:n, KO[j]:KO[j] + nq], start=(j == 0),
                            stop=(j == 2), after=[m1, m_rv[4 * h + e], freed])
                t, freed_t = tmp.take()
                m_sq.append(A.op(act.activation, t[:, :], ob[:, 0:T], ACT.Square, after=[m2, freed_t]))
                m_c = V.op(vec.tensor_copy, yr[:, 4 * h + e, :], ob[:, 0:T], after=[m_sq[-1]])
                banks.give(ob, m_sq[-1], m_c)
                outs.append((t, m_c))
            pr.give(pb, m2)
            yield
            r, freed_r = tmp.take()
            m3 = norm_stat(lambda k: outs[k][0][:, :], 4, T, "ones512", EPS, m_sq, r[:, :], freed_r)
            for e in range(4):
                tmp.give(outs[e][0], m3)
                m_yr[4 * h + e] = V.op(vec.tensor_tensor, yr[:, 4 * h + e, :], yr[:, 4 * h + e, :], r[:, :],
                                       ALU.mult, after=[m3, outs[e][1]])
            tmp.give(r, m_yr[4 * h + 3])
            yield

        for h in range(RET_HEADS):
            for _ in ret_head(h):
                pass
        m_ret = PE.last()

        m_yg = {}

        def rg_evac(panel, ps, mark):
            t, freed = tmp.take()
            m1 = A.op(act.activation, t[:, :], ps, ACT.Sigmoid, after=[mark, freed])
            m3 = V.op(vec.tensor_tensor, t[:, :], t[:, :], ps, ALU.mult, after=[m1])
            m_yg[panel] = V.op(vec.tensor_tensor, yr[:, panel, :], yr[:, panel, :], t[:, :], ALU.mult,
                               after=[m3, m_yr[panel]])
            tmp.give(t, m_yg[panel])
            return (m3,)

        project("rg", list(range(16)), h2, T, m_h, rg_evac)

        G.wait(m_ret)
        V.wait(m_ret)
        A.wait(m_ret)
        aq, ak = rq, rk
        m_aqk = {}

        def aqk_evac(panel, ps, mark):
            dst = (aq if panel < 8 else ak)[:, panel % 8, :]
            m2, m_aqk[panel] = rope_halves(dst, tabb("acos"), tabb("asin"))(ps, mark)
            return (m2,)

        project("aqk", list(range(16)), h2, T, m_h, aqk_evac)
        rv_flat = rv[:, :, :].rearrange("p a b -> p (a b)")
        avt = rv_flat[:, 0:3 * ATT_HEADS * P].rearrange("p (t n) -> p t n", t=3)
        m_av = {}
        project("av", list(range(8)), h2, T, m_h, to_tokens(avt, m_av))
        turn(avt, m_av)

        merged = sb("merged", [P, KT, T], ph)
        gatt = sb("gatt", [P, KT, T], ph)
        m_gr, m_ga, m_mg = {}, {}, {}

        def gate2_evac(panel, ps, mark):
            dst = (merged if panel < 8 else gatt)[:, panel % 8, :]
            m1 = A.op(act.activation, dst, ps, ACT.Sigmoid, after=[mark])
            (m_gr if panel < 8 else m_ga)[panel % 8] = m1
            return (m1,)

        def ret_out_evac(panel, ps, mark):
            m_mg[panel] = V.op(vec.tensor_tensor, merged[:, panel, :], merged[:, panel, :], ps, ALU.mult,
                               after=[mark, m_gr[panel]])
            return (m_mg[panel],)

        project("g2", list(range(16)), h2, T, m_h, gate2_evac)

        pbs = Ring([sb(f"pbs{i}", [P, QW], ph) for i in range(2)])
        pts = Ring([sb(f"pts{i}", [P, KW], ph) for i in range(2)])
        sts = Ring([sb(f"sts{i}", [P, 12], ph) for i in range(4)])
        ya = rv_flat[:, 3 * ATT_HEADS * P:3 * ATT_HEADS * P + ATT_HEADS * T].rearrange("p (h t) -> p h t", h=ATT_HEADS)
        m_ya = {}
        scale = 128 ** -0.5

        def att_head(h):
            pb, freed_p = pbs.take()
            st, freed_st = sts.take()
            ba, freed_a = banks.take()
            bb, freed_b = banks.take()
            for j, (q0, n, wd) in enumerate(QT):
                out = ba[:, QO[j]:QO[j] + wd] if j < 2 else bb[0:n, 0:wd]
                m = PE.op(ten.matmul, out, aq[:, h, q0:q0 + n], ak[:, h, 0:wd], start=True, stop=True,
                          after=[m_aqk[h], m_aqk[8 + h], freed_a, freed_b])
            m1 = V.op(vec.scalar_tensor_tensor, pb[:, 0:384], ba[:, 0:384], scale, mask[:, 0:384], ALU.mult, ALU.add,
                      after=[m, m_mask[0], m_mask[1], m_mask[2], freed_p, freed_st])
            m1 = V.op(vec.scalar_tensor_tensor, pb[0:16, 384:QW], bb[0:16, 0:T], scale, mask[0:16, 384:QW], ALU.mult,
                      ALU.add)
            banks.give(ba, m1)
            banks.give(bb, m1)
            for j, (q0, n, wd) in enumerate(QT):
                m2 = V.op(vec.tensor_reduce, st[0:n, j:j + 1], pb[0:n, QO[j]:QO[j] + wd], AX_X, ALU.max, after=[m1])
            m3 = V.op(vec.tensor_scalar, st[:, 3:5], st[:, 0:2], -1.0, None, ALU.mult, after=[m2])
            m3 = V.op(vec.tensor_scalar, st[0:16, 5:6], st[0:16, 2:3], -1.0, None, ALU.mult)
            for j, (q0, n, wd) in enumerate(QT):
                c = slice(QO[j], QO[j] + wd)
                m4 = A.op(act.activation, pb[0:n, c], pb[0:n, c], ACT.Exp, bias=st[0:n, 3 + j:4 + j],
                          accum_out=st[0:n, 6 + j:7 + j], after=[m3])
            m5 = V.op(vec.reciprocal, st[:, 9:11], st[:, 6:8], after=[m4])
            m5 = V.op(vec.reciprocal, st[0:16, 11:12], st[0:16, 8:9])
            for j, (q0, n, wd) in enumerate(QT):
                c = slice(QO[j], QO[j] + wd)
                m6 = V.op(vec.tensor_scalar, pb[0:n, c], pb[0:n, c], st[0:n, 9 + j:10 + j], None, ALU.mult,
                          after=[m5])
            sts.give(st, m6)
            yield
            pt, freed_pt = pts.take()
            bank, freed = banks.take()
            for k in range(3):
                nk = QT[k][1]
                for j in range(k, 3):
                    q0, n, _ = QT[j]
                    at = KO[k] + q0 - KQ[k][0]
                    m7 = PE.op(ten.transpose, bank[0:nk, at:at + n], pb[0:n, QO[j] + P * k:QO[j] + P * k + nk],
                               ident[0:n, 0:n], after=[m6, freed])
            A.op(act.activation, pt[:, 0:416], bank[:, 0:416], ACT.Copy, after=[m7, freed_pt])
            m8 = A.op(act.activation, pt[0:16, 416:KW], bank[0:16, 416:KW], ACT.Copy)
            banks.give(bank, m8)
            pbs.give(pb, m7)
            yield
            ob, freed = banks.take()
            for k in range(3):
                nk = QT[k][1]
                q0, nq = KQ[k]
                fn = PE.op if k == 2 else PE.quiet
                m9 = fn(ten.matmul, ob[:, q0:T], avt[0:nk, k, h * P:(h + 1) * P], pt[0:nk, KO[k]:KO[k] + nq],
                        start=(k == 0), stop=(k == 2), after=[m8, m_av[h], freed])
            pts.give(pt, m9)
            m_ya[h] = A.op(act.activation, ya[:, h, :], ob[:, 0:T], ACT.Copy, after=[m9])
            banks.give(ob, m_ya[h])
            yield

        m_yg_all = [m_yg[k] for k in range(16)]
        heads = [att_head(h) for h in range(ATT_HEADS)]
        live = []
        for step in range(ATT_HEADS + 3):
            if step < ATT_HEADS:
                live.append(heads[step])
            for g in list(live):
                try:
                    next(g)
                except StopIteration:
                    live.remove(g)
            if step < KT:
                project("ret_out", [step], lambda k: yr[:, k, :], T, m_yg_all, ret_out_evac, kt=16)

        def att_out_evac(panel, ps, mark):
            m1 = V.op(vec.tensor_tensor, gatt[:, panel, :], gatt[:, panel, :], ps, ALU.mult,
                      after=[mark, m_ga[panel]])
            m_mg[panel] = V.op(vec.tensor_tensor, merged[:, panel, :], merged[:, panel, :], gatt[:, panel, :],
                               ALU.add, after=[m1, m_mg[panel]])
            return (m1,)

        project("att_out", list(range(KT)), lambda k: ya[:, k, :], T, [m_ya[h] for h in range(ATT_HEADS)],
                att_out_evac)
        m_res = [None] * KT

        def mix_evac(panel, ps, mark):
            m_res[panel] = V.op(vec.tensor_tensor, x2(panel), x2(panel), ps, ALU.add, after=[mark])
            return (m_res[panel],)

        project("mix_out", list(range(KT)), lambda k: merged[:, k, :], T, [m_mg[k] for k in range(KT)], mix_evac)
        new_phase()
        ph.close()

        ffn(2, m_res)
        m_out = rmsnorm(x2, h2, sq2, rstd[:, :], "final", [V.last()] * KT, T, None)
        s_out = sem("s_out")
        for k in range(KT):
            SP.dma(outT[:, k, :], hn[:, k, N_META:T], s_out, 16 * (k + 1), after=[m_out[k]])
        SP.wait((s_out, 16 * KT))
        second.close()

        block = ctx.enter_context(nc.Block())

        @block.sync
        def _(e):
            SP.emit()

        @block.gpsimd
        def _(e):
            G.emit()

        @block.scalar
        def _(e):
            A.emit()

        @block.vector
        def _(e):
            V.emit()

        @block.tensor
        def _(e):
            PE.emit()


def kernel(**inputs):
    import concourse.bacc as _bacc
    from concourse import mybir as _mybir
    from concourse.bass_utils import run_bass_kernel_spmd as _run

    I = {k: np.asarray(v) for k, v in inputs.items()}
    nc = _bacc.Bacc("TRN2", target_bir_lowering=False, num_devices=1)
    arrays = {}

    def dram(name, a):
        a = np.ascontiguousarray(a)
        arrays[name] = a
        return nc.dram_tensor(name, a.shape, _mybir.dt.from_np(a.dtype), kind="ExternalInput").ap()

    def feature_major(a):
        return a.T.reshape(-1, P, a.shape[0]).transpose(1, 0, 2)

    def panels(wt):
        k, n = wt.shape
        return wt.reshape(k // P, P, n // P, P).transpose(2, 1, 0, 3).reshape(n // P, P, k)

    vec = {"pre0": I["pre_norm"][0], "pre1": I["pre_norm"][1], "post0": I["post_norm"][0], "post1": I["post_norm"][1],
           "memn0": I["mem_norm"][0], "memn1": I["mem_norm"][1], "kvn": I["kv_norm"], "mu": I["a_shift_mu"][0],
           "w0": I["a_w0"][0], "a0": I["a_a0"][0], "kk": I["a_k_k"][0], "ka": I["a_k_a"][0],
           "rk": I["a_r_k"][0].reshape(-1), "lnw": I["a_lnx_w"][0], "lnb": I["a_lnx_b"][0], "subln": I["b_subln"][0],
           "ffn1": I["ffn1_norm_2"][0], "mix": I["mix_norm_2"][0], "ffn2": I["ffn2_norm_2"][0],
           "final": I["final_norm_2"]}
    cols = np.zeros((P, NCOL), np.float32)
    for name, n in VECTORS:
        if name == "lam":
            for j, key in enumerate(("b_lam_q1", "b_lam_q2", "b_lam_k1", "b_lam_k2")):
                cols[:HD, COL[name] + j] = I[key][0]
        else:
            cols[:, COL[name]:COL[name] + n] = vec[name].reshape(n, P).T
    ta, tr, tb = const_tables()

    win = I["w_in_2"][0]
    o = np.cumsum([0, 1024, 1024, 2048, 2048, 1024, 1024, 1024, 512, 64, 8, 1024, 1024])
    idx = []
    for j in range(4):
        for half in range(2):
            for h in (2 * j, 2 * j + 1):
                idx += list(range(o[7] + 64 * h + 32 * half, o[7] + 64 * h + 32 * half + 32))
    for half in (0, 0, 1, 1):
        idx += list(range(o[8] + 32 * half, o[8] + 32 * half + 32))
    w = {
        "a_w_in": panels(I["a_w_in"][0]), "w_mem0": panels(I["w_mem_kv"][0]), "w_mem1": panels(I["w_mem_kv"][1]),
        "w_out0": panels(I["w_out"][0]), "w_out1": panels(I["w_out"][1]), "w_kv": panels(I["w_kv"]),
        "b_w_in": panels(I["b_w_in"][0]),
        "ffn1_gate": panels(I["ffn1_w_gate_2"][0]), "ffn1_up": panels(I["ffn1_w_up_2"][0]),
        "ffn1_down": panels(I["ffn1_w_down_2"][0]), "ffn2_gate": panels(I["ffn2_w_gate_2"][0]),
        "ffn2_up": panels(I["ffn2_w_up_2"][0]), "ffn2_down": panels(I["ffn2_w_down_2"][0]),
        "idx": panels(win[:, idx]), "ret": panels(win[:, o[0]:o[2]]), "rv": panels(win[:, o[2]:o[3]]),
        "rg": panels(win[:, o[3]:o[4]]), "aqk": panels(win[:, o[4]:o[6]]), "av": panels(win[:, o[6]:o[7]]),
        "g2": panels(win[:, o[10]:o[12]]),
        "iw": win[:, o[9]:o[10]].reshape(KT, P, IDX_HEADS).transpose(1, 0, 2).reshape(P, -1),
        "ret_out": panels(I["w_ret_out_2"][0]), "att_out": panels(I["w_att_out_2"][0]),
        "mix_out": panels(I["w_mix_out_2"][0]),
    }
    args = [dram("xT", feature_major(I["x"][0])), dram("memT", feature_major(I["mem"][0])),
            dram("metaT", feature_major(I["meta_tokens_2"])), dram("vecs", cols), dram("tab_a", ta),
            dram("tab_r", tr), dram("tab_b", tb),
            dram("lora", np.concatenate([I["a_w2"][0], I["a_a2"][0]], 0)),
            {k: dram("w_" + k, v) for k, v in w.items()}]
    out = nc.dram_tensor("outT", (P, KT, S), _mybir.dt.float32, kind="ExternalOutput").ap()
    build(nc, *args, out)
    r = _run(nc, [arrays], core_ids=[0])
    got = r.results[0]["outT"]
    return got.transpose(2, 1, 0).reshape(1, S, D)
```

```python
import math
from contextlib import ExitStack

import numpy as np
import concourse.bass as bass
from concourse import mybir

P = 128
D = 1024
KT = D // P
S = 256
N_META = 16
T = S + N_META
MEM = 256
BR = 768
BT = BR // P
HD = 64
MW = 256
MT = MW // P
MEM_HEADS = 4
Z_TILES = (3 * BR + 128) // P
LAM_INIT = 0.8 - 0.6 * math.exp(-0.3)
RET_HEADS, RET_DV = 4, 512
ATT_HEADS = 8
IDX_HEADS, IDX_DH = 8, 64
TOPK = min(256, S // 4)
FF = 2816
FT = FF // P
EPS = 1e-6
LNX_EPS = 64e-5
CH = 128
DECAY_C = math.exp(-0.5)
MID = DECAY_C * CH / 2
BIG = 1e30
TAKEN = -3e38
QT = [(0, 128, 128), (128, 128, 256), (256, 16, 272)]
QO = [0, 128, 384]
QW = 656
KO = [0, 272, 416]
KQ = [(0, 272), (128, 144), (256, 16)]
KW = 432

F32 = mybir.dt.float32
F32R = mybir.dt.float32r
ALU = mybir.AluOpType
ACT = mybir.ActivationFunctionType
AX_X = mybir.AxisListType.X

N_RAW, N_SPLIT = 4, 3
WC = 8 * P


def weight_order():
    order = [(f"w_mem{n}", p, KT) for n in range(2) for p in range(4)]
    order += [("a_w_in", p, KT) for p in [18] + list(range(6, 12)) + list(range(6)) + list(range(12, 18))
              + list(range(19, 29))]
    order += [("w_out0", p, KT) for p in range(KT)]
    order += [("b_w_in", p, KT) for p in range(6)] + [("w_kv", p, KT) for p in range(12)]
    order += [("b_w_in", p, KT) for p in range(6, 16)] + [("w_out1", p, KT) for p in range(KT)]
    ffn = lambda n: [(f"ffn{n}_{g}", p, KT) for p in range(FT) for g in ("gate", "up")] \
        + [(f"ffn{n}_down", p, FT) for p in range(KT)]
    order += ffn(1)
    order += [("idx", p, KT) for p in range(6)] + [("ret", p, KT) for p in range(16)]
    order += [("rv", p, KT) for p in range(16)] + [("rg", p, KT) for p in range(16)]
    order += [("aqk", p, KT) for p in range(16)] + [("av", p, KT) for p in range(8)]
    order += [("g2", p, KT) for p in range(16)] + [("ret_out", p, 16) for p in range(KT)]
    order += [("att_out", p, KT) for p in range(KT)] + [("mix_out", p, KT) for p in range(KT)]
    return order + ffn(2)


def chunks_of(kt):
    n = -(-kt // 8)
    cuts = [-(-kt * i // n) for i in range(n + 1)]
    return [(a, b - a) for a, b in zip(cuts, cuts[1:])]


VECTORS = [("pre0", 8), ("pre1", 8), ("post0", 8), ("post1", 8), ("memn0", 8), ("memn1", 8), ("kvn", 8),
           ("mu", Z_TILES), ("w0", BT), ("a0", BT), ("kk", BT), ("ka", BT), ("rk", BT), ("lnw", BT), ("lnb", BT),
           ("subln", 1), ("lam", 4), ("ffn1", 8), ("mix", 8), ("ffn2", 8), ("final", 8)]
COL, NCOL = {}, 0
for _name, _n in VECTORS:
    COL[_name] = NCOL
    NCOL += _n

TABLES_A = [("ident", P), ("ones_d", P), ("blk", P), ("blkm", P), ("ones", P), ("ones128", P), ("ones512", P),
            ("dist", 384), ("mid", 2)]
TABLES_R = [("neg_up", P), ("neg_m0", P), ("m0t", P)] + [(f"m{j}", P) for j in range(1, 7)] + [("up", P), ("upinc", P)]
TABLES_B = [("rcos", T), ("rsin", T), ("acos", T), ("asin", T), ("icos", T), ("isin", T), ("decay", RET_HEADS * KW),
            ("adm", QW), ("meta", 3 * N_META)]


def offsets(tables):
    at, out = 0, {}
    for name, n in tables:
        out[name] = (at, n)
        at += n
    return out, at


OFF_A, W_A = offsets(TABLES_A)
OFF_R, W_R = offsets(TABLES_R)
OFF_B, W_B = offsets(TABLES_B)


def alibi_slopes(n):
    c = 2 ** int(math.floor(math.log2(n)))

    def pow2(m):
        start = 2.0 ** (-8.0 / m)
        return [start ** (i + 1) for i in range(m)]
    s = pow2(n) if c == n else pow2(c) + pow2(2 * c)[0::2][: n - c]
    return [float(np.float32(x)) for x in s]


def rope_tables(d):
    inv = (np.float32(10000.0) ** (-np.arange(0, d, 2, dtype=np.float32) / np.float32(d))).astype(np.float32)
    ang = (np.arange(T, dtype=np.float32)[None, :] * inv[:, None]).astype(np.float32)
    return np.cos(ang).astype(np.float32), np.sin(ang).astype(np.float32)


def const_tables():
    i = np.arange(P)
    r, c = i[:, None], i[None, :]
    a = {"ident": r == c, "ones_d": np.full((P, P), 1.0 / D), "blk": (r // HD == c // HD) * 1.0,
         "blkm": (r // HD == c // HD) / HD, "ones": np.ones((P, P)), "ones128": np.full((P, P), 1.0 / P),
         "ones512": np.full((P, P), 1.0 / RET_DV), "mid": np.array([[MID, -MID]] * P)}
    t = np.concatenate([r, 128 + r, 128 + r], 1)
    key = np.arange(384)[None, :]
    key = np.where(key < 128, key, key - 128)
    tok = np.where(np.arange(384)[None, :] < 128, t[:, :1], t[:, 1:2])
    a["dist"] = np.where(key // 64 <= tok // 64, np.abs(tok - key), BIG)
    m = {"neg_up": (c > r) * -1.0, "up": (c > r) * 1.0, "upinc": (c >= r) * 1.0}
    for j in range(7):
        n = 1 << j
        m[f"m{j}"] = ((r // (2 * n) == c // (2 * n)) & (r // n > c // n)) * 1.0
    m["neg_m0"], m["m0t"] = -m["m0"], m["m0"].T
    b = {}
    b["rcos"], b["rsin"] = rope_tables(256)
    co, si = rope_tables(128)
    b["acos"], b["asin"] = np.concatenate([co, co]), np.concatenate([-si, si])
    co, si = rope_tables(64)
    b["icos"], b["isin"] = np.concatenate([co] * 4), np.concatenate([-si, -si, si, si])
    dec = np.zeros((P, RET_HEADS, KW))
    for h in range(RET_HEADS):
        g = np.log1p(-(2.0 ** (-5.0 - h)))
        for j, (q0, n) in enumerate(KQ):
            diff = (q0 + np.arange(n))[None, :] - (P * j + i)[:, None]
            dec[:, h, KO[j]:KO[j] + n] = np.where(diff >= 0, np.exp(g * np.maximum(diff, 0)), 0.0) / 16.0
    b["decay"] = dec.reshape(P, -1)
    adm, meta = np.full((P, QW), -BIG), np.full((P, 3 * N_META), -BIG)
    for j, (q0, n, w) in enumerate(QT):
        q, k = q0 + i[:, None], np.arange(w)[None, :]
        adm[:, QO[j]:QO[j] + w] = np.where((k >= N_META) & (k <= q), 0.0, -BIG)
        k = np.arange(N_META)[None, :]
        meta[:, N_META * j:N_META * (j + 1)] = np.where(k <= q, 0.0, -BIG)
    b["adm"], b["meta"] = adm, meta
    pack = lambda tables, src: np.ascontiguousarray(
        np.concatenate([np.asarray(src[n], np.float32) for n, _ in tables], 1))
    return pack(TABLES_A, a), pack(TABLES_R, m), pack(TABLES_B, b)


class Queue:

    def __init__(self, engine, sem):
        self.engine, self.sem, self.count, self.items, self.met = engine, sem, 0, [], {}

    def wait(self, *marks):
        for mark in marks:
            if mark is None:
                continue
            if isinstance(mark, list):
                self.wait(*mark)
                continue
            sem, value = mark
            if self.met.get(sem, 0) < value:
                self.met[sem] = value
                self.items.append((self.engine.wait_ge, (sem, value), {}, None, 0))

    def op(self, fn, *args, after=(), **kw):
        self.wait(*after)
        self.count += 1
        self.items.append((fn, args, kw, self.sem, 1))
        return (self.sem, self.count)

    def quiet(self, fn, *args, after=(), **kw):
        self.wait(*after)
        self.items.append((fn, args, kw, None, 0))

    def dma(self, out, in_, sem, value, after=()):
        self.wait(*after)
        self.items.append((self.engine.dma_start, (out, in_), {}, sem, 16))
        return (sem, value)

    def last(self):
        return (self.sem, self.count) if self.count else None

    def emit(self):
        for fn, args, kw, sem, inc in self.items:
            ins = fn(*args, **kw)
            if sem is not None:
                ins.then_inc(sem, inc)


class Ring:

    def __init__(self, bufs):
        self.free = [(b, []) for b in bufs]

    def take(self):
        return self.free.pop(0)

    def give(self, buf, *marks):
        self.free.append((buf, list(marks)))


def skewed(streams):
    live, streams = [], list(streams)
    while live or streams:
        if streams:
            live.append(streams.pop(0))
        for g in list(live):
            try:
                next(g)
            except StopIteration:
                live.remove(g)


def build(nc, xT, memT, metaT, vecs, tab_a, tab_r, tab_b, lora, w, outT):
    with ExitStack() as ctx:
        def sem(name):
            return ctx.enter_context(nc.semaphore(name))

        def sb(name, shape, scope=ctx, dt=F32):
            return scope.enter_context(nc.sbuf_tensor(name, shape, dt))

        V = Queue(nc.vector, sem("s_vector"))
        A = Queue(nc.scalar, sem("s_scalar"))
        PE = Queue(nc.tensor, sem("s_tensor"))
        G = Queue(nc.gpsimd, sem("s_pool"))
        SP = Queue(nc.sync, sem("s_sync"))
        vec, act, ten, pool = nc.vector, nc.scalar, nc.tensor, nc.gpsimd

        banks = Ring([ctx.enter_context(nc.psum_tensor(f"bank{i}", [P, 512], F32)) for i in range(8)])

        res = sb("res", [P, KT, T])
        xh, xl = sb("xh", [P, KT, T], dt=F32R), sb("xl", [P, KT, T], dt=F32R)
        cols = sb("cols", [P, NCOL])
        ta = sb("ta", [P, W_A])
        rstd = sb("rstd", [P, T])
        sqr = sb("sqr", [P, KT, T])

        def tab(name):
            o, n = OFF_A[name]
            return ta[:, o:o + n]

        ident = tab("ident")

        def col(name, i=0):
            return cols[:, COL[name] + i:COL[name] + i + 1]

        s_in = [sem(f"s_in{i}") for i in range(5)]
        m_cols = A.dma(cols[:, :], vecs, s_in[2], 16)

        raws = [(sb(f"raw{i}", [P, WC]), sem(f"s_raw{i}")) for i in range(N_RAW)]
        splits = Ring([(sb(f"wh{i}", [P, WC], dt=F32R), sb(f"wl{i}", [P, WC], dt=F32R)) for i in range(N_SPLIT)])
        stream = [(name, p, k0, nk) for name, p, kt in weight_order() for k0, nk in chunks_of(kt)]
        loads, ready = [], []
        raw_freed = [[] for _ in range(N_RAW)]

        def load_next():
            n = len(loads)
            if n < len(stream):
                name, p, k0, nk = stream[n]
                buf, s = raws[n % N_RAW]
                loads.append(SP.dma(buf[:, 0:nk * P], w[name][p][:, k0 * P:(k0 + nk) * P], s,
                                    16 * (n // N_RAW + 1), after=raw_freed[n % N_RAW]))

        def split_next():
            n = len(ready)
            if n == len(stream):
                return
            nk = stream[n][3]
            raw = raws[n % N_RAW][0][:, 0:nk * P]
            (hi, lo), freed = splits.take()
            m_hi = A.op(act.activation, hi[:, 0:nk * P], raw, ACT.Copy, after=[loads[n], freed])
            m_lo = V.op(vec.tensor_tensor, lo[:, 0:nk * P], raw, hi[:, 0:nk * P].bitcast(F32), ALU.subtract,
                        after=[m_hi])
            ready.append(((hi, lo), m_hi, m_lo))
            raw_freed[n % N_RAW] = [m_hi, m_lo]
            load_next()

        used = [0]

        def next_weights(name, panel, k0):
            n = used[0]
            assert stream[n][0:3] == (name, panel, k0), (stream[n], name, panel, k0)
            used[0] += 1
            while len(ready) < min(n + N_SPLIT, len(stream)):
                split_next()
            return ready[n]

        for _ in range(N_RAW):
            load_next()

        def split_input(k, src, gain, m_src, hi, lo, m_free):
            m_hi = A.op(act.activation, hi, src, ACT.Copy, scale=gain, after=[m_src, m_cols, m_free])
            if isinstance(gain, float):
                return V.op(vec.tensor_tensor, lo, src, hi.bitcast(F32), ALU.subtract, after=[m_hi, m_free])
            return V.op(vec.scalar_tensor_tensor, lo, src, gain, hi.bitcast(F32), ALU.mult, ALU.subtract,
                        after=[m_hi, m_free])

        kept = []

        def project(name, panels, x_hi, x_lo, n_tok, x_marks, evac, kt=KT, hook=None):
            for panel in panels:
                bank, freed = banks.take()
                ps = bank[:, 0:n_tok]
                for k0, nk in chunks_of(kt):
                    (hi, lo), m_hi, m_lo = next_weights(name, panel, k0)
                    for k in range(nk):
                        kk, c = k0 + k, slice(k * P, (k + 1) * P)
                        m_x = x_marks[kk] if isinstance(x_marks, (list, dict)) and len(x_marks) == kt else x_marks
                        PE.quiet(ten.matmul, ps, hi[:, c], x_hi(kk), start=(kk == 0), stop=False,
                                 after=[m_hi, m_x, freed])
                        PE.quiet(ten.matmul, ps, hi[:, c], x_lo(kk), start=False, stop=False, after=[m_x])
                        fn = PE.op if k == nk - 1 else PE.quiet
                        mark = fn(ten.matmul, ps, lo[:, c], x_hi(kk), start=False, stop=(kk == kt - 1),
                                  after=[m_lo])
                    splits.give((hi, lo), mark)
                if hook is not None:
                    hook()
                    hook = None
                marks = evac(panel, ps, mark)
                if marks is None:
                    kept.append(bank)
                else:
                    banks.give(bank, *marks)

        def norm_stat(sq_tile, n, n_tok, table, eps, m_sq, out, freed_out=None):
            bank, freed = banks.take()
            for k in range(n):
                fn = PE.op if k == n - 1 else PE.quiet
                mark = fn(ten.matmul, bank[:, 0:n_tok], tab(table), sq_tile(k), start=(k == 0), stop=(k == n - 1),
                          after=[m_ta, m_sq[k] if isinstance(m_sq, list) else m_sq, freed])
            m = rsqrt(out, bank[:, 0:n_tok], eps, ALU.add, [mark, freed_out])
            banks.give(bank, m)
            return m

        def turn(src, tiles, dst, m_src, after_dst):
            bank, freed = banks.take()
            for j, (q0, n) in enumerate(tiles):
                m = PE.op(ten.transpose, bank[0:n, j * P:(j + 1) * P], src[:, q0:q0 + n], ident,
                          after=[m_src, freed])
            full = [t for t in tiles if t[1] == P]
            m1 = A.op(act.activation, dst(0, len(full), P),
                      bank[:, 0:len(full) * P].rearrange("p (a b) -> p a b", a=len(full)), ACT.Copy,
                      after=[m, after_dst])
            if len(full) < len(tiles):
                n = tiles[-1][1]
                m1 = A.op(act.activation, dst(len(full), 1, n), bank[0:n, len(full) * P:(len(full) + 1) * P],
                          ACT.Copy)
            banks.give(bank, m1)
            return m, m1

        def rsqrt(out, x, eps, op, marks):
            m = V.op(vec.tensor_scalar, out, x, eps, None, op, after=marks)
            m = A.op(act.activation, out, out, ACT.Ln, after=[m])
            return A.op(act.activation, out, out, ACT.Exp, scale=-0.5, after=[m])

        def square(k, dst, src, marks):
            if k % 2:
                return V.op(vec.tensor_tensor, dst, src, src, ALU.mult, after=marks)
            return A.op(act.activation, dst, src, ACT.Square, after=marks)

        m_next, m_nsq, stat = [None] * KT, [None] * KT, {}

        def residual_done(k, lo, gain, m_src, m_free):
            x = res[:, k, lo:T]
            if gain is not None:
                m_next[k] = split_input(k, x, col(gain, k), m_src, xh[:, k, 0:T - lo], xl[:, k, 0:T - lo], m_free)
            m_nsq[k] = square(k, sqr[:, k, 0:T - lo], x, [m_src])

        def residual_stat(n_tok):
            stat["x"] = norm_stat(lambda k: sqr[:, k, 0:n_tok], KT, n_tok, "ones_d", EPS, m_nsq, rstd[:, 0:n_tok])

        def everyone():
            return [q.last() for q in (V, A, PE, G, SP)]

        def new_phase():
            marks = everyone()
            for q in (V, A, PE, G):
                q.wait(*marks)
            return marks

        first = ExitStack()
        kmT = sb("kmT", [P, 2, MT, MEM], first)
        vm = sb("vm", [P, 2, MEM // P, MW], first)
        tmp256 = Ring([sb(f"tmp{i}", [P, S], first) for i in range(4)])
        small = sb("small", [P, 48], first)
        x1 = lambda k: res[:, k, N_META:T]
        h1h, h1l = lambda k: xh[:, k, 0:S], lambda k: xl[:, k, 0:S]

        def memory_attention(layer, qm, gm, m_q, m_kv, m_g, bufs):
            marks = {BT: [], BT + 1: []}

            def head(h):
                j, o = h // 2, HD * (h % 2)
                pbuf, freed_p = bufs["p"].take()
                ptb, freed_pt = bufs["pt"].take()
                st, freed_st = bufs["st"].take()
                bank, freed = banks.take()
                for t in range(2):
                    m_s = PE.op(ten.matmul, bank[:, t * MEM:(t + 1) * MEM], qm[o:o + HD, j, t * P:(t + 1) * P],
                                kmT[o:o + HD, layer, j, :], start=True, stop=True, after=[m_q, m_kv, freed])
                sc = bank[:, :].rearrange("p (t m) -> p t m", t=2)
                m1 = V.op(vec.tensor_reduce, st[:, 0:2], sc, AX_X, ALU.max, after=[m_s, freed_st])
                m2 = V.op(vec.tensor_scalar, st[:, 2:4], st[:, 0:2], -(HD ** -0.5), None, ALU.mult, after=[m1])
                for t in range(2):
                    m3 = A.op(act.activation, pbuf[:, t, :], sc[:, t, :], ACT.Exp, bias=st[:, 2 + t:3 + t],
                              scale=HD ** -0.5, accum_out=st[:, 4 + t:5 + t], after=[m2, freed_p])
                banks.give(bank, m3)
                m4 = V.op(vec.reciprocal, st[:, 6:8], st[:, 4:6], after=[m3])
                for t in range(2):
                    m5 = V.op(vec.tensor_scalar, pbuf[:, t, :], pbuf[:, t, :], st[:, 6 + t:7 + t], None, ALU.mult,
                              after=[m4])
                yield
                bank, freed = banks.take()
                pt = bank[:, :].rearrange("p (k q) -> p k q", k=2)
                for t in range(2):
                    for k in range(2):
                        m6 = PE.op(ten.transpose, pt[:, k, t * P:(t + 1) * P], pbuf[:, t, k * P:(k + 1) * P], ident,
                                   after=[m5, freed])
                m7 = A.op(act.activation, ptb[:, :, :], pt, ACT.Copy, after=[m6, freed_pt])
                banks.give(bank, m7)
                bufs["p"].give(pbuf, m6)
                bufs["st"].give(st, m5)
                yield
                bank, freed = banks.take()
                for k in range(2):
                    m8 = PE.op(ten.matmul, bank[o:o + HD, 0:S], vm[:, layer, k, h * HD:(h + 1) * HD], ptb[:, k, :],
                               start=(k == 0), stop=(k == 1), after=[m7, m_kv, freed])
                bufs["pt"].give(ptb, m8)
                y, freed_y = tmp256.take()
                m9 = V.op(vec.tensor_tensor, y[o:o + HD, :], bank[o:o + HD, 0:S], gm[o:o + HD, j, :],
                          ALU.mult, after=[m8, m_g, freed_y])
                banks.give(bank, m9)
                m10 = split_input(0, y[o:o + HD, :], 1.0, m9, h1h(BT + j)[o:o + HD, :], h1l(BT + j)[o:o + HD, :],
                                  None)
                tmp256.give(y, m10)
                marks[BT + j].append(m10)
                yield

            skewed(head(h) for h in range(MEM_HEADS))
            return marks

        def mix_out(layer, m_y, ybuf, sqbuf, next_first, next_gain):
            m_yt, m_sq = [None] * KT, [None] * KT

            def evac(panel, ps, mark):
                m_yt[panel] = V.op(vec.tensor_copy, ybuf[:, panel, :], ps, after=[mark])
                m_sq[panel] = A.op(act.activation, sqbuf[:, panel, :], ybuf[:, panel, :], ACT.Square,
                                   after=[m_yt[panel]])
                return (m_yt[panel],)

            project(f"w_out{layer}", list(range(KT)), h1h, h1l, S, m_y, evac)
            m_last = PE.last()
            m_rs = norm_stat(lambda k: sqbuf[:, k, :], KT, S, "ones_d", EPS, m_sq, rstd[:, 0:S])
            for k in range(KT):
                m = V.op(vec.scalar_tensor_tensor, ybuf[:, k, :], ybuf[:, k, :], col(f"post{layer}", k),
                         rstd[:, 0:S], ALU.mult, ALU.mult, after=[m_rs, m_yt[k]])
                m = V.op(vec.tensor_tensor, x1(k), x1(k), ybuf[:, k, :], ALU.add, after=[m])
                residual_done(k, next_first, next_gain, [m, m_meta], m_last)

        ph = ExitStack()
        tr = sb("tr", [P, W_R], ph)
        zr, zk, zv = (sb(n, [P, BT, S], ph) for n in ("zr", "zk", "zv"))
        zl = sb("zl", [P, S], ph)
        gate = sb("gate", [P, BT, S], ph)
        qm = sb("qm", [P, MT, MEM], ph)
        gm = sb("gm", [P, MT, MEM], ph)
        ed = sb("ed", [P, BT, 2, CH + 1], ph)
        inv = sb("inv", [P, BT, S], ph)
        av_ = sb("av_", [P, BT, S], ph)
        kk = sb("kkh", [P, BT, S], ph)
        zt_ring = Ring([sb(f"zt{i}", [P, S + 1], ph) for i in range(2)])
        lw = sb("lw", [P, BR], ph)
        work = sb("work", [P, 5, 1024], ph)
        xt_all = sb("xt_all", [P, 6, 512], ph)
        mrs = sb("mrs", [P, MEM], ph)
        inner = ExitStack()
        xnh, xnl = sb("xnh", [P, KT, S], inner, F32R), sb("xnl", [P, KT, S], inner, F32R)
        x0h, x0l = lambda k: xnh[:, k, :], lambda k: xnl[:, k, :]

        def tabr(name):
            o, n = OFF_R[name]
            return tr[:, o:o + n]

        work_flat = work[:, :, :].rearrange("p a b -> p (a b)")
        tiles8 = lambda buf: buf.rearrange("p (k s) -> p k s", k=KT)
        mem_in, sq = tiles8(work_flat[:, 0:KT * S]), tiles8(work_flat[:, KT * S:2 * KT * S])
        sq_x = tiles8(xt_all[:, :, :].rearrange("p a b -> p (a b)")[:, 0:KT * S])
        m_mem = A.dma(mem_in, memT, s_in[3], 16)
        m_x = A.dma(res[:, :, N_META:T], xT, s_in[0], 16)
        m_ta = A.dma(ta[:, :], tab_a, s_in[1], 16)
        m_lw = A.dma(lw[:, :], lora, s_in[4], 16)
        s_in2 = [sem("s_tab_r"), sem("s_tab_b"), sem("s_meta")]
        m_tr = A.dma(tr[:, :], tab_r, s_in2[0], 16)
        m_meta = A.dma(res[:, :, 0:N_META], metaT, s_in2[2], 16)
        m_zero = V.op(vec.memset, zt_ring.free[0][0][:, 0:1], 0.0)
        m_zero = V.op(vec.memset, zt_ring.free[1][0][:, 0:1], 0.0)
        m_zero = V.op(vec.memset, ed[:, :, :, 0:1], 0.0)

        m_kv = {0: [], 1: []}
        m_mh = [split_input(k, mem_in[:, k, :], col("memn0", k), m_mem, x0h(k), x0l(k), None) for k in range(KT)]
        m_msq = [square(k, sq[:, k, :], mem_in[:, k, :], [m_mem]) for k in range(KT)]

        def mem_stat():
            stat["mem"] = norm_stat(lambda k: sq[:, k, :], KT, MEM, "ones_d", EPS, m_msq, mrs[:, :])

        def token_major(tiles, dst_of, scale, m_scale, marks, bufs):
            pending = []

            def flush():
                panel, t, m1 = pending.pop(0)
                m2, marks[panel] = turn(t, tiles, dst_of(panel), m1, None)
                bufs.give(t, m2)

            def evac(panel, ps, mark):
                t, freed_t = bufs.take()
                m1 = V.op(vec.tensor_tensor, t[:, 0:ps.shape[1]], ps, scale(), ALU.mult, after=[mark, freed_t, m_scale()])
                if pending:
                    flush()
                pending.append((panel, t, m1))
                return (m1,)

            return evac, flush

        def memory_kv(layer, hi, lo, m_in, hook):
            def k_evac(panel, ps, mark):
                m = V.op(vec.tensor_tensor, kmT[:, layer, panel, :], ps, mrs[:, :], ALU.mult,
                         after=[mark, stat["mem"]])
                m_kv[layer].append(m)
                return (m,)

            m_v_ = {}
            v_evac, flush = token_major([(0, P), (P, P)], lambda panel: lambda j, n, rows:
                                        vm[0:rows, layer, j:j + n, (panel - 2) * P:(panel - 1) * P],
                                        lambda: mrs[:, :], lambda: stat["mem"], m_v_, tmp256)
            project(f"w_mem{layer}", [0, 1], hi, lo, MEM, m_in, k_evac, hook=hook)
            project(f"w_mem{layer}", [2, 3], hi, lo, MEM, m_in, v_evac)
            flush()
            m_kv[layer] += list(m_v_.values())

        memory_kv(0, x0h, x0l, m_mh, mem_stat)
        m_mem0 = PE.last()
        m_mh1 = [split_input(k, mem_in[:, k, :], col("memn1", k), None, xh[:, k, 0:S], xl[:, k, 0:S], None)
                 for k in range(KT)]
        m_xsq = [square(k, sq_x[:, k, :], x1(k), [m_x]) for k in range(KT)]
        m_rs0 = norm_stat(lambda k: sq_x[:, k, :], KT, S, "ones_d", EPS, m_xsq, rstd[:, 0:S])
        m_h = []
        for k in range(KT):
            m = V.op(vec.tensor_tensor, sq_x[:, k, :], x1(k), rstd[:, 0:S], ALU.mult, after=[m_rs0])
            m_h.append(split_input(k, sq_x[:, k, :], col("pre0", k), m, x0h(k), x0l(k), m_mem0))
        memory_kv(1, h1h, h1l, m_mh1, None)

        m_z = {}

        def shift_evac(panel, ps, mark):
            if panel == 18:
                dst = zl[:, :]
            else:
                dst = (zr, zk, zv)[panel // BT][:, panel % BT, :]
            zt, freed = zt_ring.take()
            m1 = A.op(act.activation, zt[:, 1:S + 1], ps, ACT.Copy, after=[mark, freed, m_zero])
            m2 = V.op(vec.tensor_tensor, dst, zt[:, 0:S], zt[:, 1:S + 1], ALU.subtract, after=[m1])
            m_z[panel] = V.op(vec.scalar_tensor_tensor, dst, dst, col("mu", panel), zt[:, 1:S + 1],
                              ALU.mult, ALU.add, after=[m2, m_cols])
            zt_ring.give(zt, m_z[panel])
            return (m1,)

        project("a_w_in", [18], x0h, x0l, S, m_h, shift_evac)
        m_th = A.op(act.activation, zl[0:64, :], zl[0:64, :], ACT.Tanh, after=[m_z[18]])
        m_ed, m_inv, m_a = {}, {}, {}
        ones_s = tab("ones")

        m_cum = {}

        def low_rank(i):
            bank, freed = banks.take()
            m = PE.op(ten.matmul, bank[:, 0:S], lw[0:64, i * P:(i + 1) * P], zl[0:64, :], start=True, stop=True,
                      after=[m_lw, m_th, freed])
            e, freed_e = tmp256.take()
            m1 = A.op(act.activation, e[:, :], bank[:, 0:S], ACT.Sigmoid, bias=col("w0", i),
                      after=[m, m_cols, freed_e])
            banks.give(bank, m1)
            for c in range(2):
                m_cum[i] = V.op(vec.tensor_tensor_scan, ed[:, i, c, 1:CH + 1], ones_s, e[:, c * CH:(c + 1) * CH],
                                0.0, ALU.mult, ALU.add, after=[m1, m_ta, m_zero])
            tmp256.give(e, m_cum[i])
            bank, freed = banks.take()
            m = PE.op(ten.matmul, bank[:, 0:S], lw[64:128, i * P:(i + 1) * P], zl[64:128, :], start=True, stop=True,
                      after=[m_lw, m_z[18], freed])
            m_a[i] = A.op(act.activation, av_[:, i, :], bank[:, 0:S], ACT.Sigmoid, bias=col("a0", i), after=[m])
            banks.give(bank, m_a[i])

        def decays(i):
            mid = tab("mid")
            m_inv[i] = A.op(act.activation, inv[:, i, :].rearrange("p (c t) -> p c t", c=2), ed[:, i, :, 1:CH + 1],
                            ACT.Exp, bias=mid[:, 1:2], scale=DECAY_C, after=[m_cum[i], m_ta])
            m_ed[i] = A.op(act.activation, ed[:, i, :, :], ed[:, i, :, :], ACT.Exp, bias=mid[:, 0:1],
                           scale=-DECAY_C, after=[m_inv[i]])

        project("a_w_in", [6, 7], x0h, x0l, S, m_h, shift_evac)
        for i in range(BT):
            low_rank(i)
        for i in range(BT):
            decays(i)
        project("a_w_in", [8, 9, 10, 11], x0h, x0l, S, m_h, shift_evac)

        m_ah, m_bt, m_kt_, m_rh, m_km, m_kk = {}, {}, {}, {}, {}, {}

        def keys(i):
            t, freed_t = tmp256.take()
            m1 = V.op(vec.tensor_scalar, kk[:, i, :], zk[:, i, :], col("kk", i), None, ALU.mult,
                      after=[m_z[6 + i], m_cols])
            m2 = A.op(act.activation, t[:, :], kk[:, i, :], ACT.Square, after=[m1, freed_t])
            bank, freed = banks.take()
            m3 = PE.op(ten.matmul, bank[:, 0:S], tab("blk"), t[:, :], start=True, stop=True, after=[m2, m_ta, freed])
            m4 = rsqrt(t[:, :], bank[:, 0:S], 1e-12, ALU.max, [m3])
            banks.give(bank, m4)
            m5 = V.op(vec.tensor_tensor, kk[:, i, :], kk[:, i, :], t[:, :], ALU.mult, after=[m4, m2])
            m6 = V.op(vec.tensor_scalar, t[:, :], av_[:, i, :], 1.0, col("ka", i), ALU.subtract, ALU.mult,
                      after=[m5, m_a[i]])
            m_km[i] = V.op(vec.scalar_tensor_tensor, zk[:, i, :], t[:, :], 1.0, zk[:, i, :], ALU.add, ALU.mult,
                           after=[m6])
            tmp256.give(t, m_km[i])
            m7 = V.op(vec.tensor_tensor, av_[:, i, :], av_[:, i, :], kk[:, i, :], ALU.mult, after=[m6])
            m_bt[i] = V.op(vec.tensor_tensor, av_[:, i, :], av_[:, i, :], inv[:, i, :], ALU.mult,
                           after=[m7, m_inv[i]])
            m_kt_[i] = V.op(vec.tensor_tensor, inv[:, i, :], inv[:, i, :], zk[:, i, :], ALU.mult,
                            after=[m_bt[i], m_km[i]])
            split = lambda buf: buf[:, i, :].rearrange("p (c t) -> p c t", c=2)
            m_ah[i] = V.op(vec.tensor_tensor, split(kk), split(kk), ed[:, i, :, 0:CH], ALU.mult,
                           after=[m7, m_ed[i]])

        for i in range(BT):
            keys(i)
            project("a_w_in", [i], x0h, x0l, S, m_h, shift_evac)

        GROUPS = [(p, j) for p in range(2) for j in range(3)]
        b4 = lambda a: a.unsqueeze(1).broadcast_to([P, 4, P])
        v4 = lambda a: a.rearrange("p (g n) -> p g n", g=4)
        m_sq_done = everyone()

        def pieces(g):
            p, j = GROUPS[g]
            for q in range(4):
                yield q, 2 * j + q // 2, HD * p, (q % 2) * CH

        filler = []

        def fill(n=1):
            for _ in range(n):
                if filler:
                    filler.pop(0)()

        m_xt = {}

        def invert(g):
            slot = g % 3
            nlt, xx, yy = work_flat[:, slot * 1536:slot * 1536 + 512], \
                work_flat[:, slot * 1536 + 512:slot * 1536 + 1024], work_flat[:, slot * 1536 + 1024:slot * 1536 + 1536]
            xt = xt_all[:, g, :]
            bank, freed = banks.take()
            for q, i, o, t0 in pieces(g):
                m = PE.op(ten.matmul, bank[:, q * P:(q + 1) * P], av_[o:o + HD, i, t0:t0 + CH],
                          kk[o:o + HD, i, t0:t0 + CH], start=True, stop=True, after=[m_bt[i], m_ah[i], freed])
            m_nlt = V.op(vec.tensor_tensor, v4(nlt), v4(bank[:, :]), b4(tabr("neg_up")), ALU.mult,
                         after=[m, m_tr, m_sq_done])
            banks.give(bank, m_nlt)
            bank, freed = banks.take()
            for q, i, o, t0 in pieces(g):
                m = PE.op(ten.matmul, bank[:, q * P:(q + 1) * P], kk[o:o + HD, i, t0:t0 + CH],
                          av_[o:o + HD, i, t0:t0 + CH], start=True, stop=True, after=[freed])
            m1 = V.op(vec.tensor_tensor, v4(xx), v4(bank[:, :]), b4(tabr("neg_m0")), ALU.mult, after=[m])
            banks.give(bank, m1)
            m_x_ = V.op(vec.tensor_tensor, v4(xx), v4(xx), b4(ident), ALU.add, after=[m1])
            m2 = V.op(vec.tensor_tensor, v4(xt), v4(nlt), b4(tabr("m0t")), ALU.mult, after=[m_nlt])
            m_t_ = V.op(vec.tensor_tensor, v4(xt), v4(xt), b4(ident), ALU.add, after=[m2])
            for level in range(1, 7):
                yield
                bank, freed = banks.take()
                for q in range(4):
                    c = slice(q * P, (q + 1) * P)
                    m = PE.op(ten.matmul, bank[:, c], nlt[:, c], xx[:, c], start=True, stop=True,
                              after=[m_x_, m_nlt, freed])
                m_y = V.op(vec.tensor_tensor, v4(yy), v4(bank[:, :]), b4(tabr(f"m{level}")), ALU.mult, after=[m])
                banks.give(bank, m_y)
                yield
                if level < 6:
                    bank, freed = banks.take()
                    for q in range(4):
                        c = slice(q * P, (q + 1) * P)
                        m = PE.op(ten.matmul, bank[:, c], xt[:, c], yy[:, c], start=True, stop=True,
                                  after=[m_y, m_t_, freed])
                    m_x_ = V.op(vec.tensor_tensor, xx, xx, bank[:, :], ALU.add, after=[m])
                    banks.give(bank, m_x_)
                bank, freed = banks.take()
                for q in range(4):
                    c = slice(q * P, (q + 1) * P)
                    m = PE.op(ten.matmul, bank[:, c], yy[:, c], xt[:, c], start=True, stop=True,
                              after=[m_y, m_t_, freed])
                m_t_ = V.op(vec.tensor_tensor, xt, xt, bank[:, :], ALU.add, after=[m])
                banks.give(bank, m_t_)
                fill()
            m_xt[g] = m_t_

        m_gmem, m_gate, m_qm = [], [], []

        def silu_evac(dst, marks):
            def evac(panel, ps, mark):
                t, freed = tmp256.take()
                m1 = A.op(act.activation, t[:, :], ps, ACT.Sigmoid, after=[mark, freed])
                m3 = V.op(vec.tensor_tensor, dst(panel), t[:, :], ps, ALU.mult, after=[m1])
                tmp256.give(t, m3)
                marks.append(m3)
                return (m3,)
            return evac

        def qm_evac(panel, ps, mark):
            m = A.op(act.activation, qm[:, panel - 25, :], ps, ACT.Copy, after=[mark])
            m_qm.append(m)
            return (m,)

        gate_evac = silu_evac(lambda p_: gate[:, p_ - 19, :], m_gate)
        gm_evac = silu_evac(lambda p_: gm[:, p_ - 27, :], m_gmem)
        for pair in ([12, 13], [14, 15], [16, 17]):
            filler.append(lambda pair=pair: project("a_w_in", pair, x0h, x0l, S, m_h, shift_evac))
        for pair in ([19, 20], [21, 22], [23, 24]):
            filler.append(lambda pair=pair: project("a_w_in", pair, x0h, x0l, S, m_h, gate_evac))
        filler.append(lambda: project("a_w_in", [25, 26], x0h, x0l, S, m_h, qm_evac))
        filler.append(lambda: project("a_w_in", [27, 28], x0h, x0l, S, m_h, gm_evac))

        skewed(invert(g) for g in range(3))
        skewed(invert(g) for g in range(3, 6))
        fill(len(filler))

        m_bonus, m_vt, m_bk = [], {}, {}
        inner.close()
        inner = ExitStack()
        vtok = sb("vtok", [P, 2, BR], inner)
        btok, ktok = (sb(n, [P, BR], inner) for n in ("btok", "ktok"))
        wu_w = sb("wu_w", [P, 2, BT * HD], inner)
        wu_u = sb("wu_u", [P, 2, BT * HD], inner)
        sqr_flat = sqr[:, :, :].rearrange("p a b -> p (a b)")
        ysb = sqr_flat[:, 0:BR * 2].rearrange("p (i s) -> p i s", i=BT)
        st1 = sqr_flat[:, 2 * BR:2 * BR + BT * HD].rearrange("p (i n) -> p i n", i=BT)
        A.wait(PE.last())
        V.wait(PE.last())
        for c in range(2):
            for part in range(2):
                bank, freed = banks.take()
                for n in range(3):
                    i = 3 * part + n
                    m = PE.op(ten.transpose, bank[:, n * P:(n + 1) * P], zv[:, i, c * CH:(c + 1) * CH], ident,
                              after=[m_z[12 + i], freed])
                m_vt[c, part] = A.op(act.activation, vtok[:, c, part * 384:(part + 1) * 384], bank[:, 0:384],
                                     ACT.Copy, after=[m])
                banks.give(bank, m_vt[c, part])
        for dst, src in ((btok, av_), (ktok, inv)):
            for part in range(2):
                bank, freed = banks.take()
                for n in range(3):
                    i = 3 * part + n
                    m = PE.op(ten.transpose, bank[:, n * P:(n + 1) * P], src[:, i, 0:CH], ident,
                              after=[m_kt_[i], freed])
                m_bk[src is inv, part] = A.op(act.activation, dst[:, part * 384:(part + 1) * 384], bank[:, 0:384],
                                              ACT.Copy, after=[m])
                banks.give(bank, m_bk[src is inv, part])

        for i in range(BT):
            t, freed_t = tmp256.take()
            m1 = V.op(vec.scalar_tensor_tensor, t[:, :], zr[:, i, :], col("rk", i), zk[:, i, :], ALU.mult, ALU.mult,
                      after=[m_z[i], m_km[i], freed_t])
            bank, freed = banks.take()
            m2 = PE.op(ten.matmul, bank[:, 0:S], tab("blk"), t[:, :], start=True, stop=True, after=[m1, freed])
            m3 = V.op(vec.tensor_tensor, zk[:, i, :], bank[:, 0:S], zv[:, i, :], ALU.mult,
                      after=[m2, m_z[12 + i], m_kt_[i]])
            banks.give(bank, m3)
            m_bonus.append(m3)
            tmp256.give(t, m2)
            split = lambda buf: buf[:, i, :].rearrange("p (c t) -> p c t", c=2)
            m_rh[i] = V.op(vec.tensor_tensor, split(zr), split(zr), ed[:, i, :, 1:CH + 1], ALU.mult,
                           after=[m1, m_ed[i]])

        m_ysb = {}
        m_state = None
        m_prev = [m_xt[g] for g in range(6)]
        for c in range(2):
            t0 = c * CH
            mats = {}
            for kind, lhs, rhs, mask in (("ak", inv, kk, "up"), ("rb", av_, zr, "upinc"), ("rk", inv, zr, "upinc")):
                base = {"ak": 0, "rb": 1536, "rk": 3072}[kind]
                for p in range(2):
                    for half in range(2):
                        bank, freed = banks.take()
                        for n in range(3):
                            i = 3 * half + n
                            o = HD * p
                            m = PE.op(ten.matmul, bank[:, n * P:(n + 1) * P], lhs[o:o + HD, i, t0:t0 + CH],
                                      rhs[o:o + HD, i, t0:t0 + CH], start=True, stop=True,
                                      after=[m_kt_[i], m_ah[i], m_rh[i], freed])
                        dst = work_flat[:, base + (p * 2 + half) * 384:base + (p * 2 + half + 1) * 384]
                        m = V.op(vec.tensor_tensor, dst.rearrange("p (g n) -> p g n", g=3),
                                 bank[:, 0:384].rearrange("p (g n) -> p g n", g=3),
                                 tabr(mask).unsqueeze(1).broadcast_to([P, 3, P]), ALU.mult, after=[m, m_prev])
                        banks.give(bank, m)
                        for n in range(3):
                            mats[kind, p, 3 * half + n] = (dst[:, n * P:(n + 1) * P], m)
            m_u = {}
            for p in range(2):
                bank, freed = banks.take()
                for i in range(BT):
                    out = bank[:, i * HD:(i + 1) * HD]
                    h = 2 * i + p
                    a, m_a_ = mats["ak", p, i]
                    if c:
                        PE.quiet(ten.matmul, out, kk[HD * p:HD * p + HD, i, t0:t0 + CH], st1[HD * p:HD * p + HD, i, :],
                                 start=True, stop=False, after=[m_state, freed])
                    m = PE.op(ten.matmul, out, a, vtok[:, c, h * HD:(h + 1) * HD], start=not c, stop=True,
                              after=[m_a_, m_vt[c, i // 3], freed])
                m = A.op(act.activation, wu_w[:, p, :], bank[:, 0:BT * HD], ACT.Copy, after=[m])
                banks.give(bank, m)
                m_u["w", p] = m
            for p in range(2):
                bank, freed = banks.take()
                for i in range(BT):
                    g, q = 3 * p + i // 2, 2 * (i % 2) + c
                    m = PE.op(ten.matmul, bank[:, i * HD:(i + 1) * HD], xt_all[:, g, q * P:(q + 1) * P],
                              wu_w[:, p, i * HD:(i + 1) * HD], start=True, stop=True,
                              after=[m_u["w", p], m_xt[g], freed])
                m = A.op(act.activation, wu_u[:, p, :], bank[:, 0:BT * HD], ACT.Copy, scale=-1.0, after=[m])
                banks.give(bank, m)
                m_u[p] = m
            for i in range(BT):
                bank, freed = banks.take()
                for p in range(2):
                    h, o = 2 * i + p, HD * p
                    out = bank[o:o + HD, 0:CH]
                    vt = vtok[:, c, h * HD:(h + 1) * HD]
                    PE.quiet(ten.matmul, out, wu_u[:, p, i * HD:(i + 1) * HD], mats["rb", p, i][0], start=True,
                             stop=False, after=[m_u[p], mats["rb", p, i][1], freed])
                    m = PE.op(ten.matmul, out, vt, mats["rk", p, i][0], start=False, stop=(c == 0),
                              after=[mats["rk", p, i][1]])
                    if c:
                        m = PE.op(ten.matmul, out, st1[o:o + HD, i, :], zr[o:o + HD, i, t0:t0 + CH], start=False,
                                  stop=True)
                m_ysb[c, i] = A.op(act.activation, ysb[:, i, t0:t0 + CH], bank[:, 0:CH], ACT.Copy, after=[m])
                banks.give(bank, m_ysb[c, i])
            m_prev = [PE.last()]
            if c == 0:
                bank, freed = banks.take()
                for i in range(BT):
                    for p in range(2):
                        h, o = 2 * i + p, HD * p
                        out = bank[o:o + HD, i * HD:(i + 1) * HD]
                        PE.quiet(ten.matmul, out, btok[:, h * HD:(h + 1) * HD], wu_u[:, p, i * HD:(i + 1) * HD],
                                 start=True, stop=False, after=[m_bk[False, i // 3], freed])
                        m = PE.op(ten.matmul, out, ktok[:, h * HD:(h + 1) * HD], vtok[:, 0, h * HD:(h + 1) * HD],
                                  start=False, stop=True, after=[m_bk[True, i // 3]])
                for i in range(BT):
                    m_state = V.op(vec.tensor_scalar, st1[:, i, :], bank[:, i * HD:(i + 1) * HD],
                                   ed[:, i, 0, CH:CH + 1], math.exp(-MID), ALU.mult, ALU.mult, after=[m, m_ed[i]])
                banks.give(bank, m_state)
                m_prev = [PE.last()]

        xt_flat = xt_all[:, :, :].rearrange("p a b -> p (a b)")
        quarter = [xt_flat[:, i * 512:(i + 1) * 512].rearrange("p (a b) -> p a b", a=2) for i in range(4)]
        A.wait(*m_prev)
        bufs = {"p": Ring(quarter[0:2]), "pt": Ring(quarter[2:4]),
                "st": Ring([sb(f"mst{i}", [P, 8], inner) for i in range(3)])}
        m_y = memory_attention(0, qm, gm, m_qm, m_kv[0], m_gmem, bufs)

        for i in range(BT):
            d, freed_d = tmp256.take()
            t, freed_t = tmp256.take()
            bank, freed = banks.take()
            m1 = PE.op(ten.matmul, bank[:, 0:S], tab("blkm"), ysb[:, i, :], start=True, stop=True,
                       after=[m_ysb[0, i], m_ysb[1, i], freed])
            m2 = V.op(vec.tensor_tensor, d[:, :], ysb[:, i, :], bank[:, 0:S], ALU.subtract, after=[m1, freed_d])
            banks.give(bank, m2)
            m3 = A.op(act.activation, t[:, :], d[:, :], ACT.Square, after=[m2, freed_t])
            bank, freed = banks.take()
            m4 = PE.op(ten.matmul, bank[:, 0:S], tab("blkm"), t[:, :], start=True, stop=True, after=[m3, freed])
            m5 = rsqrt(t[:, :], bank[:, 0:S], LNX_EPS, ALU.add, [m4])
            banks.give(bank, m5)
            m6 = V.op(vec.scalar_tensor_tensor, d[:, :], d[:, :], col("lnw", i), t[:, :], ALU.mult, ALU.mult,
                      after=[m5, m3])
            tmp256.give(t, m6)
            m7 = V.op(vec.scalar_tensor_tensor, d[:, :], d[:, :], col("lnb", i), zk[:, i, :], ALU.add, ALU.add,
                      after=[m6, m_bonus[i]])
            m8 = V.op(vec.tensor_tensor, d[:, :], d[:, :], gate[:, i, :], ALU.mult, after=[m7, m_gate])
            m_y[i] = split_input(i, d[:, :], 1.0, m8, h1h(i), h1l(i), None)
            tmp256.give(d, m_y[i])

        ybuf = work_flat[:, 0:2048].rearrange("p (k s) -> p k s", k=KT)
        sqb = work_flat[:, 2048:4096].rearrange("p (k s) -> p k s", k=KT)
        V.wait(*m_prev)
        A.wait(*m_prev)
        mix_out(0, m_y, ybuf, sqb, N_META, "pre1")
        new_phase()
        inner.close()
        ph.close()

        ph = ExitStack()
        kh, kl = sb("kh", [P, KT, S], ph, F32R), sb("kl", [P, KT, S], ph, F32R)
        sq = sb("sq", [P, KT, S], ph)
        kT = sb("kT", [P, BT, S], ph)
        qT = sb("qT", [P, BT, S], ph)
        vt = sb("vt", [P, 2, BR], ph)
        gate = sb("gate1", [P, BT, S], ph)
        qm = sb("qm1", [P, MT, MEM], ph)
        gm = sb("gm1", [P, MT, MEM], ph)
        ybuf = sb("ybuf1", [P, KT, S], ph)
        bufs = {"p": Ring([sb(f"mp1{i}", [P, 2, MEM], ph) for i in range(2)]),
                "pt": Ring([sb(f"mpt1{i}", [P, 2, S], ph) for i in range(2)]),
                "st": Ring([sb(f"mst1{i}", [P, 8], ph) for i in range(3)])}
        scb = Ring([sb(f"scb{i}", [P, 2, 384], ph) for i in range(3)])
        ptb1 = Ring([sb(f"ptb1{i}", [P, 384], ph) for i in range(2)])
        stb = Ring([sb(f"stb{i}", [P, 16], ph) for i in range(4)])

        m_h = list(m_next)
        rs1 = rstd[:, 0:S]

        LQ = 2 * BT
        m = V.op(vec.tensor_tensor, small[:, LQ:LQ + 2], cols[:, COL["lam"]:COL["lam"] + 2],
                 cols[:, COL["lam"] + 2:COL["lam"] + 4], ALU.mult)
        bank, freed = banks.take()
        m = PE.op(ten.matmul, bank[:, 0:2], tab("ones"), small[:, LQ:LQ + 2], start=True, stop=True, after=[m, freed])
        m = A.op(act.activation, small[:, LQ + 2:LQ + 4], bank[:, 0:2], ACT.Exp, after=[m])
        banks.give(bank, m)
        m = V.op(vec.tensor_tensor, small[:, LQ + 4:LQ + 5], small[:, LQ + 3:LQ + 4], small[:, LQ + 2:LQ + 3],
                 ALU.subtract, after=[m])
        m_lam = V.op(vec.tensor_scalar, small[:, LQ + 5:LQ + 6], small[:, LQ + 4:LQ + 5], LAM_INIT, None,
                     ALU.subtract, after=[m])
        m_sub = V.op(vec.tensor_scalar, small[:, LQ + 6:LQ + 7], col("subln"), 1.0 - LAM_INIT, None, ALU.mult)
        neg_lam, subln = small[:, LQ + 5:LQ + 6], small[:, LQ + 6:LQ + 7]

        m_q, m_k, m_v, m_qm, m_gmem, m_gate = {}, {}, {}, [], [], []

        def scaled(dst_of, marks, extra=1.0):
            def evac(panel, ps, mark):
                m = V.op(vec.scalar_tensor_tensor, dst_of(panel), ps, extra, rs1, ALU.mult, ALU.mult,
                         after=[mark, stat["x"]])
                marks[panel] = m
                return (m,)
            return evac

        def scaled_silu(dst_of, marks):
            def evac(panel, ps, mark):
                t, freed = tmp256.take()
                m1 = V.op(vec.tensor_tensor, dst_of(panel), ps, rs1, ALU.mult, after=[mark, stat["x"]])
                m2 = A.op(act.activation, t[:, :], dst_of(panel), ACT.Sigmoid, after=[m1, freed])
                m3 = G.op(pool.tensor_tensor, dst_of(panel), dst_of(panel), t[:, :], ALU.mult, after=[m2])
                tmp256.give(t, m3)
                marks.append(m3)
                return (m1,)
            return evac

        m_qmd = {}
        slopes = alibi_slopes(BT)
        m_y = {}

        def diff_head(h):
            st, freed_st = stb.take()
            pb, freed_p = scb.take()
            for c in range(2):
                o = HD * c
                bank, freed = banks.take()
                PE.quiet(ten.matmul, bank[:, 0:P], qT[o:o + HD, h, 0:P], kT[o:o + HD, h, 0:P], start=True, stop=True,
                         after=[m_q[h], m_k[h], freed])
                m = PE.op(ten.matmul, bank[:, P:384], qT[o:o + HD, h, P:S], kT[o:o + HD, h, :], start=True, stop=True)
                m1 = V.op(vec.scalar_tensor_tensor, pb[:, c, :], tab("dist"), -slopes[h], bank[:, 0:384], ALU.mult,
                          ALU.add, after=[m, freed_p, freed_st])
                banks.give(bank, m1)
                V.op(vec.tensor_reduce, st[:, 2 * c:2 * c + 1], pb[:, c, 0:P], AX_X, ALU.max, after=[m1])
                m2 = V.op(vec.tensor_reduce, st[:, 2 * c + 1:2 * c + 2], pb[:, c, P:384], AX_X, ALU.max)
            m3 = V.op(vec.tensor_scalar, st[:, 4:8], st[:, 0:4], -1.0, None, ALU.mult, after=[m2])
            for c in range(2):
                for t, (a, b) in enumerate(((0, P), (P, 384))):
                    n = 2 * c + t
                    m4 = A.op(act.activation, pb[:, c, a:b], pb[:, c, a:b], ACT.Exp, bias=st[:, 4 + n:5 + n],
                              accum_out=st[:, 8 + n:9 + n], after=[m3])
            m5 = V.op(vec.reciprocal, st[:, 12:16], st[:, 8:12], after=[m4])
            m6 = V.op(vec.tensor_scalar, st[:, 14:16], st[:, 14:16], neg_lam, None, ALU.mult, after=[m5, m_lam])
            for t, (a, b) in enumerate(((0, P), (P, 384))):
                m7 = V.op(vec.tensor_scalar, pb[:, 0, a:b], pb[:, 0, a:b], st[:, 12 + t:13 + t], None, ALU.mult,
                          after=[m5])
                m8 = V.op(vec.scalar_tensor_tensor, pb[:, 0, a:b], pb[:, 1, a:b], st[:, 14 + t:15 + t], pb[:, 0, a:b],
                          ALU.mult, ALU.add, after=[m6, m7])
            stb.give(st, m8)
            yield
            pt, freed_pt = ptb1.take()
            bank, freed = banks.take()
            for out, src in ((0, 0), (P, P), (2 * P, 2 * P)):
                m9 = PE.op(ten.transpose, bank[:, out:out + P], pb[:, 0, src:src + P], ident, after=[m8, freed])
            m10 = A.op(act.activation, pt[:, :], bank[:, 0:384], ACT.Copy, after=[m9, freed_pt])
            banks.give(bank, m10)
            scb.give(pb, m9)
            yield
            ob, freed = banks.take()
            PE.quiet(ten.matmul, ob[:, 0:S], vt[:, 0, h * P:(h + 1) * P], pt[:, 0:S], start=True, stop=False,
                     after=[m10, freed, m_v[6 + h]])
            m11 = PE.op(ten.matmul, ob[:, P:S], vt[:, 1, h * P:(h + 1) * P], pt[:, S:384], start=False, stop=True)
            ptb1.give(pt, m11)
            t, freed_t = tmp256.take()
            m12 = A.op(act.activation, t[:, :], ob[:, 0:S], ACT.Square, after=[m11, freed_t])
            yield
            r, freed_r = tmp256.take()
            m13 = norm_stat(lambda k: t[:, :], 1, S, "ones128", EPS, m12, r[:, :], freed_r)
            tmp256.give(t, m13)
            m14 = V.op(vec.scalar_tensor_tensor, r[:, :], ob[:, 0:S], subln, r[:, :], ALU.mult, ALU.mult,
                       after=[m13, m_sub])
            banks.give(ob, m14)
            m15 = V.op(vec.tensor_tensor, r[:, :], r[:, :], gate[:, h, :], ALU.mult, after=[m14, m_gate])
            m_y[h] = split_input(h, r[:, :], 1.0, m15, h1h(h), h1l(h), None)
            tmp256.give(r, m_y[h])
            yield

        project("b_w_in", list(range(0, 6)), h1h, h1l, S, m_h, scaled(lambda p_: qT[:, p_, :], m_q, HD ** -0.5),
                hook=lambda: residual_stat(S))
        m_hk = [split_input(k, x1(k), col("kvn", k), None, kh[:, k, :], kl[:, k, :], None) for k in range(KT)]
        khk, klk = lambda k: kh[:, k, :], lambda k: kl[:, k, :]
        project("w_kv", list(range(0, 6)), khk, klk, S, m_hk, scaled(lambda p_: kT[:, p_, :], m_k))
        v_evac, flush = token_major([(0, P), (P, P)], lambda panel: lambda j, n, rows:
                                    vt[0:rows, j:j + n, (panel - 6) * P:(panel - 5) * P], lambda: rs1,
                                    lambda: stat["x"], m_v, tmp256)
        project("w_kv", list(range(6, 12)), khk, klk, S, m_hk, v_evac)
        flush()
        project("b_w_in", list(range(6, 12)), h1h, h1l, S, m_h, scaled_silu(lambda p_: gate[:, p_ - 6, :], m_gate))
        project("b_w_in", [12, 13], h1h, h1l, S, m_h, scaled(lambda p_: qm[:, p_ - 12, :], m_qmd))
        project("b_w_in", [14, 15], h1h, h1l, S, m_h, scaled_silu(lambda p_: gm[:, p_ - 14, :], m_gmem))
        m_in1 = PE.last()
        A.wait(m_in1)
        V.wait(m_in1)
        m_qm = list(m_qmd.values())
        skewed(diff_head(h) for h in range(BT))
        m_y.update(memory_attention(1, qm, gm, m_qm, m_kv[1], m_gmem, bufs))
        mix_out(1, m_y, ybuf, sq, 0, "ffn1")
        new_phase()
        ph.close()
        first.close()

        second = ExitStack()
        tb = sb("tb", [P, W_B], second)
        m_tb = A.dma(tb[:, :], tab_b, s_in2[1], 16)
        tmp = Ring([sb(f"tmp2{i}", [P, T], second) for i in range(7)])
        x2 = lambda k: res[:, k, :]
        h2h, h2l = lambda k: xh[:, k, :], lambda k: xl[:, k, :]

        def tabb(name):
            o, n = OFF_B[name]
            return tb[:, o:o + n]

        def times_rms(out, ps, mark, freed=None):
            return V.op(vec.tensor_tensor, out, ps, rstd[:, :], ALU.mult, after=[mark, stat["x"], freed])

        def ffn(n, next_gain):
            ph = ExitStack()
            hh, hl = sb(f"hh{n}", [P, FT, T], ph, F32R), sb(f"hl{n}", [P, FT, T], ph, F32R)
            m_h, m_hid, gates = list(m_next), {}, {}

            def gate_evac(panel, ps, mark):
                a, freed_a = tmp.take()
                s_, freed_s = tmp.take()
                m1 = times_rms(a[:, :], ps, mark, freed_a)
                m2 = A.op(act.activation, s_[:, :], a[:, :], ACT.Sigmoid, after=[m1, freed_s])
                gates[panel] = (a, s_, m2)
                return (m1,)

            def up_evac(panel, ps, mark):
                b, freed_b = tmp.take()
                a, s_, m2 = gates[panel]
                m1 = times_rms(b[:, :], ps, mark, freed_b)
                m3 = V.op(vec.tensor_tensor, a[:, :], a[:, :], s_[:, :], ALU.mult, after=[m2])
                m4 = V.op(vec.tensor_tensor, a[:, :], a[:, :], b[:, :], ALU.mult, after=[m3, m1])
                m5 = A.op(act.activation, hh[:, panel, :], a[:, :], ACT.Copy, after=[m4])
                m_hid[panel] = G.op(pool.tensor_tensor, hl[:, panel, :], a[:, :], hh[:, panel, :].bitcast(F32),
                                    ALU.subtract, after=[m5])
                tmp.give(a, m_hid[panel])
                tmp.give(s_, m3)
                tmp.give(b, m4)
                return (m1,)

            for panel in range(FT):
                project(f"ffn{n}_gate", [panel], h2h, h2l, T, m_h, gate_evac,
                        hook=None if panel else (lambda: residual_stat(T)))
                project(f"ffn{n}_up", [panel], h2h, h2l, T, m_h, up_evac)
            m_in = PE.last()

            def down_evac(panel, ps, mark):
                m = V.op(vec.scalar_tensor_tensor, x2(panel), ps, 0.5, x2(panel), ALU.mult, ALU.add, after=[mark])
                residual_done(panel, 0, next_gain, m, m_in)
                return (m,)

            project(f"ffn{n}_down", list(range(KT)), lambda k: hh[:, k, :], lambda k: hl[:, k, :], T, m_hid,
                    down_evac, kt=FT)
            new_phase()
            ph.close()

        ffn(1, "mix")

        ph = ExitStack()
        m_h = list(m_next)
        iq = sb("iq", [P, 4, T], ph)
        ikm = sb("ikm", [P, 2, T], ph)
        iw = sb("iw", [P, 3, IDX_HEADS], ph)
        score = sb("score", [P, QW], ph)
        mask = sb("mask", [P, QW], ph)
        top8 = sb("top8", [P, 8], ph)
        rq = sb("rq", [P, 8, T], ph)
        rk = sb("rk", [P, 8, T], ph)
        rv = sb("rv", [P, 3, RET_HEADS * RET_DV], ph)
        rel = Ring([sb(f"rel{i}", [P, QW], ph) for i in range(2)])
        m_rope = [None]

        def mix_stat():
            residual_stat(T)
            six = tb[:, 0:6 * T].rearrange("p (a t) -> p a t", a=6)
            m_rope[0] = V.op(vec.tensor_tensor, six, six, rstd[:, :].unsqueeze(1).broadcast_to([P, 6, T]), ALU.mult,
                             after=[stat["x"], m_tb])

        def rope_halves(dst, cos, sin):
            def evac(ps, mark, m_free=None):
                a, freed_a = tmp.take()
                b, freed_b = tmp.take()
                m1 = V.op(vec.tensor_tensor, a[:, :], ps, cos, ALU.mult, after=[mark, freed_a, m_rope[0]])
                m2 = V.op(vec.tensor_tensor, b[0:64, :], ps[64:128, :], sin[0:64, :], ALU.mult, after=[freed_b])
                m2 = V.op(vec.tensor_tensor, b[64:128, :], ps[0:64, :], sin[64:128, :], ALU.mult)
                m3 = G.op(pool.tensor_tensor, dst, a[:, :], b[:, :], ALU.add, after=[m1, m2, m_free])
                tmp.give(a, m3)
                tmp.give(b, m3)
                return m2, m3
            return evac

        m_iq, m_ik = {}, None

        def iq_evac(panel, ps, mark):
            nonlocal m_ik
            if panel < 4:
                m2, m_iq[panel] = rope_halves(iq[:, panel, :], tabb("icos"), tabb("isin"))(ps, mark)
            elif panel == 4:
                m2, m3 = rope_halves(ikm[:, 0, :], tabb("icos"), tabb("isin"))(ps, mark)
                m4 = V.op(vec.tensor_copy, ikm[:, 1, :], ikm[:, 0, :], after=[m3])
                for v, r in ((0, 32), (0, 96), (1, 0), (1, 64)):
                    m_ik = V.op(vec.memset, ikm[r:r + 32, v, :], 0.0, after=[m4])
            else:
                t, freed_t = tmp.take()
                m2 = times_rms(t[:, :], ps, mark, freed_t)
                held_iw.append((t, m2))
            return (m2,)

        held_iw = []

        project("idx", list(range(6)), h2h, h2l, T, m_h, iq_evac, hook=mix_stat)
        t, m1 = held_iw[0]
        bank, freed = banks.take()
        for j, (q0, n, _) in enumerate(QT):
            m = PE.op(ten.transpose, bank[0:n, j * 8:j * 8 + 8], t[0:8, q0:q0 + n], ident[0:8, 0:8],
                      after=[m1, freed])
        tmp.give(t, m)
        m_iw = V.op(vec.tensor_scalar, iw[:, 0:2, :], bank[:, 0:16].rearrange("p (a b) -> p a b", a=2),
                    (IDX_DH ** -0.5) * (IDX_HEADS ** -0.5), None, ALU.mult, after=[m])
        m_iw = V.op(vec.tensor_scalar, iw[0:16, 2, :], bank[0:16, 16:24], (IDX_DH ** -0.5) * (IDX_HEADS ** -0.5),
                    None, ALU.mult)
        banks.give(bank, m_iw)

        m_score = m_tb
        for h in range(IDX_HEADS):
            ba, freed_a = banks.take()
            bb, freed_b = banks.take()
            r, freed_r = rel.take()
            for j, (q0, n, wd) in enumerate(QT):
                out = ba[:, QO[j]:QO[j] + wd] if j < 2 else bb[0:n, 0:wd]
                m = PE.op(ten.matmul, out, iq[:, h // 2, q0:q0 + n], ikm[:, h % 2, 0:wd], start=True, stop=True,
                          after=[m_iq[h // 2], m_ik, freed_a, freed_b])
            m1 = A.op(act.activation, r[:, 0:384], ba[:, 0:384], ACT.Relu, after=[m, freed_r])
            m2 = A.op(act.activation, r[0:16, 384:QW], bb[0:16, 0:T], ACT.Relu)
            banks.give(ba, m1)
            banks.give(bb, m2)
            prev = m_score
            for j, (q0, n, wd) in enumerate(QT):
                c = slice(QO[j], QO[j] + wd)
                src = (tabb("adm") if h == 0 else score)[0:n, c]
                m_score = V.op(vec.scalar_tensor_tensor, score[0:n, c], r[0:n, c], iw[0:n, j, h:h + 1], src,
                               ALU.mult, ALU.add, after=[m2, m_iw, prev])
            rel.give(r, m_score)

        m_mask = {}

        def top_k(j):
            q0, n, wd = QT[j]
            c = slice(QO[j], QO[j] + wd)
            s = score[0:n, c]
            m = m_score
            for _ in range(TOPK // 8):
                m1 = V.op(vec.max, top8[0:n, :], s, after=[m])
                m = V.op(vec.match_replace, s, top8[0:n, :], s, TAKEN, after=[m1])
            m1 = V.op(vec.tensor_scalar, mask[0:n, c], s, 0.7 * TAKEN, -BIG, ALU.is_gt, ALU.mult, after=[m])
            m2 = V.op(vec.tensor_tensor, mask[0:n, c], mask[0:n, c], tabb("adm")[0:n, c], ALU.add, after=[m1])
            m_mask[j] = V.op(vec.tensor_copy, mask[0:n, QO[j]:QO[j] + N_META],
                             tabb("meta")[0:n, N_META * j:N_META * (j + 1)], after=[m2])

        m_rq = {}
        held = {}

        def ret_rope(dst, kind):
            def evac(panel, ps, mark):
                h, half = (panel % 8) // 2, panel % 2
                x1_, mk1 = held["x1"]
                t = []
                for src, tabn, mk in ((x1_, "rcos", mk1), (ps, "rsin", mark), (ps, "rcos", mark), (x1_, "rsin", mk1)):
                    b, freed = tmp.take()
                    t.append((b, V.op(vec.tensor_tensor, b[:, :], src, tabb(tabn), ALU.mult, after=[mk, freed, m_rope[0]])))
                ma = G.op(pool.tensor_tensor, dst[:, 2 * h, :], t[0][0][:, :], t[1][0][:, :], ALU.subtract,
                          after=[t[1][1]])
                mb = G.op(pool.tensor_tensor, dst[:, 2 * h + 1, :], t[2][0][:, :], t[3][0][:, :], ALU.add,
                          after=[t[3][1]])
                for n, (b, _) in enumerate(t):
                    tmp.give(b, ma if n < 2 else mb)
                m_rq[kind, h] = mb
                held["give"].append(t[3][1])
                return (t[3][1],)
            return evac

        def project_pair(p0, evac):
            def hold(panel, ps, mark):
                held["x1"] = (ps, mark)

            project("ret", [p0], h2h, h2l, T, m_h, hold)
            held["give"] = []
            project("ret", [p0 + 1], h2h, h2l, T, m_h, evac)
            banks.give(kept.pop(), *held["give"])

        for h in range(RET_HEADS):
            project_pair(2 * h, ret_rope(rq, "q"))
        top_k(0)
        for h in range(RET_HEADS):
            project_pair(8 + 2 * h, ret_rope(rk, "k"))
        top_k(1)

        tiles2 = [(q0, n) for q0, n, _ in QT]
        m_rv = {}
        rv_evac, flush = token_major(tiles2, lambda panel: lambda j, n, rows:
                                     rv[0:rows, j:j + n, panel * P:(panel + 1) * P], lambda: rstd[:, :],
                                     lambda: stat["x"], m_rv, tmp)
        project("rv", list(range(16)), h2h, h2l, T, m_h, rv_evac)
        flush()
        top_k(2)

        yr = Ring([sb(f"yr{i}", [P, 4, T], ph) for i in range(2)])
        yh, yl = sb("yh", [P, 16, T], ph, F32R), sb("yl", [P, 16, T], ph, F32R)
        pr = Ring([sb(f"pr{i}", [P, KW], ph) for i in range(2)])
        m_yr = {}

        def ret_head(h):
            pb, freed_p = pr.take()
            bank, freed = banks.take()
            for j, (k0, n, _) in enumerate(QT):
                q0, nq = KQ[j]
                for d in range(2):
                    fn = PE.op if d else PE.quiet
                    m = fn(ten.matmul, bank[0:n, KO[j]:KO[j] + nq], rk[:, 2 * h + d, k0:k0 + n],
                           rq[:, 2 * h + d, q0:T], start=(d == 0), stop=(d == 1),
                           after=[m_rq["q", h], m_rq["k", h], freed])
            dec = tabb("decay")[:, h * KW:(h + 1) * KW]
            V.op(vec.tensor_tensor, pb[:, 0:416], bank[:, 0:416], dec[:, 0:416], ALU.mult, after=[m, freed_p])
            m1 = V.op(vec.tensor_tensor, pb[0:16, 416:KW], bank[0:16, 416:KW], dec[0:16, 416:KW], ALU.mult)
            banks.give(bank, m1)
            yield
            yb, freed_y = yr.take()
            m_sq, outs = [], []
            for e in range(4):
                ob, freed = banks.take()
                c = slice(h * RET_DV + e * P, h * RET_DV + (e + 1) * P)
                for j, (k0, n, _) in enumerate(QT):
                    q0, nq = KQ[j]
                    fn = PE.op if j == 2 else PE.quiet
                    m2 = fn(ten.matmul, ob[:, q0:T], rv[0:n, j, c], pb[0:n, KO[j]:KO[j] + nq], start=(j == 0),
                            stop=(j == 2), after=[m1, m_rv[4 * h + e], freed])
                t, freed_t = tmp.take()
                m_sq.append(A.op(act.activation, t[:, :], ob[:, 0:T], ACT.Square, after=[m2, freed_t]))
                m_c = V.op(vec.tensor_copy, yb[:, e, :], ob[:, 0:T], after=[m_sq[-1], freed_y])
                banks.give(ob, m_sq[-1], m_c)
                outs.append((t, m_c))
            pr.give(pb, m2)
            yield
            r, freed_r = tmp.take()
            m3 = norm_stat(lambda k: outs[k][0][:, :], 4, T, "ones512", EPS, m_sq, r[:, :], freed_r)
            for e in range(4):
                tmp.give(outs[e][0], m3)
                m_yr[4 * h + e] = V.op(vec.tensor_tensor, yb[:, e, :], yb[:, e, :], r[:, :], ALU.mult,
                                       after=[m3, outs[e][1]])
            tmp.give(r, m_yr[4 * h + 3])

            def rg_evac(panel, ps, mark):
                a, freed_a = tmp.take()
                s_, freed_s = tmp.take()
                m1 = times_rms(a[:, :], ps, mark, freed_a)
                m2 = A.op(act.activation, s_[:, :], a[:, :], ACT.Sigmoid, after=[m1, freed_s])
                m4 = V.op(vec.tensor_tensor, a[:, :], a[:, :], yb[:, panel % 4, :], ALU.mult, after=[m2, m_yr[panel]])
                m5 = V.op(vec.tensor_tensor, a[:, :], a[:, :], s_[:, :], ALU.mult, after=[m4])
                m_yg[panel] = split_input(panel, a[:, :], 1.0, m5, yh[:, panel, :], yl[:, panel, :], None)
                tmp.give(a, m_yg[panel])
                tmp.give(s_, m5)
                return (m1,)

            project("rg", list(range(4 * h, 4 * h + 4)), h2h, h2l, T, m_h, rg_evac)
            yr.give(yb, m_yg[4 * h + 3])
            yield

        m_yg = {}
        skewed(ret_head(h) for h in range(RET_HEADS))
        m_ret = PE.last()

        G.wait(m_ret)
        V.wait(m_ret)
        A.wait(m_ret)
        aq, ak = rq, rk
        m_aqk = {}

        def aqk_evac(panel, ps, mark):
            dst = (aq if panel < 8 else ak)[:, panel % 8, :]
            m2, m_aqk[panel] = rope_halves(dst, tabb("acos"), tabb("asin"))(ps, mark)
            return (m2,)

        project("aqk", list(range(16)), h2h, h2l, T, m_h, aqk_evac)
        rv_flat = rv[:, :, :].rearrange("p a b -> p (a b)")
        avt = rv_flat[:, 0:3 * ATT_HEADS * P].rearrange("p (t n) -> p t n", t=3)
        m_av = {}
        av_evac, flush = token_major(tiles2, lambda panel: lambda j, n, rows:
                                     avt[0:rows, j:j + n, panel * P:(panel + 1) * P], lambda: rstd[:, :],
                                     lambda: stat["x"], m_av, tmp)
        project("av", list(range(8)), h2h, h2l, T, m_h, av_evac)
        flush()

        merged = rv_flat[:, 3 * ATT_HEADS * P:3 * ATT_HEADS * P + KT * T].rearrange("p (k t) -> p k t", k=KT)
        gatt = sqr
        m_gr, m_ga, m_mg = {}, {}, {}

        def gate2_evac(panel, ps, mark):
            dst = (merged if panel < 8 else gatt)[:, panel % 8, :]
            m1 = times_rms(dst, ps, mark)
            (m_gr if panel < 8 else m_ga)[panel % 8] = A.op(act.activation, dst, dst, ACT.Sigmoid, after=[m1])
            return (m1,)

        def ret_out_evac(panel, ps, mark):
            m_mg[panel] = V.op(vec.tensor_tensor, merged[:, panel, :], merged[:, panel, :], ps, ALU.mult,
                               after=[mark, m_gr[panel]])
            return (m_mg[panel],)

        project("g2", list(range(16)), h2h, h2l, T, m_h, gate2_evac)
        m_in = PE.last()

        pbs, pts = rel, pr
        sts = Ring([sb(f"sts{i}", [P, 12], ph) for i in range(3)])
        m_ya = {}
        scale = 128 ** -0.5

        def att_head(h):
            pb, freed_p = pbs.take()
            st, freed_st = sts.take()
            ba, freed_a = banks.take()
            bb, freed_b = banks.take()
            for j, (q0, n, wd) in enumerate(QT):
                out = ba[:, QO[j]:QO[j] + wd] if j < 2 else bb[0:n, 0:wd]
                m = PE.op(ten.matmul, out, aq[:, h, q0:q0 + n], ak[:, h, 0:wd], start=True, stop=True,
                          after=[m_aqk[h], m_aqk[8 + h], freed_a, freed_b])
            m1 = V.op(vec.scalar_tensor_tensor, pb[:, 0:384], ba[:, 0:384], scale, mask[:, 0:384], ALU.mult, ALU.add,
                      after=[m, m_mask[0], m_mask[1], m_mask[2], freed_p, freed_st])
            m1 = V.op(vec.scalar_tensor_tensor, pb[0:16, 384:QW], bb[0:16, 0:T], scale, mask[0:16, 384:QW], ALU.mult,
                      ALU.add)
            banks.give(ba, m1)
            banks.give(bb, m1)
            for j, (q0, n, wd) in enumerate(QT):
                m2 = V.op(vec.tensor_reduce, st[0:n, j:j + 1], pb[0:n, QO[j]:QO[j] + wd], AX_X, ALU.max, after=[m1])
            m3 = V.op(vec.tensor_scalar, st[:, 3:5], st[:, 0:2], -1.0, None, ALU.mult, after=[m2])
            m3 = V.op(vec.tensor_scalar, st[0:16, 5:6], st[0:16, 2:3], -1.0, None, ALU.mult)
            for j, (q0, n, wd) in enumerate(QT):
                c = slice(QO[j], QO[j] + wd)
                m4 = A.op(act.activation, pb[0:n, c], pb[0:n, c], ACT.Exp, bias=st[0:n, 3 + j:4 + j],
                          accum_out=st[0:n, 6 + j:7 + j], after=[m3])
            m5 = V.op(vec.reciprocal, st[:, 9:11], st[:, 6:8], after=[m4])
            m5 = V.op(vec.reciprocal, st[0:16, 11:12], st[0:16, 8:9])
            for j, (q0, n, wd) in enumerate(QT):
                c = slice(QO[j], QO[j] + wd)
                m6 = V.op(vec.tensor_scalar, pb[0:n, c], pb[0:n, c], st[0:n, 9 + j:10 + j], None, ALU.mult,
                          after=[m5])
            sts.give(st, m6)
            yield
            pt, freed_pt = pts.take()
            bank, freed = banks.take()
            for k in range(3):
                nk = QT[k][1]
                for j in range(k, 3):
                    q0, n, _ = QT[j]
                    at = KO[k] + q0 - KQ[k][0]
                    m7 = PE.op(ten.transpose, bank[0:nk, at:at + n], pb[0:n, QO[j] + P * k:QO[j] + P * k + nk],
                               ident[0:n, 0:n], after=[m6, freed])
            A.op(act.activation, pt[:, 0:416], bank[:, 0:416], ACT.Copy, after=[m7, freed_pt])
            m8 = A.op(act.activation, pt[0:16, 416:KW], bank[0:16, 416:KW], ACT.Copy)
            banks.give(bank, m8)
            pbs.give(pb, m7)
            yield
            ob, freed = banks.take()
            for k in range(3):
                nk = QT[k][1]
                q0, nq = KQ[k]
                fn = PE.op if k == 2 else PE.quiet
                m9 = fn(ten.matmul, ob[:, q0:T], avt[0:nk, k, h * P:(h + 1) * P], pt[0:nk, KO[k]:KO[k] + nq],
                        start=(k == 0), stop=(k == 2), after=[m8, m_av[h], freed])
            pts.give(pt, m9)
            m_ya[h] = split_input(h, ob[:, 0:T], 1.0, m9, h2h(h), h2l(h), m_in)
            banks.give(ob, m_ya[h])
            yield

        m_yg_all = [m_yg[k] for k in range(16)]
        heads = [att_head(h) for h in range(ATT_HEADS)]
        live = []
        for step in range(ATT_HEADS + 3):
            if step < ATT_HEADS:
                live.append(heads[step])
            for g in list(live):
                try:
                    next(g)
                except StopIteration:
                    live.remove(g)
            if step < KT:
                project("ret_out", [step], lambda k: yh[:, k, :], lambda k: yl[:, k, :], T, m_yg_all, ret_out_evac,
                        kt=16)
        m_ro = PE.last()

        def att_out_evac(panel, ps, mark):
            m1 = V.op(vec.tensor_tensor, gatt[:, panel, :], gatt[:, panel, :], ps, ALU.mult,
                      after=[mark, m_ga[panel]])
            m2 = V.op(vec.tensor_tensor, merged[:, panel, :], merged[:, panel, :], gatt[:, panel, :],
                      ALU.add, after=[m1, m_mg[panel]])
            m_mg[panel] = split_input(panel, merged[:, panel, :], 1.0, m2, yh[:, panel, :], yl[:, panel, :], m_ro)
            return (m1,)

        project("att_out", list(range(KT)), h2h, h2l, T, m_ya, att_out_evac)
        m_ao = PE.last()

        def mix_evac(panel, ps, mark):
            m = V.op(vec.tensor_tensor, x2(panel), x2(panel), ps, ALU.add, after=[mark])
            residual_done(panel, 0, "ffn2", m, [m_ao, m_mg[panel]])
            return (m,)

        project("mix_out", list(range(KT)), lambda k: yh[:, k, :], lambda k: yl[:, k, :], T, m_mg, mix_evac)
        new_phase()
        ph.close()

        ffn(2, None)
        residual_stat(T)
        s_out = sem("s_out")
        for k in range(KT):
            m = V.op(vec.scalar_tensor_tensor, x2(k), x2(k), col("final", k), rstd[:, :], ALU.mult, ALU.mult,
                     after=[stat["x"]])
            SP.dma(outT[:, k, :], res[:, k, N_META:T], s_out, 16 * (k + 1), after=[m])
        SP.wait((s_out, 16 * KT))
        second.close()

        block = ctx.enter_context(nc.Block())

        @block.sync
        def _(e):
            SP.emit()

        @block.gpsimd
        def _(e):
            G.emit()

        @block.scalar
        def _(e):
            A.emit()

        @block.vector
        def _(e):
            V.emit()

        @block.tensor
        def _(e):
            PE.emit()


def kernel(**inputs):
    import concourse.bacc as _bacc
    from concourse import mybir as _mybir
    from concourse.bass_utils import run_bass_kernel_spmd as _run

    I = {k: np.asarray(v) for k, v in inputs.items()}
    nc = _bacc.Bacc("TRN2", target_bir_lowering=False, num_devices=1)
    arrays = {}

    def dram(name, a):
        a = np.ascontiguousarray(a)
        arrays[name] = a
        return nc.dram_tensor(name, a.shape, _mybir.dt.from_np(a.dtype), kind="ExternalInput").ap()

    def feature_major(a):
        return a.T.reshape(-1, P, a.shape[0]).transpose(1, 0, 2)

    def panels(wt):
        k, n = wt.shape
        return wt.reshape(k // P, P, n // P, P).transpose(2, 1, 0, 3).reshape(n // P, P, k)

    vec = {"pre0": I["pre_norm"][0], "pre1": I["pre_norm"][1], "post0": I["post_norm"][0], "post1": I["post_norm"][1],
           "memn0": I["mem_norm"][0], "memn1": I["mem_norm"][1], "kvn": I["kv_norm"], "mu": I["a_shift_mu"][0],
           "w0": I["a_w0"][0], "a0": I["a_a0"][0], "kk": I["a_k_k"][0], "ka": I["a_k_a"][0],
           "rk": I["a_r_k"][0].reshape(-1), "lnw": I["a_lnx_w"][0], "lnb": I["a_lnx_b"][0], "subln": I["b_subln"][0],
           "ffn1": I["ffn1_norm_2"][0], "mix": I["mix_norm_2"][0], "ffn2": I["ffn2_norm_2"][0],
           "final": I["final_norm_2"]}
    cols = np.zeros((P, NCOL), np.float32)
    for name, n in VECTORS:
        if name == "lam":
            for j, key in enumerate(("b_lam_q1", "b_lam_q2", "b_lam_k1", "b_lam_k2")):
                cols[:HD, COL[name] + j] = I[key][0]
        else:
            cols[:, COL[name]:COL[name] + n] = vec[name].reshape(n, P).T
    ta, tr, tb = const_tables()

    win = I["w_in_2"][0]
    o = np.cumsum([0, 1024, 1024, 2048, 2048, 1024, 1024, 1024, 512, 64, 8, 1024, 1024])
    idx = []
    for j in range(4):
        for half in range(2):
            for h in (2 * j, 2 * j + 1):
                idx += list(range(o[7] + 64 * h + 32 * half, o[7] + 64 * h + 32 * half + 32))
    for half in (0, 0, 1, 1):
        idx += list(range(o[8] + 32 * half, o[8] + 32 * half + 32))
    w_idx = np.concatenate([win[:, idx], win[:, o[9]:o[10]], np.zeros((D, P - IDX_HEADS), win.dtype)], 1)
    w = {
        "a_w_in": panels(I["a_w_in"][0]), "w_mem0": panels(I["w_mem_kv"][0]), "w_mem1": panels(I["w_mem_kv"][1]),
        "w_out0": panels(I["w_out"][0]), "w_out1": panels(I["w_out"][1]), "w_kv": panels(I["w_kv"]),
        "b_w_in": panels(I["b_w_in"][0]),
        "ffn1_gate": panels(I["ffn1_w_gate_2"][0]), "ffn1_up": panels(I["ffn1_w_up_2"][0]),
        "ffn1_down": panels(I["ffn1_w_down_2"][0]), "ffn2_gate": panels(I["ffn2_w_gate_2"][0]),
        "ffn2_up": panels(I["ffn2_w_up_2"][0]), "ffn2_down": panels(I["ffn2_w_down_2"][0]),
        "idx": panels(w_idx), "ret": panels(win[:, o[0]:o[2]]), "rv": panels(win[:, o[2]:o[3]]),
        "rg": panels(win[:, o[3]:o[4]]), "aqk": panels(win[:, o[4]:o[6]]), "av": panels(win[:, o[6]:o[7]]),
        "g2": panels(win[:, o[10]:o[12]]),
        "ret_out": panels(I["w_ret_out_2"][0]), "att_out": panels(I["w_att_out_2"][0]),
        "mix_out": panels(I["w_mix_out_2"][0]),
    }
    args = [dram("xT", feature_major(I["x"][0])), dram("memT", feature_major(I["mem"][0])),
            dram("metaT", feature_major(I["meta_tokens_2"])), dram("vecs", cols), dram("tab_a", ta),
            dram("tab_r", tr), dram("tab_b", tb),
            dram("lora", np.concatenate([I["a_w2"][0], I["a_a2"][0]], 0)),
            {k: dram("w_" + k, v) for k, v in w.items()}]
    out = nc.dram_tensor("outT", (P, KT, S), _mybir.dt.float32, kind="ExternalOutput").ap()
    build(nc, *args, out)
    r = _run(nc, [arrays], core_ids=[0])
    got = r.results[0]["outT"]
    return got.transpose(2, 1, 0).reshape(1, S, D)
```

```python
import math
from contextlib import ExitStack

import numpy as np
import concourse.bass as bass
from concourse import mybir

P = 128
D = 1024
KT = D // P
S = 256
N_META = 16
T = S + N_META
MEM = 256
BR = 768
BT = BR // P
HD = 64
MW = 256
MT = MW // P
MEM_HEADS = 4
Z_TILES = (3 * BR + 128) // P
LAM_INIT = 0.8 - 0.6 * math.exp(-0.3)
RET_HEADS, RET_DV = 4, 512
ATT_HEADS = 8
IDX_HEADS, IDX_DH = 8, 64
TOPK = min(256, S // 4)
FF = 2816
FT = FF // P
EPS = 1e-6
LNX_EPS = 64e-5
CH = 128
DECAY_C = math.exp(-0.5)
MID = DECAY_C * CH / 2
BIG = 1e30
TAKEN = -3e38
QT = [(0, 128, 128), (128, 128, 256), (256, 16, 272)]
QO = [0, 128, 384]
QW = 656
KO = [0, 272, 416]
KQ = [(0, 272), (128, 144), (256, 16)]
KW = 432

F32 = mybir.dt.float32
F32R = mybir.dt.float32r
ALU = mybir.AluOpType
ACT = mybir.ActivationFunctionType
AX_X = mybir.AxisListType.X

N_RAW, N_SPLIT = 4, 3
N_EXTRA = 4
WC = 8 * P


LAYER0_BETWEEN = [("a_w_in", p) for p in [8, 9, 10, 11] + list(range(6))] + [("w_mem1", p) for p in range(4)] \
    + [("a_w_in", p) for p in list(range(12, 18)) + list(range(19, 29))]
LAYER1_BETWEEN = [pair for h in range(1, BT) for pair in (("b_w_in", h), ("w_kv", h), ("w_kv", BT + h - 1))] \
    + [("w_kv", 2 * BT - 1)] + [("b_w_in", p) for p in list(range(12, 16)) + list(range(6, 12))]


def weight_order():
    order = [("w_mem0", p, KT) for p in range(4)] + [("a_w_in", p, KT) for p in [18, 6, 7]]
    order += [(name, p, KT) for name, p in LAYER0_BETWEEN] + [("w_out0", p, KT) for p in range(KT)]
    order += [("b_w_in", 0, KT), ("w_kv", 0, KT)]
    order += [(name, p, KT) for name, p in LAYER1_BETWEEN] + [("w_out1", p, KT) for p in range(KT)]
    ffn = lambda n: [(f"ffn{n}_{g}", p, KT) for p in range(FT) for g in ("gate", "up")] \
        + [(f"ffn{n}_down", p, FT) for p in range(KT)]
    order += ffn(1)
    order += [("idx", p, KT) for p in range(6)] + [("ret", p, KT) for p in range(16)]
    order += [("rv", p, KT) for p in range(16)] + [("rg", p, KT) for p in range(16)]
    order += [("aqk", p, KT) for p in range(16)] + [("av", p, KT) for p in range(8)]
    order += [("g2", p, KT) for p in range(16)] + [("ret_out", p, 16) for p in range(KT)]
    order += [("att_out", p, KT) for p in range(KT)] + [("mix_out", p, KT) for p in range(KT)]
    return order + ffn(2)


def chunks_of(kt):
    n = -(-kt // 8)
    cuts = [-(-kt * i // n) for i in range(n + 1)]
    return [(a, b - a) for a, b in zip(cuts, cuts[1:])]


VECTORS = [("pre0", 8), ("pre1", 8), ("post0", 8), ("post1", 8), ("memn0", 8), ("memn1", 8), ("kvn", 8),
           ("mu", Z_TILES), ("w0", BT), ("a0", BT), ("kk", BT), ("ka", BT), ("rk", BT), ("lnw", BT), ("lnb", BT),
           ("subln", 1), ("lam", 4), ("ffn1", 8), ("mix", 8), ("ffn2", 8), ("final", 8)]
COL, NCOL = {}, 0
for _name, _n in VECTORS:
    COL[_name] = NCOL
    NCOL += _n

TABLES_A = [("ident", P), ("ones_d", P), ("blk", P), ("blkm", P), ("ones", P), ("ones128", P), ("ones512", P),
            ("dist", 384), ("mid", 2)]
TABLES_R = [("neg_up", P), ("neg_m0", P), ("m0t", P)] + [(f"m{j}", P) for j in range(1, 7)] + [("up", P), ("upinc", P)]
TABLES_B = [("rcos", T), ("rsin", T), ("acos", T), ("asin", T), ("icos", T), ("isin", T), ("decay", RET_HEADS * KW),
            ("adm", QW), ("meta", 3 * N_META)]


def offsets(tables):
    at, out = 0, {}
    for name, n in tables:
        out[name] = (at, n)
        at += n
    return out, at


OFF_A, W_A = offsets(TABLES_A)
OFF_R, W_R = offsets(TABLES_R)
OFF_B, W_B = offsets(TABLES_B)


def alibi_slopes(n):
    c = 2 ** int(math.floor(math.log2(n)))

    def pow2(m):
        start = 2.0 ** (-8.0 / m)
        return [start ** (i + 1) for i in range(m)]
    s = pow2(n) if c == n else pow2(c) + pow2(2 * c)[0::2][: n - c]
    return [float(np.float32(x)) for x in s]


def rope_tables(d):
    inv = (np.float32(10000.0) ** (-np.arange(0, d, 2, dtype=np.float32) / np.float32(d))).astype(np.float32)
    ang = (np.arange(T, dtype=np.float32)[None, :] * inv[:, None]).astype(np.float32)
    return np.cos(ang).astype(np.float32), np.sin(ang).astype(np.float32)


def const_tables():
    i = np.arange(P)
    r, c = i[:, None], i[None, :]
    a = {"ident": r == c, "ones_d": np.full((P, P), 1.0 / D), "blk": (r // HD == c // HD) * 1.0,
         "blkm": (r // HD == c // HD) / HD, "ones": np.ones((P, P)), "ones128": np.full((P, P), 1.0 / P),
         "ones512": np.full((P, P), 1.0 / RET_DV), "mid": np.array([[MID, -MID]] * P)}
    t = np.concatenate([r, 128 + r, 128 + r], 1)
    key = np.arange(384)[None, :]
    key = np.where(key < 128, key, key - 128)
    tok = np.where(np.arange(384)[None, :] < 128, t[:, :1], t[:, 1:2])
    a["dist"] = np.where(key // 64 <= tok // 64, np.abs(tok - key), BIG)
    m = {"neg_up": (c > r) * -1.0, "up": (c > r) * 1.0, "upinc": (c >= r) * 1.0}
    for j in range(7):
        n = 1 << j
        m[f"m{j}"] = ((r // (2 * n) == c // (2 * n)) & (r // n > c // n)) * 1.0
    m["neg_m0"], m["m0t"] = -m["m0"], m["m0"].T
    b = {}
    b["rcos"], b["rsin"] = rope_tables(256)
    co, si = rope_tables(128)
    b["acos"], b["asin"] = np.concatenate([co, co]), np.concatenate([-si, si])
    co, si = rope_tables(64)
    b["icos"], b["isin"] = np.concatenate([co] * 4), np.concatenate([-si, -si, si, si])
    dec = np.zeros((P, RET_HEADS, KW))
    for h in range(RET_HEADS):
        g = np.log1p(-(2.0 ** (-5.0 - h)))
        for j, (q0, n) in enumerate(KQ):
            diff = (q0 + np.arange(n))[None, :] - (P * j + i)[:, None]
            dec[:, h, KO[j]:KO[j] + n] = np.where(diff >= 0, np.exp(g * np.maximum(diff, 0)), 0.0) / 16.0
    b["decay"] = dec.reshape(P, -1)
    adm, meta = np.full((P, QW), -BIG), np.full((P, 3 * N_META), -BIG)
    for j, (q0, n, w) in enumerate(QT):
        q, k = q0 + i[:, None], np.arange(w)[None, :]
        adm[:, QO[j]:QO[j] + w] = np.where((k >= N_META) & (k <= q), 0.0, -BIG)
        k = np.arange(N_META)[None, :]
        meta[:, N_META * j:N_META * (j + 1)] = np.where(k <= q, 0.0, -BIG)
    b["adm"], b["meta"] = adm, meta
    pack = lambda tables, src: np.ascontiguousarray(
        np.concatenate([np.asarray(src[n], np.float32) for n, _ in tables], 1))
    return pack(TABLES_A, a), pack(TABLES_R, m), pack(TABLES_B, b)


class Queue:

    def __init__(self, engine, sem):
        self.engine, self.sem, self.count, self.items, self.met = engine, sem, 0, [], {}

    def wait(self, *marks):
        for mark in marks:
            if mark is None:
                continue
            if isinstance(mark, list):
                self.wait(*mark)
                continue
            sem, value = mark
            if self.met.get(sem, 0) < value:
                self.met[sem] = value
                self.items.append((self.engine.wait_ge, (sem, value), {}, None, 0))

    def op(self, fn, *args, after=(), **kw):
        self.wait(*after)
        self.count += 1
        self.items.append((fn, args, kw, self.sem, 1))
        return (self.sem, self.count)

    def quiet(self, fn, *args, after=(), **kw):
        self.wait(*after)
        self.items.append((fn, args, kw, None, 0))

    def dma(self, out, in_, sem, value, after=()):
        self.wait(*after)
        self.items.append((self.engine.dma_start, (out, in_), {}, sem, 16))
        return (sem, value)

    def last(self):
        return (self.sem, self.count) if self.count else None

    def emit(self):
        for fn, args, kw, sem, inc in self.items:
            ins = fn(*args, **kw)
            if sem is not None:
                ins.then_inc(sem, inc)


class ScalarQueue(Queue):
    SETS = {ACT.Exp: "natural_log_exp_and_others", ACT.Ln: "natural_log_exp_and_others",
            ACT.Sigmoid: "sigmoid_and_others", ACT.Tanh: "sigmoid_and_others"}
    loaded = None

    def op(self, fn, *args, after=(), **kw):
        wanted = self.SETS.get(args[2]) if len(args) > 2 else None
        if wanted is not None and wanted != self.loaded:
            self.items.append((self.engine.preload_act_table_set, (wanted,), {}, None, 0))
            self.loaded = wanted
        return super().op(fn, *args, after=after, **kw)


class Ring:

    def __init__(self, bufs):
        self.free = [(b, []) for b in bufs]

    def take(self):
        return self.free.pop(0)

    def give(self, buf, *marks):
        self.free.append((buf, list(marks)))


def skewed(streams):
    live, streams = [], list(streams)
    while live or streams:
        if streams:
            live.append(streams.pop(0))
        for g in list(live):
            try:
                next(g)
            except StopIteration:
                live.remove(g)


def build(nc, xT, memT, metaT, vecs, tab_a, tab_r, tab_b, lora, w, outT):
    with ExitStack() as ctx:
        def sem(name):
            return ctx.enter_context(nc.semaphore(name))

        def sb(name, shape, scope=ctx, dt=F32):
            return scope.enter_context(nc.sbuf_tensor(name, shape, dt))

        V = Queue(nc.vector, sem("s_vector"))
        A = ScalarQueue(nc.scalar, sem("s_scalar"))
        PE = Queue(nc.tensor, sem("s_tensor"))
        G = Queue(nc.gpsimd, sem("s_pool"))
        SP = Queue(nc.sync, sem("s_sync"))
        vec, act, ten, pool = nc.vector, nc.scalar, nc.tensor, nc.gpsimd

        banks = Ring([ctx.enter_context(nc.psum_tensor(f"bank{i}", [P, 512], F32)) for i in range(8)])

        res = sb("res", [P, KT, T])
        xh, xl = sb("xh", [P, KT, T], dt=F32R), sb("xl", [P, KT, T], dt=F32R)
        cols = sb("cols", [P, NCOL])
        ta = sb("ta", [P, W_A])
        rstd = sb("rstd", [P, T])
        sqr = sb("sqr", [P, KT, T])

        def tab(name):
            o, n = OFF_A[name]
            return ta[:, o:o + n]

        ident = tab("ident")

        def col(name, i=0):
            return cols[:, COL[name] + i:COL[name] + i + 1]

        s_in = [sem(f"s_in{i}") for i in range(5)]
        m_cols = A.dma(cols[:, :], vecs, s_in[2], 16)

        raws = [(sb(f"raw{i}", [P, WC]), sem(f"s_raw{i}")) for i in range(N_RAW)]
        splits = Ring([(sb(f"wh{i}", [P, WC], dt=F32R), sb(f"wl{i}", [P, WC], dt=F32R)) for i in range(N_SPLIT)])
        extra, depth = [], [N_SPLIT]
        stream = [(name, p, k0, nk) for name, p, kt in weight_order() for k0, nk in chunks_of(kt)]
        loads, his, ready = [], [], []
        raw_freed = [[] for _ in range(N_RAW)]

        def load_next():
            n = len(loads)
            if n < len(stream):
                name, p, k0, nk = stream[n]
                buf, s = raws[n % N_RAW]
                loads.append(SP.dma(buf[:, 0:nk * P], w[name][p][:, k0 * P:(k0 + nk) * P], s,
                                    16 * (n // N_RAW + 1), after=raw_freed[n % N_RAW]))

        def split_hi():
            n = len(his)
            if n < len(stream):
                nk = stream[n][3]
                buf, freed = splits.take()
                his.append((buf, A.op(act.activation, buf[0][:, 0:nk * P], raws[n % N_RAW][0][:, 0:nk * P], ACT.Copy,
                                      after=[loads[n], freed])))

        def split_lo():
            n = len(ready)
            if n < len(stream):
                nk = stream[n][3]
                (hi, lo), m_hi = his[n]
                m_lo = V.op(vec.tensor_tensor, lo[:, 0:nk * P], raws[n % N_RAW][0][:, 0:nk * P],
                            hi[:, 0:nk * P].bitcast(F32), ALU.subtract, after=[m_hi])
                ready.append(((hi, lo), m_hi, m_lo))
                raw_freed[n % N_RAW] = [m_hi, m_lo]
                load_next()

        used = [0]

        def next_weights(name, panel, k0):
            n = used[0]
            assert stream[n][0:3] == (name, panel, k0), (stream[n], name, panel, k0)
            used[0] += 1
            lag = 1 if depth[0] > N_SPLIT else 0
            while len(ready) < min(n + depth[0] - lag, len(stream)):
                while len(his) < min(len(ready) + 1 + lag, n + depth[0], len(stream)):
                    split_hi()
                split_lo()
            if len(his) < n + depth[0]:
                split_hi()
            return ready[n]

        def more_splits(bufs):
            extra.extend(bufs)
            depth[0] += len(bufs)
            for b in bufs:
                splits.give(b)

        def fewer_splits():
            splits.free = [f for f in splits.free if f[0] not in extra]
            depth[0] = N_SPLIT

        def give_split(buf, mark):
            if buf in extra and depth[0] == N_SPLIT:
                extra.remove(buf)
            else:
                splits.give(buf, mark)

        for _ in range(N_RAW):
            load_next()

        def split_input(k, src, gain, m_src, hi, lo, m_free):
            return split_inputs([(k, src, gain, m_src, hi, lo, m_free)])[0]

        def split_inputs(tiles):
            m_his = [A.op(act.activation, hi, src, ACT.Copy, scale=gain, after=[m_src, m_cols, m_free])
                     for _, src, gain, m_src, hi, lo, m_free in tiles]
            marks = []
            for (_, src, gain, m_src, hi, lo, m_free), m_hi in zip(tiles, m_his):
                if isinstance(gain, float):
                    marks.append(V.op(vec.tensor_tensor, lo, src, hi.bitcast(F32), ALU.subtract,
                                      after=[m_hi, m_free]))
                else:
                    marks.append(V.op(vec.scalar_tensor_tensor, lo, src, gain, hi.bitcast(F32), ALU.mult,
                                      ALU.subtract, after=[m_hi, m_free]))
            return marks

        kept = []
        late = []

        def settle():
            while late:
                evac, panel, ps, bank, mark = late.pop(0)
                marks = evac(panel, ps, mark)
                if marks is None:
                    kept.append(bank)
                else:
                    banks.give(bank, *marks)

        def project(name, panels, x_hi, x_lo, n_tok, x_marks, evac, kt=KT, hook=None, keep=False):
            for panel in panels:
                bank, freed = banks.take()
                ps = bank[:, 0:n_tok]
                for k0, nk in chunks_of(kt):
                    (hi, lo), m_hi, m_lo = next_weights(name, panel, k0)
                    for k in range(nk):
                        kk, c = k0 + k, slice(k * P, (k + 1) * P)
                        m_x = x_marks[kk] if isinstance(x_marks, (list, dict)) and len(x_marks) == kt else x_marks
                        PE.quiet(ten.matmul, ps, hi[:, c], x_hi(kk), start=(kk == 0), stop=False,
                                 after=[m_hi, m_x, freed])
                        PE.quiet(ten.matmul, ps, hi[:, c], x_lo(kk), start=False, stop=False, after=[m_x])
                        fn = PE.op if k == nk - 1 else PE.quiet
                        mark = fn(ten.matmul, ps, lo[:, c], x_hi(kk), start=False, stop=(kk == kt - 1),
                                  after=[m_lo])
                    give_split((hi, lo), mark)
                if hook is not None:
                    hook()
                    hook = None
                settle()
                late.append((evac, panel, ps, bank, mark))
            if not keep:
                settle()

        between = []

        def fill(n=1):
            for _ in range(n):
                if between:
                    name, panel = between.pop(0)
                    x_hi, x_lo, n_tok, marks, evac = jobs[name](panel)
                    project(name, [panel], x_hi, x_lo, n_tok, marks, evac, keep=True)

        def need(name, panel):
            while (name, panel) in between:
                fill()
            settle()

        def norm_stat(sq_tile, n, n_tok, table, eps, m_sq, out, freed_out=None):
            bank, freed = banks.take()
            for k in range(n):
                fn = PE.op if k == n - 1 else PE.quiet
                mark = fn(ten.matmul, bank[:, 0:n_tok], tab(table), sq_tile(k), start=(k == 0), stop=(k == n - 1),
                          after=[m_ta, m_sq[k] if isinstance(m_sq, list) else m_sq, freed])
            m = rsqrt(out, bank[:, 0:n_tok], eps, ALU.add, [mark, freed_out])
            banks.give(bank, m)
            return m

        def turn(src, tiles, dst, m_src, after_dst):
            bank, freed = banks.take()
            for j, (q0, n) in enumerate(tiles):
                m = PE.op(ten.transpose, bank[0:n, j * P:(j + 1) * P], src[:, q0:q0 + n], ident,
                          after=[m_src, freed])
            full = [t for t in tiles if t[1] == P]
            m1 = A.op(act.activation, dst(0, len(full), P),
                      bank[:, 0:len(full) * P].rearrange("p (a b) -> p a b", a=len(full)), ACT.Copy,
                      after=[m, after_dst])
            if len(full) < len(tiles):
                n = tiles[-1][1]
                m1 = A.op(act.activation, dst(len(full), 1, n), bank[0:n, len(full) * P:(len(full) + 1) * P],
                          ACT.Copy)
            banks.give(bank, m1)
            return m, m1

        def rsqrt(out, x, eps, op, marks):
            m = V.op(vec.tensor_scalar, out, x, eps, None, op, after=marks)
            m = A.op(act.activation, out, out, ACT.Ln, after=[m])
            return A.op(act.activation, out, out, ACT.Exp, scale=-0.5, after=[m])

        def square(k, dst, src, marks):
            if k % 2:
                return V.op(vec.tensor_tensor, dst, src, src, ALU.mult, after=marks)
            return A.op(act.activation, dst, src, ACT.Square, after=marks)

        m_next, m_nsq, stat = [None] * KT, [None] * KT, {}

        def residual_done(k, lo, gain, m_src, m_free):
            x = res[:, k, lo:T]
            if gain is not None:
                m_next[k] = split_input(k, x, col(gain, k), m_src, xh[:, k, 0:T - lo], xl[:, k, 0:T - lo], m_free)
            m_nsq[k] = square(k, sqr[:, k, 0:T - lo], x, [m_src])

        def residual_stat(n_tok):
            stat["x"] = norm_stat(lambda k: sqr[:, k, 0:n_tok], KT, n_tok, "ones_d", EPS, m_nsq, rstd[:, 0:n_tok])

        def everyone():
            return [q.last() for q in (V, A, PE, G, SP)]

        def new_phase():
            marks = everyone()
            for q in (V, A, G):
                q.wait(*marks)

        first = ExitStack()
        kmT = sb("kmT", [P, 2, MT, MEM], first)
        vm = sb("vm", [P, 2, MEM // P, MW], first)
        tmp256 = Ring([sb(f"tmp{i}", [P, S], first) for i in range(4)])
        small = sb("small", [P, 48], first)
        x1 = lambda k: res[:, k, N_META:T]
        h1h, h1l = lambda k: xh[:, k, 0:S], lambda k: xl[:, k, 0:S]

        def memory_head(layer, h, qm, gm, m_q, m_g, bufs, marks):
            j, o = h // 2, HD * (h % 2)
            pbuf, freed_p = bufs["p"].take()
            st, freed_st = bufs["st"].take()
            bank, freed = banks.take()
            for t in range(2):
                m_s = PE.op(ten.matmul, bank[:, t * MEM:(t + 1) * MEM], qm[o:o + HD, j, t * P:(t + 1) * P],
                            kmT[o:o + HD, layer, j, :], start=True, stop=True, after=[m_q[j], m_kv[layer], freed])
            sc = bank[:, :].rearrange("p (t m) -> p t m", t=2)
            m1 = V.op(vec.tensor_reduce, st[:, 0:2], sc, AX_X, ALU.max, after=[m_s, freed_st])
            m2 = V.op(vec.tensor_scalar, st[:, 2:4], st[:, 0:2], -(HD ** -0.5), None, ALU.mult, after=[m1])
            for t in range(2):
                m3 = A.op(act.activation, pbuf[:, t, :], sc[:, t, :], ACT.Exp, bias=st[:, 2 + t:3 + t],
                          scale=HD ** -0.5, accum_out=st[:, 4 + t:5 + t], after=[m2, freed_p])
            banks.give(bank, m3)
            m4 = V.op(vec.reciprocal, st[:, 6:8], st[:, 4:6], after=[m3])
            for t in range(2):
                m5 = V.op(vec.tensor_scalar, pbuf[:, t, :], pbuf[:, t, :], st[:, 6 + t:7 + t], None, ALU.mult,
                          after=[m4])
            yield
            ptb, freed_pt = bufs["pt"].take()
            bank, freed = banks.take()
            pt = bank[:, :].rearrange("p (k q) -> p k q", k=2)
            for t in range(2):
                for k in range(2):
                    m6 = PE.op(ten.transpose, pt[:, k, t * P:(t + 1) * P], pbuf[:, t, k * P:(k + 1) * P], ident,
                               after=[m5, freed])
            m7 = A.op(act.activation, ptb[:, :, :], pt, ACT.Copy, after=[m6, freed_pt])
            banks.give(bank, m7)
            bufs["p"].give(pbuf, m6)
            bufs["st"].give(st, m5)
            yield
            bank, freed = banks.take()
            for k in range(2):
                m8 = PE.op(ten.matmul, bank[o:o + HD, 0:S], vm[:, layer, k, h * HD:(h + 1) * HD], ptb[:, k, :],
                           start=(k == 0), stop=(k == 1), after=[m7, freed])
            bufs["pt"].give(ptb, m8)
            marks[h] = V.op(vec.tensor_tensor, qm[o:o + HD, j, :], bank[o:o + HD, 0:S], gm[o:o + HD, j, :],
                            ALU.mult, after=[m8, m_g[j]])
            banks.give(bank, marks[h])

        def mix_out(layer, m_y, ybuf, sqbuf, next_first, next_gain):
            m_yt, m_sq = [None] * KT, [None] * KT

            def evac(panel, ps, mark):
                m_sq[panel] = A.op(act.activation, sqbuf[:, panel, :], ps, ACT.Square, after=[mark])
                m_yt[panel] = V.op(vec.tensor_scalar, ybuf[:, panel, :], ps, col(f"post{layer}", panel), None,
                                   ALU.mult, after=[m_sq[panel]])
                return (m_yt[panel],)

            sbank, freed = banks.take()

            def stat_part(k):
                return PE.op(ten.matmul, sbank[:, 0:S], tab("ones_d"), sqbuf[:, k, :], start=(k == 0),
                             stop=(k == KT - 1), after=[m_ta, m_sq[k], freed])

            for panel in range(KT):
                project(f"w_out{layer}", [panel], h1h, h1l, S, m_y, evac, keep=True)
                if panel > 1:
                    stat_part(panel - 2)
            m_last = PE.last()
            settle()
            stat_part(KT - 2)
            m = stat_part(KT - 1)
            m_rs = rsqrt(rstd[:, 0:S], sbank[:, 0:S], EPS, ALU.add, [m])
            banks.give(sbank, m_rs)
            m_x2 = {}

            def add_pair(k):
                y2, x2 = ybuf[:, k:k + 2, :], res[:, k:k + 2, N_META:T]
                m = V.op(vec.tensor_tensor, y2, y2, rstd[:, 0:S].unsqueeze(1).broadcast_to([P, 2, S]), ALU.mult,
                         after=[m_rs, m_yt[k + 1]])
                m_x2[k] = V.op(vec.tensor_tensor, x2, x2, y2, ALU.add, after=[m])

            add_pair(0)
            for k in range(0, KT, 2):
                if k + 2 < KT:
                    add_pair(k + 2)
                m_next[k:k + 2] = split_inputs([(i, res[:, i, next_first:T], col(next_gain, i), [m_x2[k], m_meta],
                                                 xh[:, i, 0:T - next_first], xl[:, i, 0:T - next_first], m_last)
                                                for i in (k, k + 1)])
            for k in range(KT):
                m_nsq[k] = A.op(act.activation, sqr[:, k, 0:T - next_first], res[:, k, next_first:T], ACT.Square)

        ph = ExitStack()
        tr = sb("tr", [P, W_R], ph)
        zr, zk, zv = (sb(n, [P, BT, S], ph) for n in ("zr", "zk", "zv"))
        zl = sb("zl", [P, S], ph)
        gate = sb("gate", [P, BT, S], ph)
        qm = sb("qm", [P, MT, MEM], ph)
        gm = sb("gm", [P, MT, MEM], ph)
        ed = sb("ed", [P, BT, 2, CH + 1], ph)
        inv = sb("inv", [P, BT, S], ph)
        av_ = sb("av_", [P, BT, S], ph)
        kk = sb("kkh", [P, BT, S], ph)
        zt_ring = Ring([sb(f"zt{i}", [P, S + 1], ph) for i in range(2)])
        lw = sb("lw", [P, BR], ph)
        work = sb("work", [P, 5, 1024], ph)
        xt_all = sb("xt_all", [P, 6, 512], ph)
        mrs = sb("mrs", [P, MEM], ph)
        inner = ExitStack()
        mh, ml = sb("mh", [P, KT, S], inner, F32R), sb("ml", [P, KT, S], inner, F32R)
        mhk, mlk = lambda k: mh[:, k, :], lambda k: ml[:, k, :]

        def tabr(name):
            o, n = OFF_R[name]
            return tr[:, o:o + n]

        work_flat = work[:, :, :].rearrange("p a b -> p (a b)")
        tiles8 = lambda buf: buf.rearrange("p (k s) -> p k s", k=KT)
        mem_in, sq = tiles8(work_flat[:, 0:KT * S]), tiles8(work_flat[:, KT * S:2 * KT * S])
        sq_x = tiles8(xt_all[:, :, :].rearrange("p a b -> p (a b)")[:, 0:KT * S])
        m_mem = A.dma(mem_in, memT, s_in[3], 16)
        m_x = A.dma(res[:, :, N_META:T], xT, s_in[0], 16)
        m_ta = A.dma(ta[:, :], tab_a, s_in[1], 16)
        m_lw = A.dma(lw[:, :], lora, s_in[4], 16)
        s_in2 = [sem("s_tab_r"), sem("s_tab_b"), sem("s_meta")]
        m_tr = A.dma(tr[:, :], tab_r, s_in2[0], 16)
        m_meta = A.dma(res[:, :, 0:N_META], metaT, s_in2[2], 16)
        m_zero = V.op(vec.memset, zt_ring.free[0][0][:, 0:1], 0.0)
        m_zero = V.op(vec.memset, zt_ring.free[1][0][:, 0:1], 0.0)
        m_zero = V.op(vec.memset, ed[:, :, :, 0:1], 0.0)

        m_kv = {0: [], 1: []}
        m_mh = split_inputs([(k, mem_in[:, k, :], col("memn0", k), m_mem, mhk(k), mlk(k), None)
                             for k in range(KT)])
        m_msq = [square(k, sq[:, k, :], mem_in[:, k, :], [m_mem]) for k in range(KT)]

        def mem_stat():
            stat["mem"] = norm_stat(lambda k: sq[:, k, :], KT, MEM, "ones_d", EPS, m_msq, mrs[:, :])

        def token_major(tiles, dst_of, scale, m_scale, marks, bufs):
            pending = []

            def flush():
                panel, t, m1 = pending.pop(0)
                m2, marks[panel] = turn(t, tiles, dst_of(panel), m1, None)
                bufs.give(t, m2)

            def evac(panel, ps, mark):
                t, freed_t = bufs.take()
                m1 = V.op(vec.tensor_tensor, t[:, 0:ps.shape[1]], ps, scale(), ALU.mult, after=[mark, freed_t, m_scale()])
                if pending:
                    flush()
                pending.append((panel, t, m1))
                return (m1,)

            return evac, flush

        def memory_kv(layer):
            def k_evac(panel, ps, mark):
                m = V.op(vec.tensor_tensor, kmT[:, layer, panel, :], ps, mrs[:, :], ALU.mult,
                         after=[mark, stat["mem"]])
                m_kv[layer].append(m)
                return (m,)

            m_v_ = {}
            v_evac, flush = token_major([(0, P), (P, P)], lambda panel: lambda j, n, rows:
                                        vm[0:rows, layer, j:j + n, (panel - 2) * P:(panel - 1) * P],
                                        lambda: mrs[:, :], lambda: stat["mem"], m_v_, tmp256)

            def done():
                flush()
                m_kv[layer].extend(m_v_.values())
            return k_evac, v_evac, done

        k_evac, v_evac, done = memory_kv(0)
        project("w_mem0", [0, 1], mhk, mlk, MEM, m_mh, k_evac, hook=mem_stat, keep=True)
        m_xsq = [square(k, sq_x[:, k, :], x1(k), [m_x]) for k in range(KT)]
        m_rs0 = norm_stat(lambda k: sq_x[:, k, :], KT, S, "ones_d", EPS, m_xsq, rstd[:, 0:S])
        m_xr = [V.op(vec.tensor_tensor, sq_x[:, k, :], x1(k), rstd[:, 0:S], ALU.mult, after=[m_rs0])
                for k in range(KT)]
        m_h = split_inputs([(k, sq_x[:, k, :], col("pre0", k), m_xr[k], h1h(k), h1l(k), None) for k in range(KT)])
        project("w_mem0", [2, 3], mhk, mlk, MEM, m_mh, v_evac)
        m_mem0 = PE.last()
        done()

        m_z = {}

        def shift_evac(panel, ps, mark):
            if panel == 18:
                dst = zl[:, :]
            else:
                dst = (zr, zk, zv)[panel // BT][:, panel % BT, :]
            zt, freed = zt_ring.take()
            m1 = A.op(act.activation, zt[:, 1:S + 1], ps, ACT.Copy, after=[mark, freed, m_zero])
            m2 = V.op(vec.tensor_tensor, dst, zt[:, 0:S], zt[:, 1:S + 1], ALU.subtract, after=[m1])
            m_z[panel] = V.op(vec.scalar_tensor_tensor, dst, dst, col("mu", panel), zt[:, 1:S + 1],
                              ALU.mult, ALU.add, after=[m2, m_cols])
            zt_ring.give(zt, m_z[panel])
            return (m1,)

        project("a_w_in", [18], h1h, h1l, S, m_h, shift_evac)
        m_th = A.op(act.activation, zl[0:64, :], zl[0:64, :], ACT.Tanh, after=[m_z[18]])
        m_ed, m_inv, m_a = {}, {}, {}
        ones_s = tab("ones")

        m_cum = {}

        def low_rank(i):
            bank, freed = banks.take()
            m = PE.op(ten.matmul, bank[:, 0:S], lw[0:64, i * P:(i + 1) * P], zl[0:64, :], start=True, stop=True,
                      after=[m_lw, m_th, freed])
            e, freed_e = tmp256.take()
            m1 = A.op(act.activation, e[:, :], bank[:, 0:S], ACT.Sigmoid, bias=col("w0", i),
                      after=[m, m_cols, freed_e])
            banks.give(bank, m1)
            for c in range(2):
                m_cum[i] = V.op(vec.tensor_tensor_scan, ed[:, i, c, 1:CH + 1], ones_s, e[:, c * CH:(c + 1) * CH],
                                0.0, ALU.mult, ALU.add, after=[m1, m_ta, m_zero])
            tmp256.give(e, m_cum[i])
            bank, freed = banks.take()
            m = PE.op(ten.matmul, bank[:, 0:S], lw[64:128, i * P:(i + 1) * P], zl[64:128, :], start=True, stop=True,
                      after=[m_lw, m_z[18], freed])
            m_a[i] = A.op(act.activation, av_[:, i, :], bank[:, 0:S], ACT.Sigmoid, bias=col("a0", i), after=[m])
            banks.give(bank, m_a[i])

        def decays(i):
            mid = tab("mid")
            m_inv[i] = A.op(act.activation, inv[:, i, :].rearrange("p (c t) -> p c t", c=2), ed[:, i, :, 1:CH + 1],
                            ACT.Exp, bias=mid[:, 1:2], scale=DECAY_C, after=[m_cum[i], m_ta])
            m_ed[i] = A.op(act.activation, ed[:, i, :, :], ed[:, i, :, :], ACT.Exp, bias=mid[:, 0:1],
                           scale=-DECAY_C, after=[m_inv[i]])

        m_gmem, m_gate, m_qm = {}, {}, {}

        def silu_evac(dst, marks):
            def evac(panel, ps, mark):
                t, freed = tmp256.take()
                m1 = A.op(act.activation, t[:, :], ps, ACT.Sigmoid, after=[mark, freed])
                m3 = V.op(vec.tensor_tensor, dst[:, len(marks), :], t[:, :], ps, ALU.mult, after=[m1])
                tmp256.give(t, m3)
                marks[len(marks)] = m3
                return (m3,)
            return evac

        def qm_evac(panel, ps, mark):
            m_qm[panel - 25] = A.op(act.activation, qm[:, panel - 25, :], ps, ACT.Copy, after=[mark])
            return (m_qm[panel - 25],)

        gate_evac, gm_evac = silu_evac(gate, m_gate), silu_evac(gm, m_gmem)
        k1_evac, v1_evac, done = memory_kv(1)
        m_mh1 = []
        jobs = {"a_w_in": lambda p_: (h1h, h1l, S, m_h, shift_evac if p_ < 18 else gate_evac if p_ < 25 else
                                      qm_evac if p_ < 27 else gm_evac),
                "w_mem1": lambda p_: (mhk, mlk, MEM, m_mh1, k1_evac if p_ < 2 else v1_evac)}
        between.extend(LAYER0_BETWEEN)

        project("a_w_in", [6, 7], h1h, h1l, S, m_h, shift_evac, keep=True)
        for i in range(BT):
            low_rank(i)
            fill()
        for i in range(BT):
            decays(i)
        m_mh1 += split_inputs([(k, mem_in[:, k, :], col("memn1", k), None, mhk(k), mlk(k), m_mem0)
                               for k in range(KT)])

        m_ah, m_bt, m_kt_, m_rh, m_km, m_kk = {}, {}, {}, {}, {}, {}

        def keys(i):
            need("a_w_in", 6 + i)
            t, freed_t = tmp256.take()
            m1 = V.op(vec.tensor_scalar, kk[:, i, :], zk[:, i, :], col("kk", i), None, ALU.mult,
                      after=[m_z[6 + i], m_cols])
            m2 = A.op(act.activation, t[:, :], kk[:, i, :], ACT.Square, after=[m1, freed_t])
            fill()
            yield
            bank, freed = banks.take()
            m3 = PE.op(ten.matmul, bank[:, 0:S], tab("blk"), t[:, :], start=True, stop=True, after=[m2, m_ta, freed])
            m4 = rsqrt(t[:, :], bank[:, 0:S], 1e-12, ALU.max, [m3])
            banks.give(bank, m4)
            m5 = V.op(vec.tensor_tensor, kk[:, i, :], kk[:, i, :], t[:, :], ALU.mult, after=[m4, m2])
            m6 = V.op(vec.tensor_scalar, t[:, :], av_[:, i, :], 1.0, col("ka", i), ALU.subtract, ALU.mult,
                      after=[m5, m_a[i]])
            m_km[i] = V.op(vec.scalar_tensor_tensor, zk[:, i, :], t[:, :], 1.0, zk[:, i, :], ALU.add, ALU.mult,
                           after=[m6])
            tmp256.give(t, m_km[i])
            m7 = V.op(vec.tensor_tensor, av_[:, i, :], av_[:, i, :], kk[:, i, :], ALU.mult, after=[m6])
            m_bt[i] = V.op(vec.tensor_tensor, av_[:, i, :], av_[:, i, :], inv[:, i, :], ALU.mult,
                           after=[m7, m_inv[i]])
            m_kt_[i] = V.op(vec.tensor_tensor, inv[:, i, :], inv[:, i, :], zk[:, i, :], ALU.mult,
                            after=[m_bt[i], m_km[i]])
            fill()
            split = lambda buf: buf[:, i, :].rearrange("p (c t) -> p c t", c=2)
            m_ah[i] = V.op(vec.tensor_tensor, split(kk), split(kk), ed[:, i, :, 0:CH], ALU.mult,
                           after=[m7, m_ed[i]])

        skewed(keys(i) for i in range(BT))
        need("a_w_in", BT - 1)
        need("w_mem1", 3)
        done()
        inner.close()

        GROUPS = [(p, j) for p in range(2) for j in range(3)]
        b4 = lambda a: a.unsqueeze(1).broadcast_to([P, 4, P])
        v4 = lambda a: a.rearrange("p (g n) -> p g n", g=4)
        m_sq_done = everyone()

        def pieces(g):
            p, j = GROUPS[g]
            for q in range(4):
                yield q, 2 * j + q // 2, HD * p, (q % 2) * CH

        m_xt = {}

        def invert(g):
            slot = g % 3
            nlt, xx, yy = work_flat[:, slot * 1536:slot * 1536 + 512], \
                work_flat[:, slot * 1536 + 512:slot * 1536 + 1024], work_flat[:, slot * 1536 + 1024:slot * 1536 + 1536]
            xt = xt_all[:, g, :]
            bank, freed = banks.take()
            for q, i, o, t0 in pieces(g):
                m = PE.op(ten.matmul, bank[:, q * P:(q + 1) * P], av_[o:o + HD, i, t0:t0 + CH],
                          kk[o:o + HD, i, t0:t0 + CH], start=True, stop=True, after=[m_bt[i], m_ah[i], freed])
            m_nlt = V.op(vec.tensor_tensor, v4(nlt), v4(bank[:, :]), b4(tabr("neg_up")), ALU.mult,
                         after=[m, m_tr, m_sq_done])
            banks.give(bank, m_nlt)
            bank, freed = banks.take()
            for q, i, o, t0 in pieces(g):
                m = PE.op(ten.matmul, bank[:, q * P:(q + 1) * P], kk[o:o + HD, i, t0:t0 + CH],
                          av_[o:o + HD, i, t0:t0 + CH], start=True, stop=True, after=[freed])
            m1 = V.op(vec.tensor_tensor, v4(xx), v4(bank[:, :]), b4(tabr("neg_m0")), ALU.mult, after=[m])
            banks.give(bank, m1)
            m_x_ = V.op(vec.tensor_tensor, v4(xx), v4(xx), b4(ident), ALU.add, after=[m1])
            m2 = V.op(vec.tensor_tensor, v4(xt), v4(nlt), b4(tabr("m0t")), ALU.mult, after=[m_nlt])
            m_t_ = V.op(vec.tensor_tensor, v4(xt), v4(xt), b4(ident), ALU.add, after=[m2])
            for level in range(1, 7):
                yield
                bank, freed = banks.take()
                for q in range(4):
                    c = slice(q * P, (q + 1) * P)
                    m = PE.op(ten.matmul, bank[:, c], nlt[:, c], xx[:, c], start=True, stop=True,
                              after=[m_x_, m_nlt, freed])
                m_y = V.op(vec.tensor_tensor, v4(yy), v4(bank[:, :]), b4(tabr(f"m{level}")), ALU.mult, after=[m])
                banks.give(bank, m_y)
                yield
                if level < 6:
                    bank, freed = banks.take()
                    for q in range(4):
                        c = slice(q * P, (q + 1) * P)
                        m = PE.op(ten.matmul, bank[:, c], xt[:, c], yy[:, c], start=True, stop=True,
                                  after=[m_y, m_t_, freed])
                    m_x_ = V.op(vec.tensor_tensor, xx, xx, bank[:, :], ALU.add, after=[m])
                    banks.give(bank, m_x_)
                bank, freed = banks.take()
                for q in range(4):
                    c = slice(q * P, (q + 1) * P)
                    m = PE.op(ten.matmul, bank[:, c], yy[:, c], xt[:, c], start=True, stop=True,
                              after=[m_y, m_t_, freed])
                m_t_ = V.op(vec.tensor_tensor, xt, xt, bank[:, :], ALU.add, after=[m])
                banks.give(bank, m_t_)
                fill()
            m_xt[g] = m_t_

        skewed(invert(g) for g in range(3))
        skewed(invert(g) for g in range(3, 6))
        need("a_w_in", 17)

        m_bonus, m_vt, m_bk = [], {}, {}
        inner = ExitStack()
        vtok = sb("vtok", [P, 2, BR], inner)
        btok, ktok = (sb(n, [P, BR], inner) for n in ("btok", "ktok"))
        wu_w = sb("wu_w", [P, 2, BT * HD], inner)
        wu_u = sb("wu_u", [P, 2, BT * HD], inner)
        sqr_flat = sqr[:, :, :].rearrange("p a b -> p (a b)")
        ysb = sqr_flat[:, 0:BR * 2].rearrange("p (i s) -> p i s", i=BT)
        st1 = sqr_flat[:, 2 * BR:2 * BR + BT * HD].rearrange("p (i n) -> p i n", i=BT)
        A.wait(PE.last())
        V.wait(PE.last())
        for c in range(2):
            for part in range(2):
                bank, freed = banks.take()
                for n in range(3):
                    i = 3 * part + n
                    m = PE.op(ten.transpose, bank[:, n * P:(n + 1) * P], zv[:, i, c * CH:(c + 1) * CH], ident,
                              after=[m_z[12 + i], freed])
                m_vt[c, part] = A.op(act.activation, vtok[:, c, part * 384:(part + 1) * 384], bank[:, 0:384],
                                     ACT.Copy, after=[m])
                banks.give(bank, m_vt[c, part])
        for dst, src in ((btok, av_), (ktok, inv)):
            for part in range(2):
                bank, freed = banks.take()
                for n in range(3):
                    i = 3 * part + n
                    m = PE.op(ten.transpose, bank[:, n * P:(n + 1) * P], src[:, i, 0:CH], ident,
                              after=[m_kt_[i], freed])
                m_bk[src is inv, part] = A.op(act.activation, dst[:, part * 384:(part + 1) * 384], bank[:, 0:384],
                                              ACT.Copy, after=[m])
                banks.give(bank, m_bk[src is inv, part])

        for i in range(BT):
            t, freed_t = tmp256.take()
            m1 = V.op(vec.scalar_tensor_tensor, t[:, :], zr[:, i, :], col("rk", i), zk[:, i, :], ALU.mult, ALU.mult,
                      after=[m_z[i], m_km[i], freed_t])
            bank, freed = banks.take()
            m2 = PE.op(ten.matmul, bank[:, 0:S], tab("blk"), t[:, :], start=True, stop=True, after=[m1, freed])
            m3 = V.op(vec.tensor_tensor, zk[:, i, :], bank[:, 0:S], zv[:, i, :], ALU.mult,
                      after=[m2, m_z[12 + i], m_kt_[i]])
            banks.give(bank, m3)
            m_bonus.append(m3)
            tmp256.give(t, m2)
            split = lambda buf: buf[:, i, :].rearrange("p (c t) -> p c t", c=2)
            m_rh[i] = V.op(vec.tensor_tensor, split(zr), split(zr), ed[:, i, :, 1:CH + 1], ALU.mult,
                           after=[m1, m_ed[i]])

        m_ysb = {}
        m_state = None
        m_prev = [m_xt[g] for g in range(6)]
        for c in range(2):
            t0 = c * CH
            mats = {}
            for kind, lhs, rhs, mask in (("ak", inv, kk, "up"), ("rb", av_, zr, "upinc"), ("rk", inv, zr, "upinc")):
                base = {"ak": 0, "rb": 1536, "rk": 3072}[kind]
                for p in range(2):
                    for half in range(2):
                        bank, freed = banks.take()
                        for n in range(3):
                            i = 3 * half + n
                            o = HD * p
                            m = PE.op(ten.matmul, bank[:, n * P:(n + 1) * P], lhs[o:o + HD, i, t0:t0 + CH],
                                      rhs[o:o + HD, i, t0:t0 + CH], start=True, stop=True,
                                      after=[m_kt_[i], m_ah[i], m_rh[i], freed])
                        dst = work_flat[:, base + (p * 2 + half) * 384:base + (p * 2 + half + 1) * 384]
                        m = V.op(vec.tensor_tensor, dst.rearrange("p (g n) -> p g n", g=3),
                                 bank[:, 0:384].rearrange("p (g n) -> p g n", g=3),
                                 tabr(mask).unsqueeze(1).broadcast_to([P, 3, P]), ALU.mult, after=[m, m_prev])
                        banks.give(bank, m)
                        for n in range(3):
                            mats[kind, p, 3 * half + n] = (dst[:, n * P:(n + 1) * P], m)
            m_u = {}
            fill()
            for p in range(2):
                bank, freed = banks.take()
                for i in range(BT):
                    out = bank[:, i * HD:(i + 1) * HD]
                    h = 2 * i + p
                    a, m_a_ = mats["ak", p, i]
                    if c:
                        PE.quiet(ten.matmul, out, kk[HD * p:HD * p + HD, i, t0:t0 + CH], st1[HD * p:HD * p + HD, i, :],
                                 start=True, stop=False, after=[m_state, freed])
                    m = PE.op(ten.matmul, out, a, vtok[:, c, h * HD:(h + 1) * HD], start=not c, stop=True,
                              after=[m_a_, m_vt[c, i // 3], freed])
                m = A.op(act.activation, wu_w[:, p, :], bank[:, 0:BT * HD], ACT.Copy, after=[m])
                banks.give(bank, m)
                m_u["w", p] = m
            fill()
            for p in range(2):
                bank, freed = banks.take()
                for i in range(BT):
                    g, q = 3 * p + i // 2, 2 * (i % 2) + c
                    m = PE.op(ten.matmul, bank[:, i * HD:(i + 1) * HD], xt_all[:, g, q * P:(q + 1) * P],
                              wu_w[:, p, i * HD:(i + 1) * HD], start=True, stop=True,
                              after=[m_u["w", p], m_xt[g], freed])
                m = A.op(act.activation, wu_u[:, p, :], bank[:, 0:BT * HD], ACT.Copy, scale=-1.0, after=[m])
                banks.give(bank, m)
                m_u[p] = m
            fill()
            for i in range(BT):
                bank, freed = banks.take()
                for p in range(2):
                    h, o = 2 * i + p, HD * p
                    out = bank[o:o + HD, 0:CH]
                    vt = vtok[:, c, h * HD:(h + 1) * HD]
                    PE.quiet(ten.matmul, out, wu_u[:, p, i * HD:(i + 1) * HD], mats["rb", p, i][0], start=True,
                             stop=False, after=[m_u[p], mats["rb", p, i][1], freed])
                    m = PE.op(ten.matmul, out, vt, mats["rk", p, i][0], start=False, stop=(c == 0),
                              after=[mats["rk", p, i][1]])
                    if c:
                        m = PE.op(ten.matmul, out, st1[o:o + HD, i, :], zr[o:o + HD, i, t0:t0 + CH], start=False,
                                  stop=True)
                m_ysb[c, i] = A.op(act.activation, ysb[:, i, t0:t0 + CH], bank[:, 0:CH], ACT.Copy, after=[m])
                banks.give(bank, m_ysb[c, i])
            m_prev = [PE.last()]
            if c == 0:
                bank, freed = banks.take()
                for i in range(BT):
                    for p in range(2):
                        h, o = 2 * i + p, HD * p
                        out = bank[o:o + HD, i * HD:(i + 1) * HD]
                        PE.quiet(ten.matmul, out, btok[:, h * HD:(h + 1) * HD], wu_u[:, p, i * HD:(i + 1) * HD],
                                 start=True, stop=False, after=[m_bk[False, i // 3], freed])
                        m = PE.op(ten.matmul, out, ktok[:, h * HD:(h + 1) * HD], vtok[:, 0, h * HD:(h + 1) * HD],
                                  start=False, stop=True, after=[m_bk[True, i // 3]])
                for i in range(BT):
                    m_state = V.op(vec.tensor_scalar, st1[:, i, :], bank[:, i * HD:(i + 1) * HD],
                                   ed[:, i, 0, CH:CH + 1], math.exp(-MID), ALU.mult, ALU.mult, after=[m, m_ed[i]])
                banks.give(bank, m_state)
                m_prev = [PE.last()]
                fill(2)

        xt_flat = xt_all[:, :, :].rearrange("p a b -> p (a b)")
        quarter = [xt_flat[:, i * 512:(i + 1) * 512].rearrange("p (a b) -> p a b", a=2) for i in range(4)]
        A.wait(*m_prev)
        bufs = {"p": Ring(quarter[0:2]), "pt": Ring(quarter[2:4]),
                "st": Ring([sb(f"mst{i}", [P, 8], inner) for i in range(3)])}
        m_ym, m_d = {}, {}

        def group_norm(i):
            d = ysb[:, i, :]
            t, freed_t = tmp256.take()
            bank, freed = banks.take()
            m1 = PE.op(ten.matmul, bank[:, 0:S], tab("blkm"), d, start=True, stop=True,
                       after=[m_ysb[0, i], m_ysb[1, i], freed])
            m2 = V.op(vec.tensor_tensor, d, d, bank[:, 0:S], ALU.subtract, after=[m1])
            banks.give(bank, m2)
            m3 = A.op(act.activation, t[:, :], d, ACT.Square, after=[m2, freed_t])
            yield
            bank, freed = banks.take()
            m4 = PE.op(ten.matmul, bank[:, 0:S], tab("blkm"), t[:, :], start=True, stop=True, after=[m3, freed])
            m5 = rsqrt(t[:, :], bank[:, 0:S], LNX_EPS, ALU.add, [m4])
            banks.give(bank, m5)
            m6 = V.op(vec.scalar_tensor_tensor, d, d, col("lnw", i), t[:, :], ALU.mult, ALU.mult, after=[m5, m3])
            tmp256.give(t, m6)
            m_d[i] = V.op(vec.scalar_tensor_tensor, d, d, col("lnb", i), zk[:, i, :], ALU.add, ALU.add,
                          after=[m6, m_bonus[i]])

        need("a_w_in", 28)
        m_in0 = PE.last()
        skewed([memory_head(0, h, qm, gm, m_qm, m_gmem, bufs, m_ym) for h in range(MEM_HEADS)]
               + [group_norm(i) for i in range(BT)])
        m_y = {}
        m_d = [V.op(vec.tensor_tensor, ysb[:, i, :], ysb[:, i, :], gate[:, i, :], ALU.mult,
                    after=[m_d[i], m_gate[i]]) for i in range(BT)]
        m_y = split_inputs([(i, ysb[:, i, :], 1.0, m_d[i], h1h(i), h1l(i), m_in0) for i in range(BT)]
                           + [(j, qm[:, j, :], 1.0, [m_ym[2 * j], m_ym[2 * j + 1]], h1h(BT + j), h1l(BT + j), m_in0)
                              for j in range(MT)])

        ybuf = work_flat[:, 0:2048].rearrange("p (k s) -> p k s", k=KT)
        sqb = work_flat[:, 2048:4096].rearrange("p (k s) -> p k s", k=KT)
        V.wait(*m_prev)
        A.wait(*m_prev)
        mix_out(0, m_y, ybuf, sqb, N_META, "pre1")
        new_phase()
        inner.close()
        ph.close()

        ph = ExitStack()
        kh, kl = sb("kh", [P, KT, S], ph, F32R), sb("kl", [P, KT, S], ph, F32R)
        sq = sb("sq", [P, KT, S], ph)
        kT = sb("kT", [P, BT, S], ph)
        qT = sb("qT", [P, BT, S], ph)
        vt = sb("vt", [P, 2, BR], ph)
        rh = sb("rh", [P, BT, S], ph)
        gate = sb("gate1", [P, BT, S], ph)
        qm = sb("qm1", [P, MT, MEM], ph)
        gm = sb("gm1", [P, MT, MEM], ph)
        ybuf = sb("ybuf1", [P, KT, S], ph)
        bufs = {"p": Ring([sb(f"mp1{i}", [P, 2, MEM], ph) for i in range(3)]),
                "pt": Ring([sb(f"mpt1{i}", [P, 2, S], ph) for i in range(2)]),
                "st": Ring([sb(f"mst1{i}", [P, 8], ph) for i in range(4)])}
        scb = Ring([sb(f"scb{i}", [P, 2, 384], ph) for i in range(3)])
        ptb1 = Ring([sb(f"ptb1{i}", [P, 384], ph) for i in range(2)])
        stb = Ring([sb(f"stb{i}", [P, 16], ph) for i in range(4)])

        m_h = list(m_next)
        rs1 = rstd[:, 0:S]

        m_q, m_k, m_v, m_qm, m_gmem, m_gate, m_r = {}, {}, {}, {}, {}, {}, {}

        def scaled(dst, first_panel, marks, extra=1.0):
            def evac(panel, ps, mark):
                m = V.op(vec.scalar_tensor_tensor, dst[:, panel - first_panel, :], ps, extra, rs1, ALU.mult, ALU.mult,
                         after=[mark, stat["x"]])
                marks[panel - first_panel] = m
                return (m,)
            return evac

        slopes = alibi_slopes(BT)
        m_y = {}

        def silu(buf, marks, n):
            for i in range(n):
                t, freed = tmp256.take()
                m = A.op(act.activation, t[:, :], buf[:, i, :], ACT.Sigmoid, after=[marks[i], freed])
                marks[i] = G.op(pool.tensor_tensor, buf[:, i, :], buf[:, i, :], t[:, :], ALU.mult, after=[m])
                tmp256.give(t, marks[i])

        def diff_head(h):
            need("b_w_in", h)
            need("w_kv", h)
            st, freed_st = stb.take()
            pb, freed_p = scb.take()
            for c in range(2):
                o = HD * c
                bank, freed = banks.take()
                PE.quiet(ten.matmul, bank[:, 0:P], qT[o:o + HD, h, 0:P], kT[o:o + HD, h, 0:P], start=True, stop=True,
                         after=[m_q[h], m_k[h], freed])
                m = PE.op(ten.matmul, bank[:, P:384], qT[o:o + HD, h, P:S], kT[o:o + HD, h, :], start=True, stop=True)
                m1 = V.op(vec.scalar_tensor_tensor, pb[:, c, :], tab("dist"), -slopes[h], bank[:, 0:384], ALU.mult,
                          ALU.add, after=[m, freed_p, freed_st])
                banks.give(bank, m1)
                V.op(vec.tensor_reduce, st[:, 2 * c:2 * c + 1], pb[:, c, 0:P], AX_X, ALU.max, after=[m1])
                m2 = V.op(vec.tensor_reduce, st[:, 2 * c + 1:2 * c + 2], pb[:, c, P:384], AX_X, ALU.max)
            m3 = V.op(vec.tensor_scalar, st[:, 4:8], st[:, 0:4], -1.0, None, ALU.mult, after=[m2])
            for c in range(2):
                for t, (a, b) in enumerate(((0, P), (P, 384))):
                    n = 2 * c + t
                    m4 = A.op(act.activation, pb[:, c, a:b], pb[:, c, a:b], ACT.Exp, bias=st[:, 4 + n:5 + n],
                              accum_out=st[:, 8 + n:9 + n], after=[m3])
            m5 = V.op(vec.reciprocal, st[:, 12:16], st[:, 8:12], after=[m4])
            m6 = V.op(vec.tensor_scalar, st[:, 14:16], st[:, 14:16], neg_lam, None, ALU.mult, after=[m5, m_lam])
            for t, (a, b) in enumerate(((0, P), (P, 384))):
                m7 = V.op(vec.tensor_scalar, pb[:, 0, a:b], pb[:, 0, a:b], st[:, 12 + t:13 + t], None, ALU.mult,
                          after=[m5])
                m8 = V.op(vec.scalar_tensor_tensor, pb[:, 0, a:b], pb[:, 1, a:b], st[:, 14 + t:15 + t], pb[:, 0, a:b],
                          ALU.mult, ALU.add, after=[m6, m7])
            stb.give(st, m8)
            fill()
            yield
            pt, freed_pt = ptb1.take()
            bank, freed = banks.take()
            for out, src in ((0, 0), (P, P), (2 * P, 2 * P)):
                m9 = PE.op(ten.transpose, bank[:, out:out + P], pb[:, 0, src:src + P], ident, after=[m8, freed])
            m10 = A.op(act.activation, pt[:, :], bank[:, 0:384], ACT.Copy, after=[m9, freed_pt])
            banks.give(bank, m10)
            scb.give(pb, m9)
            fill()
            yield
            need("w_kv", BT + min(h + 1, BT - 1))
            if h == BT - 1:
                flush()
            ob, freed = banks.take()
            PE.quiet(ten.matmul, ob[:, 0:S], vt[:, 0, h * P:(h + 1) * P], pt[:, 0:S], start=True, stop=False,
                     after=[m10, freed, m_v[6 + h]])
            m11 = PE.op(ten.matmul, ob[:, P:S], vt[:, 1, h * P:(h + 1) * P], pt[:, S:384], start=False, stop=True)
            ptb1.give(pt, m11)
            t, freed_t = tmp256.take()
            m12 = A.op(act.activation, t[:, :], ob[:, 0:S], ACT.Square, after=[m11, freed_t])
            fill()
            yield
            r, freed_r = tmp256.take()
            m13 = norm_stat(lambda k: t[:, :], 1, S, "ones128", EPS, m12, r[:, :], freed_r)
            tmp256.give(t, m13)
            m14 = V.op(vec.scalar_tensor_tensor, rh[:, h, :], ob[:, 0:S], subln, r[:, :], ALU.mult, ALU.mult,
                       after=[m13, m_sub])
            banks.give(ob, m14)
            tmp256.give(r, m14)
            m_r[h] = m14
            fill()

        khk, klk, m_hk = lambda k: kh[:, k, :], lambda k: kl[:, k, :], []
        q_evac, k_evac = scaled(qT, 0, m_q, HD ** -0.5), scaled(kT, 0, m_k)
        v_evac, flush = token_major([(0, P), (P, P)], lambda panel: lambda j, n, rows:
                                    vt[0:rows, j:j + n, (panel - 6) * P:(panel - 5) * P], lambda: rs1,
                                    lambda: stat["x"], m_v, tmp256)
        g_evac = scaled(gate, 6, m_gate)
        qm_evac, gm_evac = scaled(qm, 12, m_qm), scaled(gm, 14, m_gmem)
        jobs = {"b_w_in": lambda p_: (h1h, h1l, S, m_h, q_evac if p_ < 6 else g_evac if p_ < 12 else
                                      qm_evac if p_ < 14 else gm_evac),
                "w_kv": lambda p_: (khk, klk, S, m_hk, k_evac if p_ < 6 else v_evac)}
        project("b_w_in", [0], h1h, h1l, S, m_h, q_evac, hook=lambda: residual_stat(S), keep=True)
        m_hk += split_inputs([(k, x1(k), col("kvn", k), m_next[k], kh[:, k, :], kl[:, k, :], None)
                              for k in range(KT)])
        project("w_kv", [0], khk, klk, S, m_hk, k_evac)

        LQ = 2 * BT
        m = V.op(vec.tensor_tensor, small[:, LQ:LQ + 2], cols[:, COL["lam"]:COL["lam"] + 2],
                 cols[:, COL["lam"] + 2:COL["lam"] + 4], ALU.mult)
        bank, freed = banks.take()
        m = PE.op(ten.matmul, bank[:, 0:2], tab("ones"), small[:, LQ:LQ + 2], start=True, stop=True, after=[m, freed])
        m = A.op(act.activation, small[:, LQ + 2:LQ + 4], bank[:, 0:2], ACT.Exp, after=[m])
        banks.give(bank, m)
        m = V.op(vec.tensor_tensor, small[:, LQ + 4:LQ + 5], small[:, LQ + 3:LQ + 4], small[:, LQ + 2:LQ + 3],
                 ALU.subtract, after=[m])
        m_lam = V.op(vec.tensor_scalar, small[:, LQ + 5:LQ + 6], small[:, LQ + 4:LQ + 5], LAM_INIT, None,
                     ALU.subtract, after=[m])
        m_sub = V.op(vec.tensor_scalar, small[:, LQ + 6:LQ + 7], col("subln"), 1.0 - LAM_INIT, None, ALU.mult)
        neg_lam, subln = small[:, LQ + 5:LQ + 6], small[:, LQ + 6:LQ + 7]

        between.extend(LAYER1_BETWEEN)
        m_ym = {}

        def memory_stream(h):
            need("b_w_in", 12 + h // 2)
            g = memory_head(1, h, qm, gm, m_qm, m_gmem, bufs, m_ym)
            for _ in range(2):
                next(g)
                fill()
                yield
            if h == 0:
                need("b_w_in", 11)
                silu(gm, m_gmem, MT)
                silu(gate, m_gate, BT)
            for _ in g:
                pass

        skewed([diff_head(h) for h in range(BT)] + [memory_stream(h) for h in range(MEM_HEADS)])
        m_in1 = PE.last()
        m_rg = [V.op(vec.tensor_tensor, rh[:, h, :], rh[:, h, :], gate[:, h, :], ALU.mult,
                     after=[m_r[h], m_gate[h]]) for h in range(BT)]
        m_y = split_inputs([(h, rh[:, h, :], 1.0, m_rg[h], h1h(h), h1l(h), m_in1) for h in range(BT)]
                           + [(j, qm[:, j, :], 1.0, [m_ym[2 * j], m_ym[2 * j + 1]], h1h(BT + j), h1l(BT + j), m_in1)
                              for j in range(MT)])
        mix_out(1, m_y, ybuf, sq, 0, "ffn1")
        new_phase()
        ph.close()
        first.close()

        second = ExitStack()
        tb = sb("tb", [P, W_B], second)
        m_tb = A.dma(tb[:, :], tab_b, s_in2[1], 16)
        tmp = Ring([sb(f"tmp2{i}", [P, T], second) for i in range(7)])
        x2 = lambda k: res[:, k, :]
        h2h, h2l = lambda k: xh[:, k, :], lambda k: xl[:, k, :]

        def tabb(name):
            o, n = OFF_B[name]
            return tb[:, o:o + n]

        def times_rms(out, ps, mark, freed=None):
            return V.op(vec.tensor_tensor, out, ps, rstd[:, :], ALU.mult, after=[mark, stat["x"], freed])

        def ffn(n, next_gain):
            ph = ExitStack()
            hh, hl = sb(f"hh{n}", [P, FT, T], ph, F32R), sb(f"hl{n}", [P, FT, T], ph, F32R)
            m_h, m_hid, gates = list(m_next), {}, {}
            more_splits([(sb(f"wh{n}_{i}", [P, WC], ph, F32R), sb(f"wl{n}_{i}", [P, WC], ph, F32R))
                         for i in range(N_EXTRA)])

            def gate_evac(panel, ps, mark):
                a, freed_a = tmp.take()
                s_, freed_s = tmp.take()
                m1 = times_rms(a[:, :], ps, mark, freed_a)
                m2 = A.op(act.activation, s_[:, :], a[:, :], ACT.Sigmoid, after=[m1, freed_s])
                gates[panel] = (a, s_, m2)
                return (m1,)

            def up_evac(panel, ps, mark):
                b, freed_b = tmp.take()
                a, s_, m2 = gates[panel]
                m1 = times_rms(b[:, :], ps, mark, freed_b)
                m3 = V.op(vec.tensor_tensor, a[:, :], a[:, :], s_[:, :], ALU.mult, after=[m2])
                m4 = V.op(vec.tensor_tensor, a[:, :], a[:, :], b[:, :], ALU.mult, after=[m3, m1])
                m5 = A.op(act.activation, hh[:, panel, :], a[:, :], ACT.Copy, after=[m4])
                m_hid[panel] = G.op(pool.tensor_tensor, hl[:, panel, :], a[:, :], hh[:, panel, :].bitcast(F32),
                                    ALU.subtract, after=[m5])
                tmp.give(a, m_hid[panel])
                tmp.give(s_, m3)
                tmp.give(b, m4)
                return (m1,)

            for panel in range(FT):
                project(f"ffn{n}_gate", [panel], h2h, h2l, T, m_h, gate_evac,
                        hook=None if panel else (lambda: residual_stat(T)), keep=True)
                project(f"ffn{n}_up", [panel], h2h, h2l, T, m_h, up_evac, keep=True)
            settle()
            m_in = PE.last()

            def down_evac(panel, ps, mark):
                m = V.op(vec.scalar_tensor_tensor, x2(panel), ps, 0.5, x2(panel), ALU.mult, ALU.add, after=[mark])
                residual_done(panel, 0, next_gain, m, m_in)
                return (m,)

            for panel in range(KT):
                if panel == KT - 3:
                    fewer_splits()
                project(f"ffn{n}_down", [panel], lambda k: hh[:, k, :], lambda k: hl[:, k, :], T, m_hid, down_evac,
                        kt=FT, keep=True)
            settle()
            assert not extra
            new_phase()
            ph.close()

        ffn(1, "mix")

        ph = ExitStack()
        m_h = list(m_next)
        iq = sb("iq", [P, 4, T], ph)
        ikm = sb("ikm", [P, 2, T], ph)
        iw = sb("iw", [P, 3, IDX_HEADS], ph)
        score = sb("score", [P, QW], ph)
        mask = sb("mask", [P, QW], ph)
        top8 = sb("top8", [P, 8], ph)
        rq = sb("rq", [P, 8, T], ph)
        rk = sb("rk", [P, 8, T], ph)
        rv = sb("rv", [P, 3, RET_HEADS * RET_DV], ph)
        rel = Ring([sb(f"rel{i}", [P, QW], ph) for i in range(2)])
        m_rope = [None]

        def mix_stat():
            residual_stat(T)
            six = tb[:, 0:6 * T].rearrange("p (a t) -> p a t", a=6)
            m_rope[0] = V.op(vec.tensor_tensor, six, six, rstd[:, :].unsqueeze(1).broadcast_to([P, 6, T]), ALU.mult,
                             after=[stat["x"], m_tb])

        def rope_halves(dst, cos, sin):
            def evac(ps, mark, m_free=None):
                a, freed_a = tmp.take()
                b, freed_b = tmp.take()
                m1 = V.op(vec.tensor_tensor, a[:, :], ps, cos, ALU.mult, after=[mark, freed_a, m_rope[0]])
                m2 = V.op(vec.tensor_tensor, b[0:64, :], ps[64:128, :], sin[0:64, :], ALU.mult, after=[freed_b])
                m2 = V.op(vec.tensor_tensor, b[64:128, :], ps[0:64, :], sin[64:128, :], ALU.mult)
                m3 = G.op(pool.tensor_tensor, dst, a[:, :], b[:, :], ALU.add, after=[m1, m2, m_free])
                tmp.give(a, m3)
                tmp.give(b, m3)
                return m2, m3
            return evac

        m_iq, m_ik = {}, None

        def iq_evac(panel, ps, mark):
            nonlocal m_ik
            if panel < 4:
                m2, m_iq[panel] = rope_halves(iq[:, panel, :], tabb("icos"), tabb("isin"))(ps, mark)
            elif panel == 4:
                m2, m3 = rope_halves(ikm[:, 0, :], tabb("icos"), tabb("isin"))(ps, mark)
                m4 = V.op(vec.tensor_copy, ikm[:, 1, :], ikm[:, 0, :], after=[m3])
                for v, r in ((0, 32), (0, 96), (1, 0), (1, 64)):
                    m_ik = V.op(vec.memset, ikm[r:r + 32, v, :], 0.0, after=[m4])
            else:
                t, freed_t = tmp.take()
                m2 = times_rms(t[:, :], ps, mark, freed_t)
                held_iw.append((t, m2))
            return (m2,)

        held_iw = []

        project("idx", list(range(6)), h2h, h2l, T, m_h, iq_evac, hook=mix_stat)
        t, m1 = held_iw[0]
        bank, freed = banks.take()
        for j, (q0, n, _) in enumerate(QT):
            m = PE.op(ten.transpose, bank[0:n, j * 8:j * 8 + 8], t[0:8, q0:q0 + n], ident[0:8, 0:8],
                      after=[m1, freed])
        tmp.give(t, m)
        m_iw = V.op(vec.tensor_scalar, iw[:, 0:2, :], bank[:, 0:16].rearrange("p (a b) -> p a b", a=2),
                    (IDX_DH ** -0.5) * (IDX_HEADS ** -0.5), None, ALU.mult, after=[m])
        m_iw = V.op(vec.tensor_scalar, iw[0:16, 2, :], bank[0:16, 16:24], (IDX_DH ** -0.5) * (IDX_HEADS ** -0.5),
                    None, ALU.mult)
        banks.give(bank, m_iw)

        m_score = m_tb
        for h in range(IDX_HEADS):
            ba, freed_a = banks.take()
            bb, freed_b = banks.take()
            r, freed_r = rel.take()
            for j, (q0, n, wd) in enumerate(QT):
                out = ba[:, QO[j]:QO[j] + wd] if j < 2 else bb[0:n, 0:wd]
                m = PE.op(ten.matmul, out, iq[:, h // 2, q0:q0 + n], ikm[:, h % 2, 0:wd], start=True, stop=True,
                          after=[m_iq[h // 2], m_ik, freed_a, freed_b])
            m1 = A.op(act.activation, r[:, 0:384], ba[:, 0:384], ACT.Relu, after=[m, freed_r])
            m2 = A.op(act.activation, r[0:16, 384:QW], bb[0:16, 0:T], ACT.Relu)
            banks.give(ba, m1)
            banks.give(bb, m2)
            prev = m_score
            for j, (q0, n, wd) in enumerate(QT):
                c = slice(QO[j], QO[j] + wd)
                src = (tabb("adm") if h == 0 else score)[0:n, c]
                m_score = V.op(vec.scalar_tensor_tensor, score[0:n, c], r[0:n, c], iw[0:n, j, h:h + 1], src,
                               ALU.mult, ALU.add, after=[m2, m_iw, prev])
            rel.give(r, m_score)

        m_mask = {}

        def top_k(j):
            q0, n, wd = QT[j]
            c = slice(QO[j], QO[j] + wd)
            s = score[0:n, c]
            m = m_score
            for _ in range(TOPK // 8):
                m1 = V.op(vec.max, top8[0:n, :], s, after=[m])
                m = V.op(vec.match_replace, s, top8[0:n, :], s, TAKEN, after=[m1])
                yield
            m1 = V.op(vec.tensor_scalar, mask[0:n, c], s, 0.7 * TAKEN, -BIG, ALU.is_gt, ALU.mult, after=[m])
            m2 = V.op(vec.tensor_tensor, mask[0:n, c], mask[0:n, c], tabb("adm")[0:n, c], ALU.add, after=[m1])
            m_mask[j] = V.op(vec.tensor_copy, mask[0:n, QO[j]:QO[j] + N_META],
                             tabb("meta")[0:n, N_META * j:N_META * (j + 1)], after=[m2])

        choosing = [step for j in range(3) for step in [top_k(j)] * (TOPK // 8 + 1)]

        def choose():
            if choosing:
                next(choosing.pop(0), None)

        m_rq = {}
        held = {}

        def ret_rope(dst, kind):
            def evac(panel, ps, mark):
                h, half = (panel % 8) // 2, panel % 2
                x1_, mk1 = held["x1"]
                t = []
                for src, tabn, mk in ((x1_, "rcos", mk1), (ps, "rsin", mark), (ps, "rcos", mark), (x1_, "rsin", mk1)):
                    b, freed = tmp.take()
                    t.append((b, V.op(vec.tensor_tensor, b[:, :], src, tabb(tabn), ALU.mult, after=[mk, freed, m_rope[0]])))
                ma = G.op(pool.tensor_tensor, dst[:, 2 * h, :], t[0][0][:, :], t[1][0][:, :], ALU.subtract,
                          after=[t[1][1]])
                mb = G.op(pool.tensor_tensor, dst[:, 2 * h + 1, :], t[2][0][:, :], t[3][0][:, :], ALU.add,
                          after=[t[3][1]])
                for n, (b, _) in enumerate(t):
                    tmp.give(b, ma if n < 2 else mb)
                m_rq[kind, h] = mb
                held["give"].append(t[3][1])
                return (t[3][1],)
            return evac

        def project_pair(p0, evac):
            def hold(panel, ps, mark):
                held["x1"] = (ps, mark)

            project("ret", [p0], h2h, h2l, T, m_h, hold)
            held["give"] = []
            project("ret", [p0 + 1], h2h, h2l, T, m_h, evac)
            banks.give(kept.pop(), *held["give"])

        for h in range(RET_HEADS):
            project_pair(2 * h, ret_rope(rq, "q"))
            choose()
        for h in range(RET_HEADS):
            project_pair(8 + 2 * h, ret_rope(rk, "k"))
            choose()

        tiles2 = [(q0, n) for q0, n, _ in QT]
        m_rv = {}
        rv_evac, flush = token_major(tiles2, lambda panel: lambda j, n, rows:
                                     rv[0:rows, j:j + n, panel * P:(panel + 1) * P], lambda: rstd[:, :],
                                     lambda: stat["x"], m_rv, tmp)
        for panel in range(16):
            project("rv", [panel], h2h, h2l, T, m_h, rv_evac, keep=True)
            choose()
        settle()
        flush()

        yr = Ring([sb(f"yr{i}", [P, 4, T], ph) for i in range(2)])
        yh, yl = sb("yh", [P, 16, T], ph, F32R), sb("yl", [P, 16, T], ph, F32R)
        pr = Ring([sb(f"pr{i}", [P, KW], ph) for i in range(2)])
        m_yr = {}

        def ret_head(h):
            pb, freed_p = pr.take()
            bank, freed = banks.take()
            for j, (k0, n, _) in enumerate(QT):
                q0, nq = KQ[j]
                for d in range(2):
                    fn = PE.op if d else PE.quiet
                    m = fn(ten.matmul, bank[0:n, KO[j]:KO[j] + nq], rk[:, 2 * h + d, k0:k0 + n],
                           rq[:, 2 * h + d, q0:T], start=(d == 0), stop=(d == 1),
                           after=[m_rq["q", h], m_rq["k", h], freed])
            dec = tabb("decay")[:, h * KW:(h + 1) * KW]
            V.op(vec.tensor_tensor, pb[:, 0:416], bank[:, 0:416], dec[:, 0:416], ALU.mult, after=[m, freed_p])
            m1 = V.op(vec.tensor_tensor, pb[0:16, 416:KW], bank[0:16, 416:KW], dec[0:16, 416:KW], ALU.mult)
            banks.give(bank, m1)
            yield
            yb, freed_y = yr.take()
            m_sq, outs = [], []
            for e in range(4):
                ob, freed = banks.take()
                c = slice(h * RET_DV + e * P, h * RET_DV + (e + 1) * P)
                for j, (k0, n, _) in enumerate(QT):
                    q0, nq = KQ[j]
                    fn = PE.op if j == 2 else PE.quiet
                    m2 = fn(ten.matmul, ob[:, q0:T], rv[0:n, j, c], pb[0:n, KO[j]:KO[j] + nq], start=(j == 0),
                            stop=(j == 2), after=[m1, m_rv[4 * h + e], freed])
                t, freed_t = tmp.take()
                m_sq.append(A.op(act.activation, t[:, :], ob[:, 0:T], ACT.Square, after=[m2, freed_t]))
                m_c = V.op(vec.tensor_copy, yb[:, e, :], ob[:, 0:T], after=[m_sq[-1], freed_y])
                banks.give(ob, m_sq[-1], m_c)
                outs.append((t, m_c))
            pr.give(pb, m2)
            yield
            r, freed_r = tmp.take()
            m3 = norm_stat(lambda k: outs[k][0][:, :], 4, T, "ones512", EPS, m_sq, r[:, :], freed_r)
            for e in range(4):
                tmp.give(outs[e][0], m3)
                m_yr[4 * h + e] = V.op(vec.tensor_tensor, yb[:, e, :], yb[:, e, :], r[:, :], ALU.mult,
                                       after=[m3, outs[e][1]])
            tmp.give(r, m_yr[4 * h + 3])

            def rg_evac(panel, ps, mark):
                a, freed_a = tmp.take()
                s_, freed_s = tmp.take()
                m1 = times_rms(a[:, :], ps, mark, freed_a)
                m2 = A.op(act.activation, s_[:, :], a[:, :], ACT.Sigmoid, after=[m1, freed_s])
                m4 = V.op(vec.tensor_tensor, a[:, :], a[:, :], yb[:, panel % 4, :], ALU.mult, after=[m2, m_yr[panel]])
                m5 = V.op(vec.tensor_tensor, a[:, :], a[:, :], s_[:, :], ALU.mult, after=[m4])
                m_yg[panel] = split_input(panel, a[:, :], 1.0, m5, yh[:, panel, :], yl[:, panel, :], None)
                tmp.give(a, m_yg[panel])
                tmp.give(s_, m5)
                return (m1,)

            choose()
            project("rg", list(range(4 * h, 4 * h + 4)), h2h, h2l, T, m_h, rg_evac)
            yr.give(yb, m_yg[4 * h + 3])
            yield

        m_yg = {}
        skewed(ret_head(h) for h in range(RET_HEADS))
        m_ret = PE.last()

        assert not choosing
        G.wait(m_ret)
        V.wait(m_ret)
        A.wait(m_ret)
        aq, ak = rq, rk
        m_aqk = {}

        def aqk_evac(panel, ps, mark):
            dst = (aq if panel < 8 else ak)[:, panel % 8, :]
            m2, m_aqk[panel] = rope_halves(dst, tabb("acos"), tabb("asin"))(ps, mark)
            return (m2,)

        project("aqk", list(range(16)), h2h, h2l, T, m_h, aqk_evac)
        rv_flat = rv[:, :, :].rearrange("p a b -> p (a b)")
        avt = rv_flat[:, 0:3 * ATT_HEADS * P].rearrange("p (t n) -> p t n", t=3)
        m_av = {}
        av_evac, flush = token_major(tiles2, lambda panel: lambda j, n, rows:
                                     avt[0:rows, j:j + n, panel * P:(panel + 1) * P], lambda: rstd[:, :],
                                     lambda: stat["x"], m_av, tmp)
        project("av", list(range(8)), h2h, h2l, T, m_h, av_evac)
        flush()

        merged = rv_flat[:, 3 * ATT_HEADS * P:3 * ATT_HEADS * P + KT * T].rearrange("p (k t) -> p k t", k=KT)
        gatt = sqr
        m_gr, m_ga, m_mg = {}, {}, {}

        def gate2_evac(panel, ps, mark):
            dst = (merged if panel < 8 else gatt)[:, panel % 8, :]
            m1 = times_rms(dst, ps, mark)
            (m_gr if panel < 8 else m_ga)[panel % 8] = A.op(act.activation, dst, dst, ACT.Sigmoid, after=[m1])
            return (m1,)

        def ret_out_evac(panel, ps, mark):
            m_mg[panel] = V.op(vec.tensor_tensor, merged[:, panel, :], merged[:, panel, :], ps, ALU.mult,
                               after=[mark, m_gr[panel]])
            return (m_mg[panel],)

        project("g2", list(range(16)), h2h, h2l, T, m_h, gate2_evac)
        m_in = PE.last()

        pbs, pts = rel, pr
        sts = Ring([sb(f"sts{i}", [P, 12], ph) for i in range(3)])
        m_ya = {}
        scale = 128 ** -0.5

        def att_head(h):
            pb, freed_p = pbs.take()
            st, freed_st = sts.take()
            ba, freed_a = banks.take()
            bb, freed_b = banks.take()
            for j, (q0, n, wd) in enumerate(QT):
                out = ba[:, QO[j]:QO[j] + wd] if j < 2 else bb[0:n, 0:wd]
                m = PE.op(ten.matmul, out, aq[:, h, q0:q0 + n], ak[:, h, 0:wd], start=True, stop=True,
                          after=[m_aqk[h], m_aqk[8 + h], freed_a, freed_b])
            m1 = V.op(vec.scalar_tensor_tensor, pb[:, 0:384], ba[:, 0:384], scale, mask[:, 0:384], ALU.mult, ALU.add,
                      after=[m, m_mask[0], m_mask[1], m_mask[2], freed_p, freed_st])
            m1 = V.op(vec.scalar_tensor_tensor, pb[0:16, 384:QW], bb[0:16, 0:T], scale, mask[0:16, 384:QW], ALU.mult,
                      ALU.add)
            banks.give(ba, m1)
            banks.give(bb, m1)
            for j, (q0, n, wd) in enumerate(QT):
                m2 = V.op(vec.tensor_reduce, st[0:n, j:j + 1], pb[0:n, QO[j]:QO[j] + wd], AX_X, ALU.max, after=[m1])
            m3 = V.op(vec.tensor_scalar, st[:, 3:5], st[:, 0:2], -1.0, None, ALU.mult, after=[m2])
            m3 = V.op(vec.tensor_scalar, st[0:16, 5:6], st[0:16, 2:3], -1.0, None, ALU.mult)
            for j, (q0, n, wd) in enumerate(QT):
                c = slice(QO[j], QO[j] + wd)
                m4 = A.op(act.activation, pb[0:n, c], pb[0:n, c], ACT.Exp, bias=st[0:n, 3 + j:4 + j],
                          accum_out=st[0:n, 6 + j:7 + j], after=[m3])
            m5 = V.op(vec.reciprocal, st[:, 9:11], st[:, 6:8], after=[m4])
            m5 = V.op(vec.reciprocal, st[0:16, 11:12], st[0:16, 8:9])
            for j, (q0, n, wd) in enumerate(QT):
                c = slice(QO[j], QO[j] + wd)
                m6 = V.op(vec.tensor_scalar, pb[0:n, c], pb[0:n, c], st[0:n, 9 + j:10 + j], None, ALU.mult,
                          after=[m5])
            sts.give(st, m6)
            yield
            pt, freed_pt = pts.take()
            bank, freed = banks.take()
            for k in range(3):
                nk = QT[k][1]
                for j in range(k, 3):
                    q0, n, _ = QT[j]
                    at = KO[k] + q0 - KQ[k][0]
                    m7 = PE.op(ten.transpose, bank[0:nk, at:at + n], pb[0:n, QO[j] + P * k:QO[j] + P * k + nk],
                               ident[0:n, 0:n], after=[m6, freed])
            A.op(act.activation, pt[:, 0:416], bank[:, 0:416], ACT.Copy, after=[m7, freed_pt])
            m8 = A.op(act.activation, pt[0:16, 416:KW], bank[0:16, 416:KW], ACT.Copy)
            banks.give(bank, m8)
            pbs.give(pb, m7)
            yield
            ob, freed = banks.take()
            for k in range(3):
                nk = QT[k][1]
                q0, nq = KQ[k]
                fn = PE.op if k == 2 else PE.quiet
                m9 = fn(ten.matmul, ob[:, q0:T], avt[0:nk, k, h * P:(h + 1) * P], pt[0:nk, KO[k]:KO[k] + nq],
                        start=(k == 0), stop=(k == 2), after=[m8, m_av[h], freed])
            pts.give(pt, m9)
            m_ya[h] = split_input(h, ob[:, 0:T], 1.0, m9, h2h(h), h2l(h), m_in)
            banks.give(ob, m_ya[h])
            yield

        m_yg_all = [m_yg[k] for k in range(16)]
        heads = [att_head(h) for h in range(ATT_HEADS)]
        live = []
        for step in range(ATT_HEADS + 3):
            if step < ATT_HEADS:
                live.append(heads[step])
            for g in list(live):
                try:
                    next(g)
                except StopIteration:
                    live.remove(g)
            if step < KT:
                project("ret_out", [step], lambda k: yh[:, k, :], lambda k: yl[:, k, :], T, m_yg_all, ret_out_evac,
                        kt=16)
        m_ro = PE.last()

        def att_out_evac(panel, ps, mark):
            m1 = V.op(vec.tensor_tensor, gatt[:, panel, :], gatt[:, panel, :], ps, ALU.mult,
                      after=[mark, m_ga[panel]])
            m2 = V.op(vec.tensor_tensor, merged[:, panel, :], merged[:, panel, :], gatt[:, panel, :],
                      ALU.add, after=[m1, m_mg[panel]])
            m_mg[panel] = split_input(panel, merged[:, panel, :], 1.0, m2, yh[:, panel, :], yl[:, panel, :], m_ro)
            return (m1,)

        project("att_out", list(range(KT)), h2h, h2l, T, m_ya, att_out_evac)
        m_ao = PE.last()

        def mix_evac(panel, ps, mark):
            m = V.op(vec.tensor_tensor, x2(panel), x2(panel), ps, ALU.add, after=[mark])
            residual_done(panel, 0, "ffn2", m, [m_ao, m_mg[panel]])
            return (m,)

        project("mix_out", list(range(KT)), lambda k: yh[:, k, :], lambda k: yl[:, k, :], T, m_mg, mix_evac)
        new_phase()
        ph.close()

        ffn(2, None)
        residual_stat(T)
        s_out = sem("s_out")
        for k in range(KT):
            m = V.op(vec.scalar_tensor_tensor, x2(k), x2(k), col("final", k), rstd[:, :], ALU.mult, ALU.mult,
                     after=[stat["x"]])
            SP.dma(outT[:, k, :], res[:, k, N_META:T], s_out, 16 * (k + 1), after=[m])
        SP.wait((s_out, 16 * KT))
        second.close()

        block = ctx.enter_context(nc.Block())

        @block.sync
        def _(e):
            SP.emit()

        @block.gpsimd
        def _(e):
            G.emit()

        @block.scalar
        def _(e):
            A.emit()

        @block.vector
        def _(e):
            V.emit()

        @block.tensor
        def _(e):
            PE.emit()


def kernel(**inputs):
    import concourse.bacc as _bacc
    from concourse import mybir as _mybir
    from concourse.bass_utils import run_bass_kernel_spmd as _run

    I = {k: np.asarray(v) for k, v in inputs.items()}
    nc = _bacc.Bacc("TRN2", target_bir_lowering=False, num_devices=1)
    arrays = {}

    def dram(name, a):
        a = np.ascontiguousarray(a)
        arrays[name] = a
        return nc.dram_tensor(name, a.shape, _mybir.dt.from_np(a.dtype), kind="ExternalInput").ap()

    def feature_major(a):
        return a.T.reshape(-1, P, a.shape[0]).transpose(1, 0, 2)

    def panels(wt):
        k, n = wt.shape
        return wt.reshape(k // P, P, n // P, P).transpose(2, 1, 0, 3).reshape(n // P, P, k)

    vec = {"pre0": I["pre_norm"][0], "pre1": I["pre_norm"][1], "post0": I["post_norm"][0], "post1": I["post_norm"][1],
           "memn0": I["mem_norm"][0], "memn1": I["mem_norm"][1], "kvn": I["kv_norm"], "mu": I["a_shift_mu"][0],
           "w0": I["a_w0"][0], "a0": I["a_a0"][0], "kk": I["a_k_k"][0], "ka": I["a_k_a"][0],
           "rk": I["a_r_k"][0].reshape(-1), "lnw": I["a_lnx_w"][0], "lnb": I["a_lnx_b"][0], "subln": I["b_subln"][0],
           "ffn1": I["ffn1_norm_2"][0], "mix": I["mix_norm_2"][0], "ffn2": I["ffn2_norm_2"][0],
           "final": I["final_norm_2"]}
    cols = np.zeros((P, NCOL), np.float32)
    for name, n in VECTORS:
        if name == "lam":
            for j, key in enumerate(("b_lam_q1", "b_lam_q2", "b_lam_k1", "b_lam_k2")):
                cols[:HD, COL[name] + j] = I[key][0]
        else:
            cols[:, COL[name]:COL[name] + n] = vec[name].reshape(n, P).T
    ta, tr, tb = const_tables()

    win = I["w_in_2"][0]
    o = np.cumsum([0, 1024, 1024, 2048, 2048, 1024, 1024, 1024, 512, 64, 8, 1024, 1024])
    idx = []
    for j in range(4):
        for half in range(2):
            for h in (2 * j, 2 * j + 1):
                idx += list(range(o[7] + 64 * h + 32 * half, o[7] + 64 * h + 32 * half + 32))
    for half in (0, 0, 1, 1):
        idx += list(range(o[8] + 32 * half, o[8] + 32 * half + 32))
    w_idx = np.concatenate([win[:, idx], win[:, o[9]:o[10]], np.zeros((D, P - IDX_HEADS), win.dtype)], 1)
    w = {
        "a_w_in": panels(I["a_w_in"][0]), "w_mem0": panels(I["w_mem_kv"][0]), "w_mem1": panels(I["w_mem_kv"][1]),
        "w_out0": panels(I["w_out"][0]), "w_out1": panels(I["w_out"][1]), "w_kv": panels(I["w_kv"]),
        "b_w_in": panels(I["b_w_in"][0]),
        "ffn1_gate": panels(I["ffn1_w_gate_2"][0]), "ffn1_up": panels(I["ffn1_w_up_2"][0]),
        "ffn1_down": panels(I["ffn1_w_down_2"][0]), "ffn2_gate": panels(I["ffn2_w_gate_2"][0]),
        "ffn2_up": panels(I["ffn2_w_up_2"][0]), "ffn2_down": panels(I["ffn2_w_down_2"][0]),
        "idx": panels(w_idx), "ret": panels(win[:, o[0]:o[2]]), "rv": panels(win[:, o[2]:o[3]]),
        "rg": panels(win[:, o[3]:o[4]]), "aqk": panels(win[:, o[4]:o[6]]), "av": panels(win[:, o[6]:o[7]]),
        "g2": panels(win[:, o[10]:o[12]]),
        "ret_out": panels(I["w_ret_out_2"][0]), "att_out": panels(I["w_att_out_2"][0]),
        "mix_out": panels(I["w_mix_out_2"][0]),
    }
    args = [dram("xT", feature_major(I["x"][0])), dram("memT", feature_major(I["mem"][0])),
            dram("metaT", feature_major(I["meta_tokens_2"])), dram("vecs", cols), dram("tab_a", ta),
            dram("tab_r", tr), dram("tab_b", tb),
            dram("lora", np.concatenate([I["a_w2"][0], I["a_a2"][0]], 0)),
            {k: dram("w_" + k, v) for k, v in w.items()}]
    out = nc.dram_tensor("outT", (P, KT, S), _mybir.dt.float32, kind="ExternalOutput").ap()
    build(nc, *args, out)
    r = _run(nc, [arrays], core_ids=[0])
    got = r.results[0]["outT"]
    return got.transpose(2, 1, 0).reshape(1, S, D)
```
